# Optimizing a Trainium2 kernel written in Bass

```python
import math
import jax, jax.numpy as jnp
from jax import lax
import numpy as np
import jax
import jax.numpy as jnp

D_MODEL = 1024
BATCH = 1
SEQ = 1024
DEPTH = 1

CTX_LEN = 256
GRID_W = 64
MIX_WIDTH = D_MODEL
HY_WIDTH = MIX_WIDTH // 2
HG_WIDTH = MIX_WIDTH - HY_WIDTH
HG_HEADS = 4
HG_HEAD_DIM = HG_WIDTH // HG_HEADS
HY_ORDER = 2
HY_SHORT = 3
HY_BANDS = 16
HY_POS_DIM = 2 * HY_BANDS + 1
HY_FILTER_HIDDEN = 64
HY_DECAY_TARGET = 1e-2
HY_FAST_DECAY = 0.3
HY_SLOW_DECAY = 1.5
HY_WINDOW_SHIFT = 0.05
CHUNK = 64
N_EXPERTS = 16
CAPACITY_FACTOR = 2
EXPERT_FF = 2 * D_MODEL
IN_COLS = 3 * HY_WIDTH + 5 * HG_WIDTH
EPS = 1e-6


def rmsnorm(x, g):
    xf = x.astype(jnp.float32)
    y = xf * lax.rsqrt(jnp.mean(xf * xf, axis=-1, keepdims=True) + EPS)
    return (y * g.astype(jnp.float32)).astype(x.dtype)

def modulate(h, shift, scale):
    return h * (1 + scale) + shift

def short_conv(u, w, b, n_rows):
    bn, L, C = u.shape
    row_len = L // n_rows
    pad = HY_SHORT // 2
    up = jnp.pad(u.reshape(bn, n_rows, row_len, C), ((0, 0), (0, 0), (pad, pad), (0, 0)))
    y = b + sum(up[:, :, j:j + row_len] * w[j] for j in range(HY_SHORT))
    return y.reshape(bn, L, C)

def hyena_filter_freqs(L, w1, b1, fr1, w2, b2, fr2, w3):
    C = w3.shape[1] // (HY_ORDER * 2)
    t = jnp.linspace(0.0, 1.0, L, dtype=jnp.float32)[:, None]
    w = 2.0 * math.pi * jnp.arange(L, dtype=jnp.float32)[:, None] / L
    f = jnp.linspace(1e-4, HY_BANDS - 1, HY_BANDS, dtype=jnp.float32)[None, :]
    z = jnp.concatenate([t, jnp.cos(f * w), -jnp.sin(f * w)], axis=-1)
    h = jnp.sin(fr1.astype(jnp.float32) * (z @ w1.astype(jnp.float32) + b1.astype(jnp.float32)))
    h = jnp.sin(fr2.astype(jnp.float32) * (h @ w2.astype(jnp.float32) + b2.astype(jnp.float32)))
    h = (h @ w3.astype(jnp.float32)).reshape(L, HY_ORDER, 2, C)
    min_decay = math.log(HY_DECAY_TARGET) / HY_SLOW_DECAY
    max_decay = math.log(HY_DECAY_TARGET) / HY_FAST_DECAY
    deltas = jnp.abs(jnp.linspace(min_decay, max_decay, C, dtype=jnp.float32))
    window = jnp.exp(-t * deltas[None, :]) + HY_WINDOW_SHIFT
    h = h * window[:, None, None, :]
    full = jnp.concatenate([h[:, :, 0], jnp.zeros((1, HY_ORDER, C), jnp.float32), h[:0:-1, :, 1]], axis=0)
    full = full / (jnp.sum(jnp.abs(full), axis=0, keepdims=True) + EPS)
    return jnp.fft.rfft(full, axis=0)

def long_conv(u, hf, bias):
    L = u.shape[1]
    U = jnp.fft.rfft(u, n=2 * L, axis=1)
    y = jnp.fft.irfft(U * hf[None], n=2 * L, axis=1)[:, :L]
    return y + u * bias.astype(jnp.float32)

def hyena_mixer(p, n_rows, conv_w, conv_b, filt, bias):
    L = p.shape[1]
    u = short_conv(p, conv_w, conv_b, n_rows).astype(jnp.float32)
    v, x1, x2 = jnp.split(u, 3, axis=-1)
    hf = hyena_filter_freqs(L, *filt)
    z = x1 * long_conv(v, hf[:, 0], bias[0])
    y = x2 * long_conv(z, hf[:, 1], bias[1])
    return y.astype(p.dtype)

def chunk_scan(q, k, v, logf, s0):
    bn, L, H, K = q.shape
    n = L // CHUNK

    def blocks(a):
        return a.reshape(bn, n, CHUNK, H, a.shape[-1]).swapaxes(0, 1)

    earlier_or_same = jnp.tril(jnp.ones((CHUNK, CHUNK), dtype=bool))[None, :, :, None, None]

    def step(S, inp):
        qb, kb, vb, gb = inp
        G = jnp.cumsum(gb, axis=1)
        o_inter = jnp.einsum('bthk,bhkv->bthv', qb * jnp.exp(G), S)
        decay = jnp.exp(jnp.where(earlier_or_same, G[:, :, None] - G[:, None, :], -jnp.inf))
        A = jnp.einsum('bthk,bshk,btshk->bhts', qb, kb, decay)
        o_intra = jnp.einsum('bhts,bshv->bthv', A, vb)
        G_last = G[:, -1]
        S_new = jnp.exp(G_last)[..., None] * S + jnp.einsum('bshk,bshv->bhkv', kb * jnp.exp(G_last[:, None] - G), vb)
        return S_new, o_inter + o_intra

    S_fin, o = lax.scan(step, s0, (blocks(q), blocks(k), blocks(v), blocks(logf)))
    return o.swapaxes(0, 1).reshape(bn, L, H, v.shape[-1]), S_fin

def hgrn_project(p, lb):
    bn, L, _ = p.shape
    q, i, zf, zb, g = jnp.split(p, 5, axis=-1)

    def heads(a):
        return a.reshape(bn, L, HG_HEADS, HG_HEAD_DIM)

    q = heads(jax.nn.silu(q.astype(jnp.float32)) * HG_HEAD_DIM ** -0.5)
    v = heads(i.astype(jnp.float32))

    def gate(z, lb_d):
        f = lb_d + (1.0 - lb_d) * jax.nn.sigmoid(z.astype(jnp.float32))
        return heads(1.0 - f), heads(jnp.log(f))

    return q, v, gate(zf, lb[0]), gate(zb, lb[1]), g

def hgrn_readout(o, g, norm_g):
    bn, L = o.shape[:2]
    o = rmsnorm(o, norm_g).reshape(bn, L, HG_WIDTH)
    return (o * jax.nn.silu(g.astype(jnp.float32))).astype(g.dtype)

def hgrn_mixer(p_lat, p_ctx, lb, norm_g, need_ctx):
    ql, vl, (kfl, gfl), (kbl, gbl), g_lat = hgrn_project(p_lat, lb)
    qc, vc, (kfc, gfc), (kbc, gbc), g_ctx = hgrn_project(p_ctx, lb)
    s0 = jnp.zeros((p_lat.shape[0], HG_HEADS, HG_HEAD_DIM, HG_HEAD_DIM), jnp.float32)
    flip = lambda a: a[:, ::-1]
    oc_f, S_f = chunk_scan(qc, kfc, vc, gfc, s0)
    oc_b, S_b = chunk_scan(flip(qc), flip(kbc), flip(vc), flip(gbc), s0)
    ol_f, _ = chunk_scan(ql, kfl, vl, gfl, S_f)
    ol_b, _ = chunk_scan(flip(ql), flip(kbl), flip(vl), flip(gbl), S_b)
    out_lat = hgrn_readout(ol_f + flip(ol_b), g_lat, norm_g)
    out_ctx = hgrn_readout(oc_f + flip(oc_b), g_ctx, norm_g) if need_ctx else None
    return out_lat, out_ctx

def ec_moe(h, router_w, w1, w3, w2):
    bn, N, D = h.shape
    cap = CAPACITY_FACTOR * N // N_EXPERTS
    aff = jax.nn.softmax(jnp.einsum('bnd,de->bne', h, router_w).astype(jnp.float32), axis=-1)
    gates, idx = lax.top_k(jnp.swapaxes(aff, 1, 2), cap)
    xg = jax.vmap(lambda hb, ib: hb[ib])(h, idx)
    a = jnp.einsum('becd,edf->becf', xg, w1)
    b = jnp.einsum('becd,edf->becf', xg, w3)
    y = jnp.einsum('becf,efd->becd', jax.nn.silu(a) * b, w2)
    y = y * gates[..., None].astype(y.dtype)
    return jax.vmap(lambda yb, ib: jnp.zeros((N, D), yb.dtype).at[ib.reshape(-1)].add(yb.reshape(-1, D)))(y, idx)

def first_inputs(seed: int = 0) -> dict:
    key = jax.random.key(seed)
    ks = jax.random.split(key, 28)

    def nrm(k, shape, s):
        return jax.random.normal(k, shape, jnp.float32) * s

    D, L_ = D_MODEL, DEPTH
    return {
        "x": nrm(ks[0], (BATCH, SEQ, D), 1.0),
        "c": nrm(ks[1], (BATCH, D), 1.0),
        "ctx": nrm(ks[2], (BATCH, CTX_LEN, D), 1.0),
        "c_ctx": nrm(ks[3], (D,), 1.0),
        "ada_w": nrm(ks[4], (L_, D, 6 * D), 0.5 * D ** -0.5),
        "ada_b": nrm(ks[5], (L_, 6 * D), 0.02),
        "norm1_g": 1.0 + nrm(ks[6], (L_, D), 0.05),
        "w_in": nrm(ks[7], (L_, D, IN_COLS), D ** -0.5),
        "hy_conv_w": nrm(ks[8], (L_, HY_SHORT, 3 * HY_WIDTH), HY_SHORT ** -0.5),
        "hy_conv_b": nrm(ks[9], (L_, 3 * HY_WIDTH), 0.02),
        "hy_pos_w1": nrm(ks[10], (L_, HY_POS_DIM, HY_FILTER_HIDDEN), HY_POS_DIM ** -0.5),
        "hy_pos_b1": nrm(ks[11], (L_, HY_FILTER_HIDDEN), 0.1),
        "hy_freq1": 1.0 + nrm(ks[12], (L_, HY_FILTER_HIDDEN), 0.1),
        "hy_pos_w2": nrm(ks[13], (L_, HY_FILTER_HIDDEN, HY_FILTER_HIDDEN), HY_FILTER_HIDDEN ** -0.5),
        "hy_pos_b2": nrm(ks[14], (L_, HY_FILTER_HIDDEN), 0.1),
        "hy_freq2": 1.0 + nrm(ks[15], (L_, HY_FILTER_HIDDEN), 0.1),
        "hy_pos_w3": nrm(ks[16], (L_, HY_FILTER_HIDDEN, HY_ORDER * 2 * HY_WIDTH), HY_FILTER_HIDDEN ** -0.5),
        "hy_bias": nrm(ks[17], (L_, HY_ORDER, HY_WIDTH), 0.5),
        "hy_norm_g": 1.0 + nrm(ks[18], (L_, HY_WIDTH), 0.05),
        "hg_lb": nrm(ks[19], (L_ + 1, 2, HG_WIDTH), 1.0),
        "hg_norm_g": 1.0 + nrm(ks[20], (L_, HG_HEAD_DIM), 0.05),
        "w_out": nrm(ks[21], (L_, MIX_WIDTH, D), MIX_WIDTH ** -0.5),
        "norm2_g": 1.0 + nrm(ks[22], (L_, D), 0.05),
        "router_w": nrm(ks[23], (L_, D, N_EXPERTS), D ** -0.5),
        "exp_w1": nrm(ks[24], (L_, N_EXPERTS, D, EXPERT_FF), D ** -0.5),
        "exp_w3": nrm(ks[25], (L_, N_EXPERTS, D, EXPERT_FF), D ** -0.5),
        "exp_w2": nrm(ks[26], (L_, N_EXPERTS, EXPERT_FF, D), EXPERT_FF ** -0.5),
        "final_g": 1.0 + nrm(ks[27], (D,), 0.05),
    }

def first_block(x, c, ctx, c_ctx, ada_w, ada_b, norm1_g, w_in, hy_conv_w, hy_conv_b, hy_pos_w1, hy_pos_b1,
              hy_freq1, hy_pos_w2, hy_pos_b2, hy_freq2, hy_pos_w3, hy_bias, hy_norm_g, hg_lb, hg_norm_g,
              w_out, norm2_g, router_w, exp_w1, exp_w3, exp_w2, final_g):
    rows = x.shape[1] // GRID_W
    lb_all = jnp.cumsum(jax.nn.softmax(hg_lb.astype(jnp.float32), axis=0), axis=0)
    xc = ctx
    s_lat = jax.nn.silu(c)
    s_ctx = jax.nn.silu(c_ctx)
    for l in range(DEPTH):
        last = l == DEPTH - 1
        sh1, sc1, g1, sh2, sc2, g2 = jnp.split((s_lat @ ada_w[l] + ada_b[l])[:, None, :], 6, axis=-1)
        sh1c, sc1c, g1c, sh2c, sc2c, g2c = jnp.split(s_ctx @ ada_w[l] + ada_b[l], 6, axis=-1)

        h = modulate(rmsnorm(x, norm1_g[l]), sh1, sc1)
        hc = modulate(rmsnorm(xc, norm1_g[l]), sh1c, sc1c)
        p = h @ w_in[l]
        pc = hc @ w_in[l]
        filt = (hy_pos_w1[l], hy_pos_b1[l], hy_freq1[l], hy_pos_w2[l], hy_pos_b2[l], hy_freq2[l], hy_pos_w3[l])
        y_hy = hyena_mixer(p[..., :3 * HY_WIDTH], rows, hy_conv_w[l], hy_conv_b[l], filt, hy_bias[l])
        y_hg, y_hg_c = hgrn_mixer(p[..., 3 * HY_WIDTH:], pc[..., 3 * HY_WIDTH:], lb_all[l], hg_norm_g[l], not last)
        mix = jnp.concatenate([rmsnorm(y_hy, hy_norm_g[l]).astype(x.dtype), y_hg.astype(x.dtype)], axis=-1) @ w_out[l]
        x = x + g1 * mix
        if not last:
            y_hy_c = hyena_mixer(pc[..., :3 * HY_WIDTH], 1, hy_conv_w[l], hy_conv_b[l], filt, hy_bias[l])
            mix_c = jnp.concatenate([rmsnorm(y_hy_c, hy_norm_g[l]).astype(xc.dtype), y_hg_c.astype(xc.dtype)], axis=-1) @ w_out[l]
            xc = xc + g1c * mix_c

        h2 = modulate(rmsnorm(x, norm2_g[l]), sh2, sc2)
        x = x + g2 * ec_moe(h2, router_w[l], exp_w1[l], exp_w3[l], exp_w2[l])
        if not last:
            h2c = modulate(rmsnorm(xc, norm2_g[l]), sh2c, sc2c)
            xc = xc + g2c * ec_moe(h2c, router_w[l], exp_w1[l], exp_w3[l], exp_w2[l])
    return rmsnorm(x, final_g)


DEPTH_2 = 2

MIX_W = D_MODEL
FOURIER_W = MIX_W // 4
FOURIER_GROUPS = 4
FOURIER_GD = FOURIER_W // FOURIER_GROUPS
POOL_W = MIX_W // 4
POOL_WINDOWS = (2, 4, 8, 16)
POOL_GD = POOL_W // len(POOL_WINDOWS)
ATTN_W = MIX_W - FOURIER_W - POOL_W
QK_DIM = 64
V_DIM = 2 * QK_DIM
N_HEADS = ATTN_W // V_DIM
QK_W = N_HEADS * 2 * QK_DIM
Q_BLOCK = 128
ROPE_THETA = 10000.0

A_OFF = 0
B_OFF = A_OFF + FOURIER_W
Q_OFF = B_OFF + POOL_W
K_OFF = Q_OFF + QK_W
V_OFF = K_OFF + QK_W
G_OFF = V_OFF + ATTN_W
IN_W = G_OFF + MIX_W


def rms_norm(t, g):
    tf = t.astype(jnp.float32)
    y = tf * lax.rsqrt(jnp.mean(tf * tf, axis=-1, keepdims=True) + EPS)
    return (y * g.astype(jnp.float32)).astype(t.dtype)

def axial_rope_tables(rows):
    row = jnp.repeat(jnp.arange(rows), GRID_W).astype(jnp.float32)
    col = jnp.tile(jnp.arange(GRID_W), rows).astype(jnp.float32)
    half = QK_DIM // 2
    inv_freq = ROPE_THETA ** (-jnp.arange(0, half, 2, dtype=jnp.float32) / half)
    ang_r = row[:, None] * inv_freq[None, :]
    ang_c = col[:, None] * inv_freq[None, :]
    ang = jnp.concatenate([ang_r, ang_r, ang_c, ang_c], axis=-1)
    return jnp.cos(ang), jnp.sin(ang)

def apply_rope(t, cos, sin):
    tr = t.reshape(t.shape[:-1] + (2, 2, QK_DIM // 4))
    rot = jnp.stack([-tr[..., 1, :], tr[..., 0, :]], axis=-2).reshape(t.shape)
    return (t * cos + rot * sin).astype(t.dtype)

def centred_window_mean(u, w):
    L = u.shape[1]
    lo = w // 2
    hi = w - lo - 1
    cs = jnp.pad(jnp.cumsum(u.astype(jnp.float32), axis=1), ((0, 0), (1, 0), (0, 0)))
    t = jnp.arange(L)
    a = jnp.clip(t - lo, 0, L - 1)
    b = jnp.clip(t + hi, 0, L - 1)
    s = cs[:, b + 1] - cs[:, a]
    cnt = (b - a + 1).astype(jnp.float32)
    return (s / cnt[None, :, None]).astype(u.dtype)

def fourier_mix(a, w_fourier):
    B_, L = a.shape[:2]
    ag = a.reshape(B_, L, FOURIER_GROUPS, FOURIER_GD).astype(jnp.float32)
    f = jnp.fft.fftn(ag, axes=(1, 3), norm='ortho').real.astype(a.dtype)
    y = jnp.einsum('blgc,gcd->blgd', f, w_fourier)
    return y.reshape(B_, L, FOURIER_W)

def pool_mix(b, w_pool, pool_scale):
    B_, L = b.shape[:2]
    bg = b.reshape(B_, L, len(POOL_WINDOWS), POOL_GD)
    pooled = jnp.stack([centred_window_mean(bg[:, :, gi], w) for gi, w in enumerate(POOL_WINDOWS)], axis=2) - bg
    y = jnp.einsum('blgc,gcd->blgd', pooled, w_pool).reshape(B_, L, POOL_W)
    return y * pool_scale

def split_heads_qk(t):
    B_, L = t.shape[:2]
    return t.reshape(B_, L, N_HEADS, 2, QK_DIM).transpose(0, 2, 3, 1, 4)

def split_heads_v(t):
    B_, L = t.shape[:2]
    return t.reshape(B_, L, N_HEADS, V_DIM).transpose(0, 2, 1, 3)

def diff_attend(q, k, v, lam):
    s = jnp.einsum('bhmqd,bhmkd->bhmqk', q, k).astype(jnp.float32) * (QK_DIM ** -0.5)
    p = jax.nn.softmax(s, axis=-1)
    p = p[:, :, 0] - lam * p[:, :, 1]
    return jnp.einsum('bhqk,bhkd->bhqd', p.astype(v.dtype), v)

def attn_post(o, subln_g, lam_init):
    o = rms_norm(o, subln_g) * (1.0 - lam_init)
    B_, H, L, dv = o.shape
    return o.transpose(0, 2, 1, 3).reshape(B_, L, H * dv)

def mixer_out(a_in, b_in, attn, gate, w_fourier, w_pool, pool_scale, w_out):
    y = jnp.concatenate([fourier_mix(a_in, w_fourier), pool_mix(b_in, w_pool, pool_scale), attn], axis=-1)
    return (y * jax.nn.silu(gate)) @ w_out

def mixer_layer(layer_idx, x, ctx, c, c_ctx, norm_g, w_mod, b_mod, w_in, w_fourier, w_pool,
                pool_scale, qk_norm_g, lam_vecs, subln_g, w_out, rope_cos, rope_sin, update_ctx):
    shift, scale, gate = jnp.split(jax.nn.silu(c) @ w_mod + b_mod, 3, axis=-1)
    shift_c, scale_c, gate_c = jnp.split(jax.nn.silu(c_ctx) @ w_mod + b_mod, 3, axis=-1)
    h = rms_norm(x, norm_g) * (1 + scale[:, None]) + shift[:, None]
    hc = rms_norm(ctx, norm_g) * (1 + scale_c) + shift_c

    lam_init = 0.8 - 0.6 * math.exp(-0.3 * layer_idx)
    lv = lam_vecs.astype(jnp.float32)
    lam = jnp.exp(jnp.sum(lv[0] * lv[1])) - jnp.exp(jnp.sum(lv[2] * lv[3])) + lam_init

    p = h @ w_in
    a_in, b_in = p[..., A_OFF:B_OFF], p[..., B_OFF:Q_OFF]
    q, k, v, g = p[..., Q_OFF:K_OFF], p[..., K_OFF:V_OFF], p[..., V_OFF:G_OFF], p[..., G_OFF:]

    if update_ctx:
        pc = hc @ w_in
        kc, vc = pc[..., K_OFF:V_OFF], pc[..., V_OFF:G_OFF]
    else:
        pkv = hc @ w_in[:, K_OFF:G_OFF]
        kc, vc = pkv[..., :QK_W], pkv[..., QK_W:]

    q_lat = apply_rope(rms_norm(split_heads_qk(q), qk_norm_g[0]), rope_cos, rope_sin)
    k_lat = apply_rope(rms_norm(split_heads_qk(k), qk_norm_g[1]), rope_cos, rope_sin)
    k_ctx = rms_norm(split_heads_qk(kc), qk_norm_g[1])
    v_ctx = split_heads_v(vc)
    k_all = jnp.concatenate([k_ctx, k_lat], axis=3)
    v_all = jnp.concatenate([v_ctx, split_heads_v(v)], axis=2)

    B_, H, _, L, d = q_lat.shape
    nb = L // Q_BLOCK
    qb = jnp.moveaxis(q_lat.reshape(B_, H, 2, nb, Q_BLOCK, d), 3, 0)
    ob = lax.map(lambda qblk: diff_attend(qblk, k_all, v_all, lam), qb)
    o = jnp.moveaxis(ob, 0, 2).reshape(B_, H, L, V_DIM)
    attn = attn_post(o, subln_g, lam_init)

    x_new = x + gate[:, None] * mixer_out(a_in, b_in, attn, g, w_fourier, w_pool, pool_scale, w_out)

    if update_ctx:
        qc = rms_norm(split_heads_qk(pc[..., Q_OFF:K_OFF]), qk_norm_g[0])
        attn_c = attn_post(diff_attend(qc, k_ctx, v_ctx, lam), subln_g, lam_init)
        ctx = ctx + gate_c * mixer_out(pc[..., A_OFF:B_OFF], pc[..., B_OFF:Q_OFF], attn_c,
                                       pc[..., G_OFF:], w_fourier, w_pool, pool_scale, w_out)
    return x_new, ctx

def second_inputs(seed: int = 0) -> dict:
    key = jax.random.key(seed)
    ks = jax.random.split(key, 16)
    f32 = jnp.float32
    nrm = lambda k, shape: jax.random.normal(k, shape, dtype=f32)
    return {
        'x': nrm(ks[0], (BATCH, SEQ, D_MODEL)),
        'c': nrm(ks[1], (BATCH, D_MODEL)),
        'ctx': nrm(ks[2], (BATCH, CTX_LEN, D_MODEL)),
        'c_ctx': nrm(ks[3], (D_MODEL,)),
        'norm_g': 1.0 + 0.02 * nrm(ks[4], (DEPTH_2, D_MODEL)),
        'w_mod': nrm(ks[5], (DEPTH_2, D_MODEL, 3 * D_MODEL)) * D_MODEL ** -0.5,
        'b_mod': 0.02 * nrm(ks[6], (DEPTH_2, 3 * D_MODEL)),
        'w_in': nrm(ks[7], (DEPTH_2, D_MODEL, IN_W)) * D_MODEL ** -0.5,
        'w_fourier': nrm(ks[8], (DEPTH_2, FOURIER_GROUPS, FOURIER_GD, FOURIER_GD)) * FOURIER_GD ** -0.5,
        'w_pool': nrm(ks[9], (DEPTH_2, len(POOL_WINDOWS), POOL_GD, POOL_GD)) * POOL_GD ** -0.5,
        'pool_scale': 1.0 + 0.1 * nrm(ks[10], (DEPTH_2, POOL_W)),
        'qk_norm_g': 1.0 + 0.02 * nrm(ks[11], (DEPTH_2, 2, QK_DIM)),
        'lam_vecs': 0.1 * nrm(ks[12], (DEPTH_2, 4, QK_DIM)),
        'subln_g': 1.0 + 0.02 * nrm(ks[13], (DEPTH_2, V_DIM)),
        'w_out': nrm(ks[14], (DEPTH_2, MIX_W, D_MODEL)) * MIX_W ** -0.5,
    }

def second_block(x, c, ctx, c_ctx, norm_g, w_mod, b_mod, w_in, w_fourier, w_pool, pool_scale,
              qk_norm_g, lam_vecs, subln_g, w_out):
    rows = x.shape[1] // GRID_W
    rope_cos, rope_sin = axial_rope_tables(rows)
    for l in range(DEPTH_2):
        x, ctx = mixer_layer(l, x, ctx, c, c_ctx, norm_g[l], w_mod[l], b_mod[l], w_in[l],
                             w_fourier[l], w_pool[l], pool_scale[l], qk_norm_g[l], lam_vecs[l],
                             subln_g[l], w_out[l], rope_cos, rope_sin, l < DEPTH_2 - 1)
    return x


def setup_inputs(seed=0):
    out = dict(first_inputs(seed))
    for name, value in second_inputs(seed + 1).items():
        if name != "x":
            out[name + "_2"] = value
    return out


def reference(
    x, c, ctx, c_ctx, ada_w, ada_b, norm1_g, w_in, hy_conv_w, hy_conv_b, hy_pos_w1, hy_pos_b1,
    hy_freq1, hy_pos_w2, hy_pos_b2, hy_freq2, hy_pos_w3, hy_bias, hy_norm_g, hg_lb, hg_norm_g,
    w_out, norm2_g, router_w, exp_w1, exp_w3, exp_w2, final_g, c_2, ctx_2, c_ctx_2, norm_g_2,
    w_mod_2, b_mod_2, w_in_2, w_fourier_2, w_pool_2, pool_scale_2, qk_norm_g_2, lam_vecs_2,
    subln_g_2, w_out_2,
):
    x = first_block(
        x, c, ctx, c_ctx, ada_w, ada_b, norm1_g, w_in, hy_conv_w, hy_conv_b, hy_pos_w1,
        hy_pos_b1, hy_freq1, hy_pos_w2, hy_pos_b2, hy_freq2, hy_pos_w3, hy_bias, hy_norm_g,
        hg_lb, hg_norm_g, w_out, norm2_g, router_w, exp_w1, exp_w3, exp_w2, final_g,
    )
    return second_block(
        x, c_2, ctx_2, c_ctx_2, norm_g_2, w_mod_2, b_mod_2, w_in_2, w_fourier_2, w_pool_2,
        pool_scale_2, qk_norm_g_2, lam_vecs_2, subln_g_2, w_out_2,
    )


_drawn_inputs = setup_inputs


def setup_inputs(seed=0):
    import zlib

    import numpy as np

    out = dict(_drawn_inputs(seed))
    spreads = {}
    factors = {'ctx': 8.0,
     'c_ctx': 8.0,
     'hy_conv_b': 5.138,
     'hy_pos_b1': 3.801,
     'hy_freq1': 8.0,
     'hy_pos_b2': 3.218,
     'hy_freq2': 8.0,
     'hy_norm_g': 5.101,
     'hg_lb': 5.534,
     'hg_norm_g': 7.145,
     'norm2_g': 4.88,
     'ctx_2': 2.706,
     'norm_g_2': 4.217,
     'qk_norm_g_2': 8.0,
     'lam_vecs_2': 8.0,
     'subln_g_2': 7.177}
    for name, (base, spread) in spreads.items():
        noise = np.random.default_rng([zlib.crc32(name.encode()), seed]).standard_normal(out[name].shape)
        drawn = base * np.exp(spread * noise) if base else spread * noise
        out[name] = jnp.asarray(drawn.astype(out[name].dtype))
    for name, factor in factors.items():
        out[name] = (out[name] * factor).astype(out[name].dtype)
    return out
```

```python
import math
from contextlib import ExitStack, contextmanager

import concourse.bass as bass
import numpy as np
from concourse import mybir

F32 = mybir.dt.float32
F32R = mybir.dt.float32r
BF16 = mybir.dt.bfloat16
U32 = mybir.dt.uint32
ALU = mybir.AluOpType
ACT = mybir.ActivationFunctionType
AX = mybir.AxisListType.X

P = 128
D = 1024
KD = D // P
SEQ = 1024
NT = SEQ // P
CTX = 256
NC_ = CTX // P
TOK = SEQ + CTX
BANK = 512
GRID = 64
EPS = 1e-6
HY = 512
HG_HEADS = 4
LEVELS = 7
HFF = 64
POS = 33
E = 16
CAP = 128
FF = 2048
EPS_F = 1e-6
TWO_PI = 2.0 * math.pi
TWO_PI_HI = 6.28125
TWO_PI_LO = TWO_PI - TWO_PI_HI
ROUND = 1.5 * 2.0 ** 23
PI_IN = 3.1415925
HEADS2 = 4
QK = 64


class Chain:

    def __init__(self, sem):
        self.sem, self.n = sem, 0

    def __call__(self, eng, ins):
        self.n += 1
        ins.then_inc(self.sem, 1)
        eng.wait_ge(self.sem, self.n)


class Lane:

    def __init__(self, sem):
        self.sem, self.base = sem, 0

    def at(self, k):
        return self.base + 16 * k

    def close(self, k):
        self.base += 16 * k


class Core:

    def __init__(self, nc, io, tap):
        self.nc, self.io, self.tap = nc, io, tap
        self.stack = ExitStack()
        self.zeroed_sems, self.used_sems, self.retired_sems, self.n_stage_sems = [], [], [], 0
        self.dve = Chain(self.sem("dve_step_done"))
        self.act = Chain(self.sem("act_step_done"))
        self.pool = Chain(self.sem("pool_step_done"))
        self.load = [Lane(self.sem(f"load_done_{i}")) for i in range(12)]
        self.store = [Lane(self.sem(f"store_done_{i}")) for i in range(8)]
        self.hstore = [Lane(self.sem(f"store_done_hw_{i}")) for i in range(6)]

    def sem(self, name):
        return self.stack.enter_context(self.nc.semaphore(name))

    def dram(self, name, shape, dt=F32):
        kind = "ExternalOutput" if self.tap and name in self.tap else "Internal"
        return self.nc.dram_tensor(name, shape, dt, kind=kind).ap()

    def keep(self, name, shape, dt=F32):
        return self.stack.enter_context(self.nc.sbuf_tensor(name, shape, dt))


class Stage:

    def __init__(self, core, name):
        self.core, self.nc, self.name = core, core.nc, name
        self.stack = ExitStack()

    def __enter__(self):
        return self

    def __exit__(self, *a):
        self.stack.close()

    def sb(self, name, shape, dt=F32):
        return self.stack.enter_context(self.nc.sbuf_tensor(f"{self.name}_{name}", shape, dt))

    def banks(self, n, dt=F32):
        return [self.stack.enter_context(self.nc.psum_tensor(f"{self.name}_bank{i}", [P, BANK], dt))
                for i in range(n)]

    def sem(self, name):
        core = self.core
        s = core.zeroed_sems.pop() if core.zeroed_sems else core.sem(f"stage_{core.n_stage_sems}_{self.name}_{name}")
        core.n_stage_sems += 1
        core.used_sems.append(s)
        return s

    def dma_sem(self, name):
        return self.core.sem(f"{self.name}_{name}")

    @contextmanager
    def block(self):
        core = self.core
        mine, core.used_sems = core.used_sems, []
        with self.nc.Block() as block:
            retired, core.retired_sems = core.retired_sems, mine
            if retired:
                @block.sync
                def _(sp):
                    for s in retired:
                        sp.sem_clear(s)
            yield block
        core.zeroed_sems += retired


VEC_A = [("c", 8), ("c_ctx", 8), ("c_2", 8), ("c_ctx_2", 8), ("norm1_g", 8), ("norm2_g", 8),
         ("norm_g_2", 16), ("hy_norm_g", 4), ("hg_norm_g", 1), ("hy_conv_w", 36), ("hy_conv_b", 12)]
VEC_B = [("hg_lb", 16), ("pool_scale_2", 4), ("subln_g_2", 2)]
VEC_C = [("hy_pos_b1", 1), ("hy_freq1", 1), ("hy_pos_b2", 1), ("hy_freq2", 1)]


class Parts:

    def __init__(self, st, name, shape):
        self.high, self.low = st.sb(name + "_high", shape, F32R), st.sb(name + "_low", shape, F32R)

    def __getitem__(self, key):
        return self.high[key], self.low[key]


def product(nc, out, lhs, rhs, start, stop):
    nc.tensor.matmul(out, lhs[0], rhs[0], start=start, stop=False)
    nc.tensor.matmul(out, lhs[0], rhs[1], start=False, stop=False)
    return nc.tensor.matmul(out, lhs[1], rhs[0], start=False, stop=stop)


def offsets(vec):
    at, n = {}, 0
    for name, k in vec:
        at[name] = n
        n += k
    return at, n


AT_A, N_A = offsets(VEC_A)
AT_B, N_B = offsets(VEC_B)


def as_rows(ap, width):
    s = " ".join(f"a{i}" for i in range(len(ap.shape)))
    flat = ap.rearrange(f"{s} -> ({s})")
    return flat.rearrange("(r w) -> r w", w=width)


def stage_mods(core):
    nc, io = core.nc, core.io
    groups = [("ada_w", 0, g) for g in range(12)] + [("w_mod_2", l, g) for l in range(2) for g in range(6)]
    RING = 5
    with Stage(core, "mods") as st:
        rows_a, rows_b = st.sb("rows_a", [N_A, P]), st.sb("rows_b", [N_B, P])
        rows_c = st.sb("rows_c", [4, HFF])
        silu = st.sb("silu", [P, 32])
        w = [st.sb(f"w{i}", [P, KD, BANK]) for i in range(RING)]
        lbmax, lbd = st.sb("lbmax", [P, 8]), st.sb("lbd", [P, 2, 8])
        lbe, lbs = st.sb("lbe", [P, 2, 8]), st.sb("lbs", [P, 8])
        rows = st.sb("rows", [2, len(groups) * BANK])
        bias = st.sb("bias", [2, len(groups) * BANK])
        bank = st.banks(6)
        vecs, columns, silu_done, mods_done = (st.sem(x) for x in ("vecs", "columns", "silu", "mods"))
        cols_copied, w_used, stored, bias_added = (st.sem(x) for x in ("cols_copied", "w_used", "stored", "bias_added"))
        biases, turned = st.sem("biases"), st.sem("turned")
        n_vec = 0
        loads = []
        for dst, vec, width in ((rows_a, VEC_A, P), (rows_b, VEC_B, P), (rows_c, VEC_C, HFF)):
            r = 0
            for name, k in vec:
                loads.append((dst[r:r + k, :], as_rows(io[name], width)))
                r += k
        with st.block() as block:
            @block.sync
            def _(sp):
                sp.dma_start(core.ident[:, :], io["t_ident"]).then_inc(vecs, 16)
                for dst, src in loads:
                    sp.dma_start(dst, src).then_inc(vecs, 16)
                sp.dma_start(bias[:, 0:6 * D], io["ada_b"][0].partition_broadcast(2)).then_inc(biases, 16)
                for l in range(2):
                    sp.dma_start(bias[:, (6 + 3 * l) * D:(9 + 3 * l) * D],
                                 io["b_mod_2"][l].partition_broadcast(2)).then_inc(biases, 16)
                for i, (name, l, g) in enumerate(groups):
                    if i >= RING:
                        sp.wait_ge(w_used, i - RING + 1)
                    sp.dma_start(w[i % RING][:, :, :],
                                 io[name][l, :, g * BANK:(g + 1) * BANK].rearrange("(k p) n -> p k n", p=P)
                                 ).then_inc(core.load[i % RING].sem, 16)
                for l, (c0, c1) in enumerate(((0, 6 * D), (6 * D, 9 * D), (9 * D, 12 * D))):
                    sp.wait_ge(bias_added, c1 // BANK)
                    sp.dma_start(core.mod_rows[l], rows[:, c0:c1]).then_inc(stored, 16)
                sp.wait_ge(stored, 16 * 3)

            @block.gpsimd
            def _(pool):
                nc.gpsimd.memset(core.eps[:, :], EPS)

            @block.tensor
            def _(pe):
                pe.wait_ge(vecs, 16 * (1 + len(loads)))
                nc.tensor.transpose(bank[0][:, 0:N_A], rows_a[:, :], core.ident[0:N_A, 0:N_A])
                nc.tensor.transpose(bank[0][:, P:P + N_B], rows_b[:, :], core.ident[0:N_B, 0:N_B])
                nc.tensor.transpose(bank[0][0:HFF, 2 * P:2 * P + 4], rows_c[:, :],
                                    core.ident[0:4, 0:4]).then_inc(columns, 1)
                pe.wait_ge(silu_done, 1)

                def to_columns(i):
                    pe.wait_ge(bias_added, i + 1)
                    for s in range(4):
                        o = 2 * (4 * i + s)
                        c = i * BANK + s * P
                        last = nc.tensor.transpose(bank[1][:, o:o + 2], rows[:, c:c + P], core.ident[0:2, 0:2])
                    last.then_inc(turned, 1)

                for i, (name, l, g) in enumerate(groups):
                    pe.wait_ge(core.load[i % RING].sem, core.load[i % RING].at(i // RING + 1))
                    if i >= 4:
                        pe.wait_ge(bias_added, i - 3)
                    v0 = 0 if name == "ada_w" else 2
                    for k in range(KD):
                        last = nc.tensor.matmul(bank[2 + i % 4][0:2, :], silu[:, v0 * 8 + k:v0 * 8 + k + 9:8],
                                                w[i % RING][:, k, :], start=(k == 0), stop=(k == KD - 1))
                    last.then_inc(w_used, 1)
                    if i:
                        to_columns(i - 1)
                to_columns(len(groups) - 1)

            @block.scalar
            def _(act):
                act.wait_ge(cols_copied, 1)
                nc.scalar.activation(silu[:, :], core.col_a[:, 0:32], ACT.Silu).then_inc(silu_done, 1)
                act.wait_ge(cols_copied, 2)
                nc.scalar.activation(lbe[:, :, :], lbd[:, :, :], ACT.Exp).then_inc(mods_done, 1)

            @block.vector
            def _(dve):
                step = lambda ins: core.dve(dve, ins)
                dve.wait_ge(columns, 1)
                core.dve(dve, nc.vector.tensor_copy(core.col_b[:, :], bank[0][:, P:P + N_B]))
                core.dve(dve, nc.vector.tensor_copy(core.col_c[:, :], bank[0][0:HFF, 2 * P:2 * P + 4]))
                nc.vector.tensor_copy(core.col_a[:, :], bank[0][:, 0:N_A]).then_inc(cols_copied, 1)
                lb = core.col_b[:, AT_B["hg_lb"]:AT_B["hg_lb"] + 16].rearrange("p (l c) -> p l c", l=2)
                core.dve(dve, nc.vector.tensor_tensor(lbmax[:, :], lb[:, 0, :], lb[:, 1, :], ALU.max))
                nc.vector.tensor_tensor(lbd[:, :, :], lb, lbmax[:, :].unsqueeze(1).to_broadcast([P, 2, 8]),
                                        ALU.subtract).then_inc(cols_copied, 1)
                dve.wait_ge(mods_done, 1)
                core.dve(dve, nc.vector.tensor_tensor(lbs[:, :], lbe[:, 0, :], lbe[:, 1, :], ALU.add))
                core.dve(dve, nc.vector.reciprocal(lbs[:, :], lbs[:, :]))
                core.dve(dve, nc.vector.tensor_tensor(core.lb[:, 0, :], lbe[:, 0, :], lbs[:, :], ALU.mult))
                core.dve(dve, nc.vector.tensor_tensor(core.lb[:, 1, :], lbe[:, 1, :], lbs[:, :], ALU.mult))
                dve.wait_ge(biases, 48)
                for i in range(len(groups)):
                    c = slice(i * BANK, (i + 1) * BANK)
                    dve.wait_ge(w_used, i + 1)
                    nc.vector.tensor_tensor(rows[:, c], bank[2 + i % 4][0:2, :], bias[:, c], ALU.add).then_inc(bias_added, 1)
                dve.wait_ge(turned, len(groups))
                for m, o, n in ((core.mod1, 0, 48), (core.mod2[0], 96, 24), (core.mod2[1], 144, 24)):
                    step(nc.vector.tensor_copy(m[:, :, :], bank[1][:, o:o + 2 * n].rearrange("p (c v) -> p c v", v=2)))
                for out, m, c0, v, g in (
                        (core.sc[0], core.mod1, 8, 0, AT_A["norm1_g"]), (core.sc[1], core.mod1, 8, 1, AT_A["norm1_g"]),
                        (core.sc[2], core.mod1, 32, 0, AT_A["norm2_g"]),
                        (core.sc[3], core.mod2[0], 8, 0, AT_A["norm_g_2"]), (core.sc[4], core.mod2[0], 8, 1, AT_A["norm_g_2"]),
                        (core.sc[5], core.mod2[1], 8, 0, AT_A["norm_g_2"] + 8), (core.sc[6], core.mod2[1], 8, 1, AT_A["norm_g_2"] + 8)):
                    core.dve(dve, nc.vector.scalar_tensor_tensor(out[:, :], m[:, c0:c0 + 8, v], 1.0,
                                                                 core.col_a[:, g:g + 8], ALU.add, ALU.mult))
        for i in range(RING):
            core.load[i].close(len([x for x in range(len(groups)) if x % RING == i]))


def stage_norm(core, name, segs, hT, xn_dram=None, pre_gain=None):
    nc = core.nc
    tiles = [(src[t * P:(t + 1) * P, :], sc, sh) for src, sc, sh in segs for t in range(src.shape[0] // P)]
    n = len(tiles)
    RX = 3
    with Stage(core, name) as st:
        x = [st.sb(f"x{i}", [P, D]) for i in range(RX)]
        xn = [st.sb(f"xn{i}", [P, D]) for i in range(RX)]
        junk = st.sb("junk", [P, D])
        ss, rms, rstd = st.sb("ss", [P, n]), st.sb("rms", [P, n]), st.sb("rstd", [P, n])
        parts = isinstance(hT, Parts)
        whole = [[st.sb(f"whole{half}_{i}", [P, 4, P]) for i in range(2)] for half in range(2)] if parts else None
        split = st.sem("split")
        bank = st.banks(4)

        def modulated(i, k):
            return whole[k // 4][i % 2][:, k % 4, :] if parts else hT[:, k, i * P:(i + 1) * P]

        rms_done, xn_done, turned, out_a, out_v = (st.sem(k) for k in ("rms", "xn", "turned", "out_a", "out_v"))
        with st.block() as block:
            @block.sync
            def _(sp):
                for i, (src, _, _) in enumerate(tiles):
                    if i >= RX:
                        sp.wait_ge(xn_done, i - RX + 1)
                    sp.dma_start(x[i % RX][:, :], src).then_inc(core.load[i % RX].sem, 16)

            @block.gpsimd
            def _(pool):
                if parts:
                    for i in range(n):
                        for half, moved in enumerate((out_a, out_v)):
                            pool.wait_ge(moved, i + 1)
                            src, c = whole[half][i % 2][:, :, :], slice(4 * half, 4 * half + 4)
                            high, low = (y[:, c, i * P:(i + 1) * P] for y in (hT.high, hT.low))
                            core.pool(pool, nc.gpsimd.tensor_copy(high, src))
                            nc.gpsimd.tensor_tensor(low, src, high.bitcast(F32), ALU.subtract).then_inc(split, 1)
                if xn_dram is not None:
                    for i in range(n):
                        pool.wait_ge(xn_done, i + 1)
                        pool.dma_start(xn_dram[i * P:(i + 1) * P, :], xn[i % RX][:, :]
                                       ).then_inc(core.store[i % RX].sem, 16)
                    for j in range(RX):
                        pool.wait_ge(core.store[j].sem, core.store[j].at(len(range(j, n, RX))))

            @block.scalar
            def _(act):
                def measure(i):
                    act.wait_ge(core.load[i % RX].sem, core.load[i % RX].at(i // RX + 1))
                    core.act(act, nc.scalar.activation(junk[:, :], x[i % RX][:, :], ACT.Square,
                                                       accum_out=ss[:, i:i + 1]))
                    nc.scalar.activation(rms[:, i:i + 1], ss[:, i:i + 1], ACT.Sqrt, bias=core.eps[:, 0:1],
                                         scale=1.0 / D).then_inc(rms_done, 1)

                measure(0)
                for i, (_, sc, sh) in enumerate(tiles):
                    if i + 1 < n:
                        measure(i + 1)
                    act.wait_ge(turned, 2 * i + 1)
                    if parts and i >= 2:
                        act.wait_ge(split, 2 * (i - 2) + 1)
                    for k in range(4):
                        last = nc.scalar.activation(modulated(i, k),
                                                    bank[2 * (i % 2)][:, k * P:(k + 1) * P], ACT.Identity,
                                                    bias=sh[:, k:k + 1], scale=sc[:, k:k + 1])
                    last.then_inc(out_a, 1)

            @block.vector
            def _(dve):
                def normalise(i):
                    dve.wait_ge(rms_done, i + 1)
                    core.dve(dve, nc.vector.reciprocal(rstd[:, i:i + 1], rms[:, i:i + 1]))
                    if i >= RX:
                        dve.wait_ge(turned, 2 * (i - RX) + 2)
                        if xn_dram is not None:
                            dve.wait_ge(core.store[i % RX].sem, core.store[i % RX].at(i // RX))
                    nc.vector.tensor_scalar(xn[i % RX][:, :], x[i % RX][:, :], rstd[:, i:i + 1], None,
                                            ALU.mult).then_inc(xn_done, 1)

                normalise(0)
                for i, (_, sc, sh) in enumerate(tiles):
                    if i + 1 < n:
                        normalise(i + 1)
                    dve.wait_ge(turned, 2 * i + 2)
                    if parts and i >= 2:
                        dve.wait_ge(split, 2 * (i - 2) + 2)
                    for k in range(4, 8):
                        last = nc.vector.tensor_scalar(modulated(i, k),
                                                       bank[2 * (i % 2) + 1][:, (k - 4) * P:(k - 3) * P],
                                                       sc[:, k:k + 1], sh[:, k:k + 1], ALU.mult, ALU.add)
                    last.then_inc(out_v, 1)

            @block.tensor
            def _(pe):
                for i in range(n):
                    pe.wait_ge(xn_done, i + 1)
                    if i >= 2:
                        pe.wait_ge(out_a, i - 1)
                        pe.wait_ge(out_v, i - 1)
                    for half in range(2):
                        for k in range(4):
                            c = (4 * half + k) * P
                            last = nc.tensor.transpose(bank[2 * (i % 2) + half][:, k * P:(k + 1) * P],
                                                       xn[i % RX][:, c:c + P], core.ident[:, :])
                        last.then_inc(turned, 1)
        for j in range(RX):
            core.load[j].close(len(range(j, n, RX)))
            if xn_dram is not None:
                core.store[j].close(len(range(j, n, RX)))


def stage_project(core, name, hT, groups):
    nc = core.nc
    RW, RP, RS, NB = 2, 2, 8, 8
    SP_ = 4
    KP = KD // SP_
    jobs = [(g, j) for g, (_, js) in enumerate(groups) for j in js]
    first = {}
    for i, (g, _) in enumerate(jobs):
        first.setdefault(g, i)
    with Stage(core, name) as st:
        raw = [st.sb(f"raw{i}", [P, KD, BANK]) for i in range(RW)]
        w = [Parts(st, f"w{i}", [P, KD, BANK]) for i in range(RP)]
        out = [st.sb(f"out{i}", [P, BANK]) for i in range(RS)]
        bank = st.banks(NB)
        done, copied_a, copied_v, high, low = (st.sem(k) for k in ("product", "copied_a", "copied_v", "high", "low"))

        def wait_copied(eng, i):
            eng.wait_ge(copied_v if i % 2 else copied_a, i // 2 + 1)

        with st.block() as block:
            @block.sync
            def _(sp):
                for g, (src, _) in enumerate(groups):
                    if g >= RW:
                        sp.wait_ge(low, SP_ * (g - RW + 1))
                    sp.dma_start(raw[g % RW][:, :, 0:src.shape[1]], src.rearrange("(k p) n -> p k n", p=P)
                                 ).then_inc(core.load[g % RW].sem, 16)

            @block.tensor
            def _(pe):
                for i, (g, (kind, a, b, n, _)) in enumerate(jobs):
                    if i >= NB:
                        wait_copied(pe, i - NB)
                    for k in range(KD):
                        if first[g] == i and k % KP == 0:
                            pe.wait_ge(low, SP_ * g + k // KP + 1)
                        if kind == "ch":
                            lhs, rhs = w[g % RP][:, k, a * P:(a + 1) * P], hT[:, k, b:b + n]
                        else:
                            lhs, rhs = hT[:, k, a * P:(a + 1) * P], w[g % RP][:, k, b:b + n]
                        last = product(nc, bank[i % NB][:, 0:n], lhs, rhs, k == 0, k == KD - 1)
                    last.then_inc(done, 1)

            def piece(g, p):
                c = slice(p * KP, (p + 1) * KP)
                return raw[g % RW][:, c, :], w[g % RP].high[:, c, :], w[g % RP].low[:, c, :]

            def split_high(eng, g, p):
                if p == 0:
                    eng.wait_ge(core.load[g % RW].sem, core.load[g % RW].at(g // RW + 1))
                    if g >= RP:
                        eng.wait_ge(done, first[g - RP + 1])
                x, hi, _ = piece(g, p)
                nc.scalar.activation(hi, x, ACT.Copy).then_inc(high, 1)

            def split_low(eng, g, p):
                eng.wait_ge(high, SP_ * g + p + 1)
                x, hi, lo = piece(g, p)
                nc.vector.tensor_tensor(lo, x, hi.bitcast(F32), ALU.subtract).then_inc(low, 1)

            def run(eng, fn, odd, sem, split):
                for p in range(SP_):
                    split(eng, 0, p)
                for i, (g, (kind, a, b, n, _)) in enumerate(jobs):
                    if i - first[g] < SP_ and g + 1 < len(groups):
                        split(eng, g + 1, i - first[g])
                    if i % 2 != odd:
                        continue
                    eng.wait_ge(done, i + 1)
                    if i >= RS:
                        eng.wait_ge(core.store[i % RS].sem, core.store[i % RS].at(i // RS))
                    fn(out[i % RS][:, 0:n], bank[i % NB][:, 0:n]).then_inc(sem, 1)

            @block.scalar
            def _(act):
                run(act, lambda o, i: nc.scalar.activation(o, i, ACT.Copy), 0, copied_a, split_high)

            @block.vector
            def _(dve):
                run(dve, nc.vector.tensor_copy, 1, copied_v, split_low)

            @block.gpsimd
            def _(pool):
                for i, (g, (kind, a, b, n, dst)) in enumerate(jobs):
                    wait_copied(pool, i)
                    pool.dma_start(dst, out[i % RS][:, 0:n]).then_inc(core.store[i % RS].sem, 16)
                for j in range(RS):
                    pool.wait_ge(core.store[j].sem, core.store[j].at(len(range(j, len(jobs), RS))))
        for j in range(RW):
            core.load[j].close(len(range(j, len(groups), RW)))
        for j in range(RS):
            core.store[j].close(len(range(j, len(jobs), RS)))


def stage_filter(core, name="filter"):
    nc, io = core.nc, core.io
    NU = 2 * NT
    HF = NT // 2
    RS = 6
    with Stage(core, name) as st:
        z, w1, w2 = st.sb("z", [POS, SEQ]), st.sb("w1", [POS, HFF]), st.sb("w2", [HFF, HFF])
        w3 = st.sb("w3", [HFF, 4 * HY])
        tab = [st.sb("cos", [P, NT, SEQ // 2]), st.sb("sin", [P, NT, SEQ // 2])]
        win, win0 = st.sb("win", [P, NT, HY]), st.sb("win0", [P, HY])
        lin, turns, h = st.sb("lin", [HFF, SEQ]), st.sb("turns", [HFF, SEQ]), st.sb("h", [HFF, SEQ])
        ha, hb = [[st.sb(f"h{c}{i}", [P, HY]) for i in range(2)] for c in "ab"]
        aa, ab = [[st.sb(f"abs{c}{i}", [P, HY]) for i in range(2)] for c in "ab"]
        acc = [st.sb(f"acc{o}", [P, HY]) for o in range(2)]
        eo = [[st.sb(f"{c}{i}", [P, HY]) for i in range(2)] for c in ("even", "odd")]
        fold = [[st.sb(f"sum{o}", [P, NT, HY]), st.sb(f"dif{o}", [P, NT, HY])] for o in range(2)]
        gain = [st.sb(f"gain{o}", [P, HY]) for o in range(2)]
        skip = [st.sb(f"skip{o}", [P, HY]) for o in range(2)]
        ones = st.sb("ones", [P, P])
        out = [st.sb(f"out{i}", [P, HY]) for i in range(RS)]
        bank = st.banks(8)
        small, tables, lay, sines, taps, windowed, absd, folded, normed, gains, spec, scaled, final, ones_set = (
            st.sem(k) for k in ("small", "tables", "layer", "sines", "taps", "windowed", "abs", "folded",
                                "normed", "gains", "spec", "scaled", "final", "ones"))
        summed = st.sem("summed")
        b1, fr1, b2, fr2 = (core.col_c[:, i:i + 1] for i in range(4))
        pairs = [(o, f, s) for o in range(2) for f in range(HF) for s in range(2)]
        with st.block() as block:
            @block.sync
            def _(sp):
                sp.dma_start(z[:, :], io["t_pos"]).then_inc(small, 16)
                sp.dma_start(w1[:, :], io["hy_pos_w1"][0]).then_inc(small, 16)
                sp.dma_start(w2[:, :], io["hy_pos_w2"][0]).then_inc(small, 16)
                sp.dma_start(w3[:, :], io["hy_pos_w3"][0]).then_inc(small, 16)
                for o in range(2):
                    sp.dma_start(skip[o][:, :], io["hy_bias"][0][o].partition_broadcast(P)).then_inc(small, 16)
                sp.dma_start(win[:, :, :], io["t_window"].rearrange("(j p) c -> p j c", p=P)).then_inc(small, 16)
                sp.dma_start(win0[:, :], io["t_window0"]).then_inc(small, 16)
                sp.dma_start(tab[0][:, :, :], io["t_lag_cos"].rearrange("(j p) k -> p j k", p=P)).then_inc(tables, 16)
                sp.dma_start(tab[1][:, :, :], io["t_lag_sin"].rearrange("(j p) k -> p j k", p=P)).then_inc(tables, 16)
                for i, (o, f, s) in enumerate(pairs):
                    for m in range(2):
                        n = 2 * i + m
                        sp.wait_ge(final, n + 1)
                        row = (f + m * HF) * P
                        sp.dma_start(core.spectra[o, s, row:row + P, :], out[n % RS][:, :]
                                     ).then_inc(core.hstore[n % RS].sem, 16)
                for j in range(RS):
                    sp.wait_ge(core.hstore[j].sem, core.hstore[j].at(len(range(j, 2 * len(pairs), RS))))

            @block.tensor
            def _(pe):
                pe.wait_ge(small, 16 * 8)
                for layer, (w, x, k) in enumerate(((w1, z, POS), (w2, h, HFF))):
                    if layer:
                        pe.wait_ge(sines, 1)
                    for t in range(2):
                        last = nc.tensor.matmul(bank[6 + t][0:HFF, :], w[0:k, :], x[0:k, t * BANK:(t + 1) * BANK],
                                                start=True, stop=True)
                    last.then_inc(lay, 1)
                pe.wait_ge(sines, 2)
                pe.wait_ge(ones_set, 1)

                for u in range(NU):
                    j, o = divmod(u, 2)
                    if u >= 2:
                        pe.wait_ge(windowed, u - 1)
                    for s in range(2):
                        last = nc.tensor.matmul(bank[2 * (u % 2) + s][:, :], h[:, j * P:(j + 1) * P],
                                                w3[:, (2 * o + s) * HY:(2 * o + s + 1) * HY], start=True, stop=True)
                    last.then_inc(taps, 1)
                pe.wait_ge(summed, NU)
                for o in range(2):
                    nc.tensor.matmul(bank[6 + o][:, :], ones[:, :], acc[o][:, :], start=True, stop=True).then_inc(normed, 1)
                pe.wait_ge(folded, NU)
                pe.wait_ge(windowed, NU)
                pe.wait_ge(tables, 32)
                for i, (o, f, s) in enumerate(pairs):
                    if i >= 3:
                        pe.wait_ge(scaled, 2 * (i - 2))
                    for odd in range(2):
                        for j in range(HF):
                            jj = odd * HF + j
                            last = nc.tensor.matmul(bank[2 * (i % 3) + odd][:, :], tab[s][:, jj, f * P:(f + 1) * P],
                                                    fold[o][s][:, jj, :], start=(j == 0), stop=(j == HF - 1))
                        last.then_inc(spec, 1)

            @block.scalar
            def _(act):
                for layer in range(2):
                    act.wait_ge(gains, layer + 1)
                    nc.scalar.activation(h[:, :], lin[:, :], ACT.Sin).then_inc(sines, 1)

                for u in range(NU):
                    act.wait_ge(windowed, u + 1)
                    if u >= 2:
                        act.wait_ge(summed, u - 1)
                    nc.scalar.activation(aa[u % 2][:, :], ha[u % 2][:, :], ACT.Abs)
                    nc.scalar.activation(ab[u % 2][:, :], hb[u % 2][:, :], ACT.Abs).then_inc(absd, 1)

            @block.gpsimd
            def _(pool):
                nc.gpsimd.memset(ones[:, :], 1.0).then_inc(ones_set, 1)
                for u in range(NU):
                    j, o = divmod(u, 2)
                    pool.wait_ge(windowed, u + 1)
                    nc.gpsimd.tensor_tensor(fold[o][0][:, j, :], ha[u % 2][:, :], hb[u % 2][:, :], ALU.add)
                    nc.gpsimd.tensor_tensor(fold[o][1][:, j, :], ha[u % 2][:, :], hb[u % 2][:, :],
                                            ALU.subtract).then_inc(folded, 1)
                for i, (o, f, s) in enumerate(pairs):
                    pool.wait_ge(scaled, 2 * (i + 1))
                    for m in range(2):
                        n = 2 * i + m
                        if n >= RS:
                            pool.wait_ge(core.hstore[n % RS].sem, core.hstore[n % RS].at(n // RS))
                        a, b = (eo[0], eo[1]) if s == 0 else (eo[1], eo[0])
                        nc.gpsimd.tensor_tensor(out[n % RS][:, :], a[i % 2][:, :], b[i % 2][:, :],
                                                ALU.subtract if m else ALU.add).then_inc(final, 1)

            @block.vector
            def _(dve):
                step = lambda ins: core.dve(dve, ins)
                for layer, (b, fr) in enumerate(((b1, fr1), (b2, fr2))):
                    dve.wait_ge(lay, layer + 1)
                    if layer:
                        dve.wait_ge(sines, 1)
                    for t in range(2):
                        c = slice(t * BANK, (t + 1) * BANK)
                        step(nc.vector.tensor_scalar(lin[:, c], bank[6 + t][0:HFF, :], b, fr, ALU.add, ALU.mult))
                    step(nc.vector.tensor_scalar(turns[:, :], lin[:, :], 1.0 / TWO_PI, ROUND, ALU.mult, ALU.add))
                    step(nc.vector.tensor_scalar(turns[:, :], turns[:, :], ROUND, None, ALU.subtract))
                    step(nc.vector.scalar_tensor_tensor(lin[:, :], turns[:, :], -TWO_PI_HI, lin[:, :], ALU.mult, ALU.add))
                    step(nc.vector.scalar_tensor_tensor(lin[:, :], turns[:, :], -TWO_PI_LO, lin[:, :], ALU.mult, ALU.add))
                    nc.vector.tensor_scalar(lin[:, :], lin[:, :], PI_IN, -PI_IN, ALU.min, ALU.max).then_inc(gains, 1)

                def add_up(u):
                    j, o = divmod(u, 2)
                    dve.wait_ge(absd, u + 1)
                    if j:
                        step(nc.vector.tensor_tensor(acc[o][:, :], acc[o][:, :], aa[u % 2][:, :], ALU.add))
                        ins = nc.vector.tensor_tensor(acc[o][:, :], acc[o][:, :], ab[u % 2][:, :], ALU.add)
                    else:
                        ins = nc.vector.tensor_tensor(acc[o][:, :], aa[u % 2][:, :], ab[u % 2][:, :], ALU.add)
                    ins.then_inc(summed, 1)
                    dve.wait_ge(summed, u + 1)

                for u in range(NU):
                    j, o = divmod(u, 2)
                    dve.wait_ge(taps, u + 1)
                    if u >= 2:
                        dve.wait_ge(folded, u - 1)
                        dve.wait_ge(absd, u - 1)
                    nc.vector.tensor_tensor(ha[u % 2][:, :], bank[2 * (u % 2)][:, :], win[:, j, :], ALU.mult)
                    nc.vector.tensor_tensor(hb[u % 2][:, :], bank[2 * (u % 2) + 1][:, :],
                                            win0[:, :] if j == 0 else win[:, j, :], ALU.mult).then_inc(windowed, 1)
                    if u:
                        add_up(u - 1)
                add_up(NU - 1)
                dve.wait_ge(normed, 2)
                for o in range(2):
                    step(nc.vector.tensor_scalar(gain[o][:, :], bank[6 + o][:, :], EPS, None, ALU.add))
                    step(nc.vector.reciprocal(gain[o][:, :], gain[o][:, :]))
                    step(nc.vector.tensor_scalar(gain[o][:, :], gain[o][:, :], 0.5 / SEQ, None, ALU.mult))
                    step(nc.vector.tensor_scalar(skip[o][:, :], skip[o][:, :], 0.5 / SEQ, None, ALU.mult))
                for i, (o, f, s) in enumerate(pairs):
                    if i >= 2:
                        dve.wait_ge(final, 2 * (i - 1))
                    for odd in range(2):
                        dve.wait_ge(spec, 2 * i + odd + 1)
                        to = eo[odd][i % 2][:, :]
                        ins = nc.vector.tensor_tensor(to, bank[2 * (i % 3) + odd][:, :], gain[o][:, :], ALU.mult)
                        if s == 0 and odd == 0:
                            step(ins)
                            ins = nc.vector.tensor_tensor(to, to, skip[o][:, :], ALU.add)
                        ins.then_inc(scaled, 1)
        for j in range(RS):
            core.hstore[j].close(len(range(j, 2 * len(pairs), RS)))


def stage_hyena(core, name="hyena"):
    nc, io = core.nc, core.io
    CH, TH = HY // P, SEQ // 2
    RAW, RSP = 2, 4
    with Stage(core, name) as st:
        raw = [st.sb(f"raw{i}", [P, SEQ]) for i in range(RAW)]
        mix = [st.sb(f"mix{i}", [P, SEQ]) for i in range(3 * CH)]
        fwd = [st.sb("fwd_add", [P, 4, SEQ]), st.sb("fwd_sub", [P, 4, SEQ])]
        inv = [st.sb("inv_add", [P, NT, TH]), st.sb("inv_sub", [P, NT, TH])]
        spec = [st.sb(f"spec{i}", [P, 2, HY]) for i in range(RSP)]
        fs = [[st.sb(f"fold{s}{i}", [P, TH]) for s in "ad"] for i in range(2)]
        u = [st.sb("u_add", [P, 4, HY]), st.sb("u_sub", [P, 4, HY])]
        pq = [st.sb("p", [P, NT, HY]), st.sb("q", [P, NT, HY])]
        prod = [st.sb(f"prod{i}", [P, TH]) for i in range(4)]
        bsb, sm, df = st.sb("bsb", [P, TH]), prod[2], prod[3]
        ones = st.sb("ones", [P, 1])
        bank = st.banks(8)
        (table, lohi, folded, turned, u_ready, spectrum, multiplied, filtered, back, b_copied, used, y_done,
         squared, ssq, rooted, ones_set) = (st.sem(k) for k in (
             "table", "lohi", "folded", "turned", "u_ready", "spectrum", "multiplied", "filtered", "back",
             "b_copied", "used", "y_done", "squared", "ssq", "rooted", "ones"))
        w0, b0 = AT_A["hy_conv_w"], AT_A["hy_conv_b"]
        order = [0, 1, 2, 3, 4, 5, 6, 7, 8, 9, 10, 11]

        def half(tile, h):
            return tile[:, 0:TH] if h == 0 else tile[:, SEQ - 1:TH - 1:-1]

        with st.block() as block:
            @block.sync
            def _(sp):
                for i in order:
                    if i >= RAW:
                        sp.wait_ge(used, i - RAW + 1)
                    sp.dma_start(raw[i % RAW][:, :], core.proj_t[i * P:(i + 1) * P, 0:SEQ]
                                 ).then_inc(core.load[i % RAW].sem, 16)

            @block.gpsimd
            def _(pool):
                nc.gpsimd.memset(ones[:, :], 1.0).then_inc(ones_set, 1)
                for o in range(2):
                    for c in range(CH):
                        n = o * CH + c
                        pool.wait_ge(lohi, n + 1)
                        if n >= 2:
                            pool.wait_ge(turned, 2 * (n - 1))
                        lo, hi = (half(mix[c], 0), half(mix[c], 1)) if o == 0 else (mix[c][:, 0:TH], mix[c][:, TH:SEQ])
                        nc.gpsimd.tensor_tensor(fs[n % 2][0][:, :], lo, hi, ALU.add)
                        nc.gpsimd.tensor_tensor(fs[n % 2][1][:, :], lo, hi, ALU.subtract).then_inc(folded, 1)
                    for f in range(NT):
                        n = o * NT + f
                        pool.wait_ge(multiplied, n + 1)
                        nc.gpsimd.tensor_tensor(pq[0][:, f, :], prod[0][:, :], prod[1][:, :], ALU.add)
                        nc.gpsimd.tensor_tensor(pq[1][:, f, :], prod[2][:, :], prod[3][:, :],
                                                ALU.subtract).then_inc(filtered, 1)

            @block.scalar
            def _(act):
                act.dma_start(fwd[0][:, :, :], io["t_fwd_add"].rearrange("(j p) k -> p j k", p=P)).then_inc(table, 16)
                act.dma_start(fwd[1][:, :, :], io["t_fwd_sub"].rearrange("(j p) k -> p j k", p=P)).then_inc(table, 16)
                act.dma_start(inv[0][:, :, :], io["t_inv_add"].rearrange("(j p) k -> p j k", p=P)).then_inc(table, 16)
                act.dma_start(inv[1][:, :, :], io["t_inv_sub"].rearrange("(j p) k -> p j k", p=P)).then_inc(table, 16)
                for o in range(2):
                    for f in range(min(NT, RSP) if o == 0 else 0):
                        act.dma_start(spec[f][:, :, :], core.spectra[0, :, f * P:(f + 1) * P, :].rearrange("s p c -> p s c")
                                      ).then_inc(core.load[4 + f].sem, 16)
                    for c in range(CH):
                        for s in range(2):
                            n = 2 * (o * CH + c) + s
                            act.wait_ge(turned, n + 1)
                            nc.scalar.activation(u[s][:, :, c * P:(c + 1) * P],
                                                 bank[n % 2][:, :].rearrange("p (j c) -> p j c", c=P),
                                                 ACT.Copy).then_inc(u_ready, 1)
                    for f in range(NT):
                        n = o * NT + f + RSP
                        if n < 2 * NT:
                            act.wait_ge(multiplied, n - RSP + 1)
                            act.dma_start(spec[n % RSP][:, :, :],
                                          core.spectra[n // NT, :, (n % NT) * P:(n % NT + 1) * P, :].rearrange("s p c -> p s c")
                                          ).then_inc(core.load[4 + n % RSP].sem, 16)
                    for c in range(CH):
                        n = o * CH + c
                        act.wait_ge(back, n + 1)
                        if n:
                            act.wait_ge(lohi if n <= CH else y_done, CH + n if n <= CH else n - CH)
                        nc.scalar.activation(bsb[:, :], bank[2 + 2 * (n % 3) + 1][:, :], ACT.Copy).then_inc(b_copied, 1)
                        if o:
                            act.wait_ge(y_done, c + 1)
                            core.act(act, nc.scalar.activation(mix[CH + c][:, :], mix[2 * CH + c][:, :], ACT.Square))
                            nc.scalar.activation(mix[c][:, :], mix[2 * CH + c][:, :], ACT.Copy,
                                                 scale=core.col_a[:, AT_A["hy_norm_g"] + c:AT_A["hy_norm_g"] + c + 1]
                                                 ).then_inc(squared, 1)
                            act.wait_ge(squared, c + 1)
                            act.dma_start(core.mix_t[c * P:(c + 1) * P, :], mix[c][:, :]).then_inc(core.hstore[c].sem, 16)
                act.wait_ge(ssq, 1)
                nc.scalar.activation(core.hy_rms[:, :], bank[0][:, 0:NT], ACT.Sqrt, bias=core.eps[:, 0:1],
                                     scale=1.0 / HY).then_inc(rooted, 1)
                for c in range(CH):
                    act.wait_ge(core.hstore[c].sem, core.hstore[c].at(1))

            @block.tensor
            def _(pe):
                for o in range(2):
                    for c in range(CH):
                        n = o * CH + c
                        pe.wait_ge(folded, n + 1)
                        for s in range(2):
                            if 2 * n + s >= 2:
                                pe.wait_ge(u_ready, 2 * n + s - 1)
                            for j in range(4):
                                last = nc.tensor.transpose(bank[s][:, j * P:(j + 1) * P],
                                                           fs[n % 2][s][:, j * P:(j + 1) * P], core.ident[:, :])
                            last.then_inc(turned, 1)
                    pe.wait_ge(u_ready, 2 * CH * (o + 1))
                    pe.wait_ge(table, 64)
                    for f in range(NT):
                        n = o * NT + f
                        if n >= 3:
                            pe.wait_ge(multiplied, n - 2)
                        if f < 3 and o:
                            pe.wait_ge(lohi, 2 * CH)
                        for s in range(2):
                            src = u[s] if f < NT // 2 else u[1 - s]
                            for j in range(4):
                                last = nc.tensor.matmul(bank[2 + 2 * (n % 3) + s][:, :], fwd[s][:, j, f * P:(f + 1) * P],
                                                        src[:, j, :], start=(j == 0), stop=(j == 3))
                        last.then_inc(spectrum, 1)
                    pe.wait_ge(filtered, NT * (o + 1))
                    for c in range(CH):
                        n = o * CH + c
                        if c == 0:
                            pe.wait_ge(multiplied, NT * (o + 1))
                        if c == 3:
                            pe.wait_ge(lohi if o == 0 else y_done, CH + 1 if o == 0 else 1)
                        for s in range(2):
                            for i, f in enumerate(list(range(NT))):
                                even = f < NT // 2
                                k = s if even else 1 - s
                                last = nc.tensor.matmul(bank[2 + 2 * (n % 3) + s][:, :],
                                                        pq[k][:, f, c * P:(c + 1) * P], inv[k][:, f, :],
                                                        start=(i == 0), stop=(i == NT - 1))
                        last.then_inc(back, 1)
                pe.wait_ge(squared, CH)
                pe.wait_ge(ones_set, 1)
                for t in range(NT):
                    for c in range(CH):
                        last = nc.tensor.matmul(bank[0][:, t:t + 1], mix[CH + c][:, t * P:(t + 1) * P], ones[:, :],
                                                start=(c == 0), stop=(c == CH - 1))
                last.then_inc(ssq, 1)

            @block.vector
            def _(dve):
                step = lambda ins: core.dve(dve, ins)

                def short_conv(i):
                    dve.wait_ge(core.load[i % RAW].sem, core.load[i % RAW].at(i // RAW + 1))
                    w = [core.col_a[:, w0 + 12 * j + i:w0 + 12 * j + i + 1] for j in range(3)]
                    r = raw[i % RAW][:, :].rearrange("p (r c) -> p r c", c=GRID)
                    m = mix[i][:, :].rearrange("p (r c) -> p r c", c=GRID)
                    step(nc.vector.tensor_scalar(mix[i][:, :], raw[i % RAW][:, :], w[1], core.col_a[:, b0 + i:b0 + i + 1],
                                                 ALU.mult, ALU.add))
                    step(nc.vector.scalar_tensor_tensor(m[:, :, 1:GRID], r[:, :, 0:GRID - 1], w[0], m[:, :, 1:GRID],
                                                        ALU.mult, ALU.add))
                    return nc.vector.scalar_tensor_tensor(m[:, :, 0:GRID - 1], r[:, :, 1:GRID], w[2],
                                                          m[:, :, 0:GRID - 1], ALU.mult, ALU.add)

                for i in range(CH):
                    short_conv(i).then_inc(used, 1)
                    dve.wait_ge(used, i + 1)
                    dve.sem_inc(lohi, 1)
                for i in range(CH, 3 * CH):
                    short_conv(i).then_inc(used, 1)
                dve.wait_ge(used, 3 * CH)
                for o in range(2):
                    for f in range(NT):
                        n = o * NT + f
                        dve.wait_ge(spectrum, n + 1)
                        dve.wait_ge(core.load[4 + n % RSP].sem, core.load[4 + n % RSP].at(n // RSP + 1))
                        if n:
                            dve.wait_ge(filtered, n)
                        p, q = bank[2 + 2 * (n % 3)][:, :], bank[2 + 2 * (n % 3) + 1][:, :]
                        c_, d_ = spec[n % RSP][:, 0, :], spec[n % RSP][:, 1, :]
                        nc.vector.tensor_tensor(prod[0][:, :], p, c_, ALU.mult)
                        nc.vector.tensor_tensor(prod[1][:, :], q, d_, ALU.mult)
                        nc.vector.tensor_tensor(prod[2][:, :], q, c_, ALU.mult)
                        nc.vector.tensor_tensor(prod[3][:, :], p, d_, ALU.mult).then_inc(multiplied, 1)
                    for c in range(CH):
                        n = o * CH + c
                        a = bank[2 + 2 * (n % 3)][:, :]
                        dve.wait_ge(b_copied, n + 1)
                        step(nc.vector.tensor_tensor(sm[:, :], a, bsb[:, :], ALU.add))
                        step(nc.vector.tensor_tensor(df[:, :], a, bsb[:, :], ALU.subtract))
                        x = mix[(o + 1) * CH + c]
                        if o == 0:
                            nc.vector.tensor_tensor(mix[c][:, 0:TH], sm[:, :], half(x, 0), ALU.mult)
                            nc.vector.tensor_tensor(mix[c][:, TH:SEQ], df[:, :], half(x, 1), ALU.mult).then_inc(lohi, 1)
                            dve.wait_ge(lohi, CH + c + 1)
                        else:
                            nc.vector.tensor_tensor(x[:, 0:TH], sm[:, :], half(x, 0), ALU.mult)
                            nc.vector.tensor_tensor(half(x, 1), df[:, :], half(x, 1), ALU.mult).then_inc(y_done, 1)
                            dve.wait_ge(y_done, c + 1)
                dve.wait_ge(rooted, 1)
                step(nc.vector.reciprocal(core.hy_rstd[:, :], core.hy_rms[:, :]))
        for j in range(RAW):
            core.load[j].close(3 * CH // RAW)
        for j in range(RSP):
            core.load[4 + j].close(2 * NT // RSP)
        for j in range(CH):
            core.hstore[j].close(1)


def stage_hgrn(core, name="hgrn"):
    nc, io = core.nc, core.io
    H, TL = HG_HEADS, NT + NC_
    ORDER = [[NT + c for c in range(NC_)] + list(range(NT)), [NT + c for c in reversed(range(NC_))] + list(reversed(range(NT)))]
    STEPS = TL - 1
    UT = NT // 2
    NP = 2 * LEVELS
    NB = 2
    with Stage(core, name) as st:
        z = [st.sb(f"z{d}", [P, TL * P]) for d in range(2)]
        gates, X = st.sb("gates", [P, TL, P + 1]), [st.sb(f"x{d}", [P, TL, P + 1]) for d in range(2)]
        carry = st.sb("carry", [P, TL, P + 1])
        k_ = [[st.sb(f"k{d}{i}", [P, TL, P]) for d in range(2)] for i in range(2)]
        ksum = [st.sb(f"ksum{i}", [P, NT, P]) for i in range(2)]
        q_ = [st.sb(f"q{i}", [P, NT, P]) for i in range(2)]
        qh = [[st.sb(f"qh{d}{i}", [P, NT, P]) for d in range(2)] for i in range(2)]
        kh = [st.sb(f"kh{d}", [P, TL, P]) for d in range(2)]
        dec = [[st.sb(f"dec{d}{i}", [P, TL]) for d in range(2)] for i in range(2)]
        S = [[st.sb(f"s{d}{i}", [P, NT, P]) for d in range(2)] for i in range(2)]
        s0 = st.sb("s0", [P, P])
        R = [st.sb(f"r{i}", [P, NP, UT, P]) for i in range(2)]
        kt = [st.sb(f"kt{i}", [P, P]) for i in range(4)]
        masked = [st.sb(f"masked{i}", [P, 4, P]) for i in range(4)]
        ob = [st.sb(f"ob{i}", [P, P]) for i in range(4)]
        v = st.sb("v", [P, TL, BANK])
        mask = st.sb("mask", [P, 4 * NB, P])
        bank = st.banks(8)
        (inputs, zeroed, sig, qsilu, qscaled, fdone, gdone, xdone, ddk, ek, khd, turned, kts, ds, sdone, dd, ed,
         rd, prod, maskd, odone, ocopied) = (st.sem(x) for x in (
             "inputs", "zeroed", "sigmoid", "q_silu", "q_scaled", "f", "log_f", "x", "carry_exponent", "carry_exp",
             "carried", "turned", "kt", "ds", "state", "exponent", "exp", "level", "product", "masked", "o", "o_copied"))

        def blocks(ap, l):
            return ap.rearrange("p t (b r) -> p t b r", r=P >> l)

        def piece_of(j, u):
            side, l = divmod(j, LEVELS)
            return blocks(R[u % 2][:, j, :, :], l), P >> l + 1, side, l

        def running(d, l, u):
            t0, shift = (u % 2) * UT, 1 - d
            m = blocks(X[d][:, t0:t0 + UT, 0:P], l)[:, :, :, P >> l + 1:(P >> l + 1) + 1]
            return (blocks(X[d][:, t0:t0 + UT, shift:shift + P], l), m.to_broadcast([P, UT, 1 << l, P >> l + 1]))

        with st.block() as block:
            @block.sync
            def _(sp):
                sp.dma_start(v[:, :, :], core.vg[:, 0:BANK].rearrange("(t p) c -> p t c", p=P)).then_inc(inputs, 16)
                sp.dma_start(mask[:, :, :], io["t_pair_masks"].rearrange("p (i t) -> p i t", t=P)).then_inc(inputs, 16)
                for h in range(H):
                    for d in range(2):
                        if h:
                            sp.wait_ge(xdone, 2 * (h - 1) + d + 1)
                        row = (16 + 4 * d + h) * P
                        sp.dma_start(z[d][:, :], core.proj_t[row:row + P, :]).then_inc(core.load[d].sem, 16)
                    if h >= 2:
                        sp.wait_ge(prod, NB * NT * (h - 1))
                        sp.wait_ge(khd, 2 * (h - 1))
                    row = (12 + h) * P
                    sp.dma_start(q_[h % 2][:, :, :], core.proj_t[row:row + P, 0:SEQ].rearrange("p (t c) -> p t c", c=P)
                                 ).then_inc(core.load[2 + h % 2].sem, 16)

            @block.gpsimd
            def _(pool):
                nc.gpsimd.memset(gates[:, :, 0:1], 0.0)
                nc.gpsimd.memset(carry[:, :, :], 1.0).then_inc(zeroed, 1)
                pool.wait_ge(zeroed, 1)
                nc.gpsimd.memset(carry[:, :, 0:1], 0.0).then_inc(zeroed, 1)

                def prep(h):
                    for d in range(2):
                        pool.wait_ge(ek, 2 * h + d + 1)
                        nc.gpsimd.tensor_tensor(kh[d][:, :, :], kh[d][:, :, :], k_[h % 2][d][:, :, :], ALU.mult)
                        nc.gpsimd.tensor_tensor(qh[h % 2][d][:, :, :], qh[h % 2][d][:, :, :], q_[h % 2][:, :, :],
                                                ALU.mult).then_inc(khd, 1)

                def level(u, j):
                    pool.wait_ge(ed, u * NP + j + 1)
                    out, half, side, l = piece_of(j, u)
                    b, t0 = u // 2 % 2, u % 2 * UT
                    if side:
                        r = R[u % 2][:, j, :, :]
                        nc.gpsimd.tensor_tensor(r, r, q_[b][:, t0:t0 + UT, :], ALU.mult).then_inc(rd, 1)
                    else:
                        kf, kb = (blocks(k_[b][d][:, t0:t0 + UT, :], l) for d in range(2))
                        nc.gpsimd.tensor_tensor(out[:, :, :, 0:half], out[:, :, :, 0:half], kf[:, :, :, 0:half], ALU.mult)
                        nc.gpsimd.tensor_tensor(out[:, :, :, half:], out[:, :, :, half:], kb[:, :, :, half:],
                                                ALU.mult).then_inc(rd, 1)

                def store(h, t):
                    n = h * NT + t
                    pool.wait_ge(ocopied, n + 1)
                    pool.dma_start(core.hg_o[t * P:(t + 1) * P, h * P:(h + 1) * P], ob[n % 4][:, :]
                                   ).then_inc(core.store[n % 4].sem, 16)

                prep(0)
                for j in range(NP):
                    level(0, j)
                for u in range(2 * H):
                    h, second = divmod(u, 2)
                    if second and h + 1 < H:
                        prep(h + 1)
                    for a in range(UT):
                        if u + 1 < 2 * H:
                            for b in range(4):
                                if 4 * a + b < NP:
                                    level(u + 1, 4 * a + b)
                        if a:
                            store(h, second * UT + a - 1)
                    store(h, second * UT + UT - 1)
                for j in range(4):
                    pool.wait_ge(core.store[j].sem, core.store[j].at(H * NT // 4))

            @block.scalar
            def _(act):
                def prep(h):
                    for d in range(2):
                        act.wait_ge(core.load[d].sem, core.load[d].at(h + 1))
                        nc.scalar.activation(z[d][:, :], z[d][:, :], ACT.Sigmoid).then_inc(sig, 1)
                    act.wait_ge(core.load[2 + h % 2].sem, core.load[2 + h % 2].at(h // 2 + 1))
                    nc.scalar.activation(q_[h % 2][:, :, :], q_[h % 2][:, :, :], ACT.Silu).then_inc(qsilu, 1)
                    for d in range(2):
                        i = 2 * h + d
                        act.wait_ge(fdone, i + 1)
                        if i:
                            act.wait_ge(xdone, i)
                        else:
                            act.wait_ge(zeroed, 2)
                        nc.scalar.activation(gates[:, :, 1:P + 1], z[d][:, :].rearrange("p (t c) -> p t c", c=P),
                                             ACT.Ln).then_inc(gdone, 1)
                    for d in range(2):
                        i = 2 * h + d
                        act.wait_ge(ddk, i + 1)
                        x = X[d]
                        nc.scalar.activation(dec[h % 2][d][:, :], x[:, :, P], ACT.Exp)
                        if d == 0:
                            nc.scalar.activation(kh[d][:, :, :], kh[d][:, :, :], ACT.Exp)
                            nc.scalar.activation(qh[h % 2][d][:, :, :], x[:, 0:NT, 1:P + 1], ACT.Exp).then_inc(ek, 1)
                        else:
                            nc.scalar.activation(kh[d][:, :, :], x[:, :, 0:P], ACT.Exp)
                            nc.scalar.activation(qh[h % 2][d][:, :, :], qh[h % 2][d][:, :, :], ACT.Exp).then_inc(ek, 1)

                def level(u, j):
                    act.wait_ge(dd, u * NP + j + 1)
                    r = R[u % 2][:, j, :, :]
                    nc.scalar.activation(r, r, ACT.Exp).then_inc(ed, 1)

                def kt_copy(h, s):
                    n = h * 2 * STEPS + s
                    act.wait_ge(turned, n + 1)
                    if n >= 4:
                        act.wait_ge(ds, n - 3)
                    nc.scalar.activation(kt[n % 4][:, :], bank[4 + n % 2][:, 0:P], ACT.Copy).then_inc(kts, 1)

                def o_copy(h, t):
                    n = h * NT + t
                    act.wait_ge(odone, n + 1)
                    if n >= 4:
                        act.wait_ge(core.store[n % 4].sem, core.store[n % 4].at(n // 4))
                    nc.scalar.activation(ob[n % 4][:, :], bank[3][:, 0:P], ACT.Copy).then_inc(ocopied, 1)

                prep(0)
                for s in range(2 * STEPS):
                    kt_copy(0, s)
                for j in range(NP):
                    level(0, j)
                for u in range(2 * H):
                    h, second = divmod(u, 2)
                    if second and h + 1 < H:
                        prep(h + 1)
                    for a in range(UT):
                        if u + 1 < 2 * H:
                            for b in range(4):
                                if 4 * a + b < NP:
                                    level(u + 1, 4 * a + b)
                        if second and h + 1 < H:
                            for s in range(5 * a, min(5 * a + 5, 2 * STEPS)):
                                kt_copy(h + 1, s)
                        if a:
                            o_copy(h, second * UT + a - 1)
                    o_copy(h, second * UT + UT - 1)

            @block.tensor
            def _(pe):
                def step_of(s):
                    return divmod(s, STEPS)

                def turn(h, s):
                    d, i = step_of(s)
                    n = h * 2 * STEPS + s
                    pe.wait_ge(khd, 2 * h + d + 1)
                    if n >= 2:
                        pe.wait_ge(kts, n - 1)
                    nc.tensor.transpose(bank[4 + n % 2][:, 0:P], kh[d][:, ORDER[d][i], :],
                                        core.ident[:, :]).then_inc(turned, 1)

                def state(h, s):
                    d, i = step_of(s)
                    n = h * 2 * STEPS + s
                    pe.wait_ge(kts, n + 1)
                    if n >= 2:
                        pe.wait_ge(sdone, n - 1)
                    nc.tensor.matmul(bank[6 + n % 2][:, 0:P], kt[n % 4][:, :],
                                     v[:, ORDER[d][i], h * P:(h + 1) * P], start=True, stop=True).then_inc(ds, 1)

                def states(h, s0_, s1):
                    for s in range(s0_, s1):
                        turn(h, s)
                        if s > s0_:
                            state(h, s - 1)
                    state(h, s1 - 1)

                def out(h, t):
                    n = h * NT + t
                    if n:
                        pe.wait_ge(ocopied, n)
                    o = bank[3][:, 0:P]
                    for b in range(NB):
                        m = NB * n + b
                        pe.wait_ge(maskd, m + 1)
                        for i in range(4):
                            nc.tensor.matmul(o, masked[m % 4][:, i, :], v[:, t, h * P:(h + 1) * P],
                                             start=(b + i == 0), stop=False)
                    if t == 0:
                        pe.wait_ge(sdone, 2 * STEPS * (h + 1))
                    for d in range(2):
                        last = nc.tensor.matmul(o, qh[h % 2][d][:, t, :], S[h % 2][d][:, t, :], start=False, stop=(d == 1))
                    last.then_inc(odone, 1)

                pe.wait_ge(inputs, 32)
                states(0, 0, 2 * STEPS)
                for u in range(2 * H):
                    h, second = divmod(u, 2)
                    pe.wait_ge(rd, NP * (u + 1))
                    for a in range(UT):
                        t = second * UT + a
                        for b in range(NB):
                            m = NB * (h * NT + t) + b
                            if m >= 3:
                                pe.wait_ge(maskd, m - 2)
                            for i in range(4):
                                l = 4 * b + i
                                if l < LEVELS:
                                    lhs, rhs = R[u % 2][:, l, a, :], R[u % 2][:, LEVELS + l, a, :]
                                else:
                                    lhs, rhs = ksum[h % 2][:, t, :], q_[h % 2][:, t, :]
                                last = nc.tensor.matmul(bank[m % 3][:, i * P:(i + 1) * P], lhs, rhs, start=True, stop=True)
                            last.then_inc(prod, 1)
                            if b == 0 and a:
                                out(h, t - 1)
                        if second and h + 1 < H:
                            states(h + 1, 5 * a, min(5 * a + 5, 2 * STEPS))
                    out(h, second * UT + UT - 1)

            @block.vector
            def _(dve):
                step = lambda ins: core.dve(dve, ins)

                def prep(h):
                    b = h % 2
                    if h >= 2:
                        dve.wait_ge(prod, NB * NT * (h - 1))
                        dve.wait_ge(odone, NT * (h - 1))
                    for d in range(2):
                        dve.wait_ge(sig, 2 * h + d + 1)
                        c = d * 4 + h
                        nc.vector.tensor_scalar(z[d][:, :], z[d][:, :], core.lb[:, 1, c:c + 1], core.lb[:, 0, c:c + 1],
                                                ALU.mult, ALU.add).then_inc(fdone, 1)
                    dve.wait_ge(qsilu, h + 1)
                    nc.vector.tensor_scalar(q_[b][:, :, :], q_[b][:, :, :], float(P) ** -0.5, None,
                                            ALU.mult).then_inc(qscaled, 1)
                    for d in range(2):
                        i = 2 * h + d
                        dve.wait_ge(fdone, i + 1)
                        step(nc.vector.tensor_scalar(k_[b][d][:, :, :], z[d][:, :].rearrange("p (t c) -> p t c", c=P),
                                                     -1.0, 1.0, ALU.mult, ALU.add))
                        if d:
                            step(nc.vector.tensor_tensor(ksum[b][:, :, :], k_[b][0][:, 0:NT, :], k_[b][1][:, 0:NT, :], ALU.add))
                        dve.wait_ge(gdone, i + 1)
                        if i < 1:
                            dve.wait_ge(zeroed, 2)
                        if h:
                            dve.wait_ge(ek, i - 1)
                        nc.vector.tensor_tensor_scan(X[d][:, :, :].rearrange("p t c -> p (t c)"),
                                                     carry[:, :, :].rearrange("p t c -> p (t c)"),
                                                     gates[:, :, :].rearrange("p t c -> p (t c)"),
                                                     0.0, ALU.mult, ALU.add).then_inc(xdone, 1)
                        dve.wait_ge(xdone, i + 1)
                        if h:
                            dve.wait_ge(turned, 2 * STEPS * h - (STEPS if d == 0 else 0))
                        last = X[d][:, :, P:P + 1]
                        if d == 0:
                            nc.vector.tensor_tensor(kh[d][:, :, :], last.to_broadcast([P, TL, P]), X[d][:, :, 1:P + 1],
                                                    ALU.subtract).then_inc(ddk, 1)
                        else:
                            nc.vector.tensor_tensor(qh[b][d][:, :, :], last[:, 0:NT, :].to_broadcast([P, NT, P]),
                                                    X[d][:, 0:NT, 0:P], ALU.subtract).then_inc(ddk, 1)

                def level(u, j):
                    if u >= 2 and j == 0:
                        dve.wait_ge(prod, NB * UT * (u - 1))
                    out, half, side, l = piece_of(j, u)
                    (xl, ml), (xr, mr) = running(side, l, u), running(1 - side, l, u)
                    nc.vector.tensor_tensor(out[:, :, :, 0:half], ml, xl[:, :, :, 0:half], ALU.subtract)
                    nc.vector.tensor_tensor(out[:, :, :, half:], xr[:, :, :, half:], mr, ALU.subtract).then_inc(dd, 1)

                def carry_state(h, s):
                    d, i = divmod(s, STEPS)
                    n = h * 2 * STEPS + s
                    dve.wait_ge(ds, n + 1)
                    new = bank[6 + n % 2][:, 0:P]
                    to = s0[:, :] if i == 0 else S[h % 2][d][:, ORDER[d][i + 1], :]
                    if i == 0:
                        ins = nc.vector.tensor_copy(to, new)
                    else:
                        was = s0[:, :] if i == 1 else S[h % 2][d][:, ORDER[d][i], :]
                        t = ORDER[d][i]
                        ins = nc.vector.scalar_tensor_tensor(to, was, dec[h % 2][d][:, t:t + 1], new, ALU.mult, ALU.add)
                    ins.then_inc(sdone, 1)
                    dve.wait_ge(sdone, n + 1)

                prep(0)
                for s in range(2 * STEPS):
                    carry_state(0, s)
                for j in range(NP):
                    level(0, j)
                dve.wait_ge(inputs, 32)
                for u in range(2 * H):
                    h, second = divmod(u, 2)
                    if second and h + 1 < H:
                        prep(h + 1)
                    for a in range(UT):
                        t = second * UT + a
                        for b in range(NB):
                            n = h * NT + t
                            m = NB * n + b
                            dve.wait_ge(prod, m + 1)
                            if n >= 2:
                                dve.wait_ge(odone, n - 1)
                            nc.vector.tensor_tensor(masked[m % 4][:, :, :], bank[m % 3][:, :].rearrange("p (i t) -> p i t", t=P),
                                                    mask[:, 4 * b:4 * b + 4, :], ALU.mult).then_inc(maskd, 1)
                            for j in range(4 * a + 2 * b, 4 * a + 2 * b + 2):
                                if u + 1 < 2 * H and j < NP:
                                    level(u + 1, j)
                        if second and h + 1 < H:
                            for s in range(5 * a, min(5 * a + 5, 2 * STEPS)):
                                carry_state(h + 1, s)
        for j in range(2):
            core.load[j].close(H)
            core.load[2 + j].close(H // 2)
        for j in range(4):
            core.store[j].close(H * NT // 4)


def stage_mix_out(core, name="mixout"):
    nc, io = core.nc, core.io
    H = HG_HEADS
    with Stage(core, name) as st:
        o = [st.sb(f"o{i}", [P, H, P]) for i in range(2)]
        g = [st.sb(f"g{i}", [P, BANK]) for i in range(2)]
        og = [st.sb(f"og{i}", [P, H, P]) for i in range(2)]
        junk = st.sb("junk", [P, P])
        ss, rms = st.sb("ss", [P, NT, H]), st.sb("rms", [P, NT, H])
        yT = st.sb("yT", [P, KD, SEQ])
        w = st.sb("w", [P, KD, D])
        gate = st.sb("gate", [P, D])
        x = [st.sb(f"x{i}", [P, D]) for i in range(3)]
        out = [st.sb(f"out{i}", [P, BANK]) for i in range(4)]
        bank = st.banks(8)
        weights, rooted, silu, gated, turned, placed, product, added = (st.sem(k) for k in (
            "weights", "rooted", "silu", "gated", "turned", "placed", "product", "added"))
        with st.block() as block:
            @block.sync
            def _(sp):
                def tile(t):
                    if t >= 2:
                        sp.wait_ge(gated, t - 1)
                    sp.dma_start(o[t % 2][:, :, :], core.hg_o[t * P:(t + 1) * P, :].rearrange("p (h c) -> p h c", c=P)
                                 ).then_inc(core.load[t % 2].sem, 16)
                    sp.dma_start(g[t % 2][:, :], core.vg[t * P:(t + 1) * P, BANK:2 * BANK]
                                 ).then_inc(core.load[2 + t % 2].sem, 16)

                tile(0)
                tile(1)
                sp.dma_start(yT[:, 0:4, :], core.mix_t[0:HY, :].rearrange("(k p) t -> p k t", p=P)).then_inc(weights, 16)
                sp.dma_start(w[:, :, :], io["w_out"][0].rearrange("(k p) n -> p k n", p=P)).then_inc(weights, 16)
                sp.dma_start(gate[:, :], core.mod_rows[0][0, 2 * D:3 * D].partition_broadcast(P)).then_inc(weights, 16)
                for t in range(2, NT):
                    tile(t)
                for t in range(NT):
                    if t >= 3:
                        sp.wait_ge(added, 2 * (t - 2))
                    sp.dma_start(x[t % 3][:, :], io["x"][0][t * P:(t + 1) * P, :]).then_inc(core.load[4 + t % 3].sem, 16)

            @block.scalar
            def _(act):
                def place(t):
                    act.wait_ge(turned, t + 1)
                    nc.scalar.activation(yT[:, 4:8, t * P:(t + 1) * P],
                                         bank[t % 2][:, :].rearrange("p (k t) -> p k t", t=P), ACT.Copy,
                                         scale=core.col_a[:, AT_A["hg_norm_g"]:AT_A["hg_norm_g"] + 1]).then_inc(placed, 1)

                for t in range(NT):
                    act.wait_ge(core.load[t % 2].sem, core.load[t % 2].at(t // 2 + 1))
                    for h in range(H):
                        core.act(act, nc.scalar.activation(junk[:, :], o[t % 2][:, h, :], ACT.Square,
                                                           accum_out=ss[:, t, h:h + 1]))
                    nc.scalar.activation(rms[:, t, :], ss[:, t, :], ACT.Sqrt, bias=core.eps[:, 0:1],
                                         scale=1.0 / P).then_inc(rooted, 1)
                    act.wait_ge(core.load[2 + t % 2].sem, core.load[2 + t % 2].at(t // 2 + 1))
                    nc.scalar.activation(g[t % 2][:, :], g[t % 2][:, :], ACT.Silu).then_inc(silu, 1)
                    if t:
                        place(t - 1)
                place(NT - 1)

            @block.tensor
            def _(pe):
                for t in range(NT):
                    pe.wait_ge(gated, t + 1)
                    if t >= 2:
                        pe.wait_ge(placed, t - 1)
                    for h in range(H):
                        last = nc.tensor.transpose(bank[t % 2][:, h * P:(h + 1) * P], og[t % 2][:, h, :], core.ident[:, :])
                    last.then_inc(turned, 1)
                pe.wait_ge(weights, 48)
                pe.wait_ge(placed, NT)
                for t in range(NT):
                    for half in range(2):
                        n = 2 * t + half
                        if n >= 3:
                            pe.wait_ge(added, n - 2)
                        for part in range(2):
                            for k in range(4):
                                last = nc.tensor.matmul(bank[2 + 2 * (n % 3) + part][:, :],
                                                        yT[:, 4 * part + k, t * P:(t + 1) * P],
                                                        w[:, 4 * part + k, half * BANK:(half + 1) * BANK],
                                                        start=(k == 0), stop=(k == 3))
                        last.then_inc(product, 1)

            @block.vector
            def _(dve):
                step = lambda ins: core.dve(dve, ins)
                for t in range(NT):
                    dve.wait_ge(rooted, t + 1)
                    step(nc.vector.reciprocal(rms[:, t, :], rms[:, t, :]))
                    if t >= 2:
                        dve.wait_ge(turned, t - 1)
                    step(nc.vector.tensor_tensor(og[t % 2][:, :, :], o[t % 2][:, :, :],
                                                 rms[:, t, :].unsqueeze(2).to_broadcast([P, H, P]), ALU.mult))
                    dve.wait_ge(silu, t + 1)
                    nc.vector.tensor_tensor(og[t % 2][:, :, :], og[t % 2][:, :, :],
                                            g[t % 2][:, :].rearrange("p (h c) -> p h c", c=P), ALU.mult).then_inc(gated, 1)
                dve.wait_ge(weights, 48)
                for t in range(NT):
                    dve.wait_ge(core.load[4 + t % 3].sem, core.load[4 + t % 3].at(t // 3 + 1))
                    for half in range(2):
                        n = 2 * t + half
                        c = slice(half * BANK, (half + 1) * BANK)
                        dve.wait_ge(product, n + 1)
                        if n >= 4:
                            dve.wait_ge(core.store[n % 4].sem, core.store[n % 4].at(n // 4))
                        y = out[n % 4][:, :]
                        a, b = bank[2 + 2 * (n % 3)][:, :], bank[3 + 2 * (n % 3)][:, :]
                        step(nc.vector.tensor_scalar(y, a, core.hy_rstd[:, t:t + 1], None, ALU.mult))
                        step(nc.vector.tensor_tensor(y, y, b, ALU.add))
                        step(nc.vector.tensor_tensor(y, y, gate[:, c], ALU.mult))
                        nc.vector.tensor_tensor(y, y, x[t % 3][:, c], ALU.add).then_inc(added, 1)

            @block.gpsimd
            def _(pool):
                for n in range(2 * NT):
                    t, half = divmod(n, 2)
                    pool.wait_ge(added, n + 1)
                    pool.dma_start(core.x1[t * P:(t + 1) * P, half * BANK:(half + 1) * BANK], out[n % 4][:, :]
                                   ).then_inc(core.store[n % 4].sem, 16)
                for j in range(4):
                    pool.wait_ge(core.store[j].sem, core.store[j].at(NT // 2))
        for j in range(2):
            core.load[j].close(NT // 2)
            core.load[2 + j].close(NT // 2)
        for j in range(3):
            core.load[4 + j].close(len(range(j, NT, 3)))
        for j in range(4):
            core.store[j].close(NT // 2)


def stage_router(core, hT, name="router"):
    nc, io = core.nc, core.io
    ROUNDS = CAP // 8
    with Stage(core, name) as st:
        rw = st.sb("rw", [P, KD, E])
        iota, tokid = st.sb("iota", [P, P]), st.sb("tokid", [P, NT])
        aff, mx, sm = st.sb("aff", [P, NT, E]), st.sb("mx", [P, NT]), st.sb("sm", [P, NT])
        tv = st.sb("tv", [P, NT, E, 2])
        work, best = st.sb("work", [E, SEQ]), st.sb("best", [E, 8])
        mask, one, rank = st.sb("mask", [E, SEQ]), st.sb("one", [E, SEQ]), st.sb("rank", [E, SEQ])
        slot = st.sb("slot", [P, NT, E])
        hot = [st.sb(f"hot{i}", [P, NT, P]) for i in range(2)]
        bank = st.banks(5)
        inputs, logits, less, exps, ready, turned, ranked, unturned, onehot, picked, ones_set = (st.sem(k) for k in (
            "inputs", "logits", "less", "exps", "ready", "turned", "ranked", "unturned", "onehot", "picked", "ones"))
        with st.block() as block:
            @block.sync
            def _(sp):
                with nc.allow_non_contiguous_dma(reason="64-byte rows"):
                    sp.dma_start(rw[:, :, :], io["router_w"][0].rearrange("(k p) e -> p k e", p=P)).then_inc(inputs, 16)
                sp.dma_start(iota[:, :], io["t_iota"][:, 0:P]).then_inc(inputs, 16)
                sp.dma_start(tokid[:, :], io["t_tokid"]).then_inc(inputs, 16)

            @block.gpsimd
            def _(pool):
                nc.gpsimd.memset(one[:, :], 1.0).then_inc(ones_set, 1)

            @block.tensor
            def _(pe):
                pe.wait_ge(inputs, 48)
                for t in range(NT):
                    for k in range(KD):
                        last = nc.tensor.matmul(bank[0][:, t * E:(t + 1) * E], hT[:, k, t * P:(t + 1) * P], rw[:, k, :],
                                                start=(k == 0), stop=(k == KD - 1))
                last.then_inc(logits, 1)
                pe.wait_ge(ready, 1)
                for t in range(NT):
                    last = nc.tensor.transpose(bank[1 + t // 4][0:E, (t % 4) * P:(t % 4 + 1) * P], aff[:, t, :], core.ident[:, :])
                last.then_inc(turned, 1)
                pe.wait_ge(ranked, 1)
                for t in range(NT):
                    last = nc.tensor.transpose(bank[3][:, t * E:(t + 1) * E], rank[:, t * P:(t + 1) * P], core.ident[0:E, 0:E])
                last.then_inc(unturned, 1)
                for e in range(E):
                    pe.wait_ge(onehot, e + 1)
                    for t in range(NT):
                        last = nc.tensor.matmul(bank[4][:, 2 * e:2 * e + 2], hot[e % 2][:, t, :], tv[:, t, e, :],
                                                start=(t == 0), stop=(t == NT - 1))
                    last.then_inc(picked, 1)

            @block.scalar
            def _(act):
                act.wait_ge(less, 1)
                nc.scalar.activation(aff[:, :, :], aff[:, :, :], ACT.Exp).then_inc(exps, 1)

            @block.vector
            def _(dve):
                step = lambda ins: core.dve(dve, ins)
                dve.wait_ge(logits, 1)
                lg = bank[0][:, 0:NT * E].rearrange("p (t e) -> p t e", e=E)
                step(nc.vector.tensor_reduce(mx[:, :], lg, AX, ALU.max))
                nc.vector.tensor_tensor(aff[:, :, :], lg, mx[:, :].unsqueeze(2).to_broadcast([P, NT, E]),
                                        ALU.subtract).then_inc(less, 1)
                dve.wait_ge(exps, 1)
                step(nc.vector.tensor_reduce(sm[:, :], aff[:, :, :], AX, ALU.add))
                step(nc.vector.reciprocal(sm[:, :], sm[:, :]))
                nc.vector.tensor_tensor(aff[:, :, :], aff[:, :, :], sm[:, :].unsqueeze(2).to_broadcast([P, NT, E]),
                                        ALU.mult).then_inc(ready, 1)
                dve.wait_ge(inputs, 48)
                dve.wait_ge(ready, 1)
                step(nc.vector.tensor_copy(tv[:, :, :, 1], aff[:, :, :]))
                step(nc.vector.tensor_copy(tv[:, :, :, 0], tokid[:, :].unsqueeze(2).to_broadcast([P, NT, E])))
                dve.wait_ge(turned, 1)
                for h in range(2):
                    step(nc.vector.tensor_copy(work[:, h * BANK:(h + 1) * BANK], bank[1 + h][0:E, :]))
                for _r in range(ROUNDS):
                    step(nc.vector.max(best[:, :], work[:, :]))
                    step(nc.vector.match_replace(work[:, :], best[:, :], work[:, :], -1.0))
                step(nc.vector.tensor_scalar(mask[:, :], work[:, :], 0.0, None, ALU.is_lt))
                dve.wait_ge(ones_set, 1)
                step(nc.vector.tensor_tensor_scan(rank[:, :], one[:, :], mask[:, :], 0.0, ALU.mult, ALU.add))
                step(nc.vector.tensor_tensor(rank[:, :], rank[:, :], mask[:, :], ALU.mult))
                nc.vector.tensor_scalar(rank[:, :], rank[:, :], 1.0, None, ALU.subtract).then_inc(ranked, 1)
                dve.wait_ge(unturned, 1)
                step(nc.vector.tensor_copy(slot[:, :, :], bank[3][:, 0:NT * E].rearrange("p (t e) -> p t e", e=E)))
                for e in range(E):
                    if e >= 2:
                        dve.wait_ge(picked, e - 1)
                    nc.vector.tensor_tensor(hot[e % 2][:, :, :], iota[:, :].unsqueeze(1).to_broadcast([P, NT, P]),
                                            slot[:, :, e:e + 1].to_broadcast([P, NT, P]), ALU.is_equal).then_inc(onehot, 1)
                dve.wait_ge(picked, E)
                sel = bank[4][:, 0:2 * E].rearrange("p (e v) -> p e v", v=2)
                step(nc.vector.tensor_copy(core.moe_idx[:, :], sel[:, :, 0]))
                step(nc.vector.tensor_copy(core.moe_gate[:, :], sel[:, :, 1]))


def stage_moe(core, name="moe"):
    nc, io = core.nc, core.io
    RW, RP = 3, 3
    FG = FF // BANK
    UNITS = 3 * FG
    with Stage(core, name) as st:
        raw = [st.sb(f"raw{i}", [P, KD * BANK]) for i in range(RW)]
        w = [Parts(st, f"w{i}", [P, KD * BANK]) for i in range(RP)]
        xg = [st.sb(f"xg{i}", [P, D]) for i in range(2)]
        xw, xgT = st.sb("xw", [P, KD, P]), Parts(st, "xgT", [P, KD, P])
        sa = [st.sb(f"sa{i}", [P, BANK]) for i in range(2)]
        hid = [st.sb(f"hid{i}", [P, BANK]) for i in range(2)]
        hidT = Parts(st, "hidT", [P, FF // P, P])
        yo = [st.sb(f"yo{i}", [P, D]) for i in range(2)]
        g2 = st.sb("g2", [P, D])
        bank = st.banks(8)
        gathered, scattered = st.dma_sem("gathered"), st.dma_sem("scattered")
        (high, low, xwhole, gain, w_used, xturn, xplaced, silu, hidden, hturn, hhigh, hplaced, yout) = (
            st.sem(k) for k in ("high", "low", "x_whole", "gain", "w_used", "x_turned", "x_placed", "silu", "hidden",
                                "h_turned", "h_high", "h_placed", "y_out"))
        sc, sh = core.sc[2], core.mod1[:, 24:32, 0]

        def piece(e, i):
            if i < 2 * FG:
                src = io["exp_w1" if i % 2 == 0 else "exp_w3"][0][e][:, (i // 2) * BANK:(i // 2 + 1) * BANK]
                return src.rearrange("(k p) n -> p k n", p=P)
            q = i - 2 * FG
            return io["exp_w2"][0][e][q * BANK:(q + 1) * BANK, :].rearrange("(k p) n -> p k n", p=P)

        def w_view(n, cols, k, c0, c1):
            return w[n % RP][:, k * cols + c0:k * cols + c1]

        with st.block() as block:
            @block.sync
            def _(sp):
                sp.dma_start(g2[:, :], core.mod_rows[0][0, 5 * D:6 * D].partition_broadcast(P)).then_inc(gain, 16)
                for e in range(E):
                    for i in range(UNITS):
                        n = e * UNITS + i
                        if n >= RW:
                            sp.wait_ge(low, 2 * (n - RW + 1))
                        cols = BANK if i < 2 * FG else D
                        sp.dma_start(raw[n % RW][:, :].rearrange("p (k n) -> p k n", n=cols), piece(e, i)
                                     ).then_inc(core.load[n % RW].sem, 16)

            @block.gpsimd
            def _(pool):
                def gather(e):
                    if e >= 2:
                        pool.wait_ge(xturn, 2 * (e - 1))
                    pool.indirect_dma_start(out=xg[e % 2][:, :], out_offset=None, in_=core.xn2,
                                            in_offset=bass.IndirectOffsetOnAxis(ap=core.moe_idx[:, e:e + 1], axis=0)
                                            ).then_inc(gathered, 16)

                def split_x(e):
                    for half in range(2):
                        pool.wait_ge(xwhole, 2 * e + half + 1)
                        c = slice(4 * half, 4 * half + 4)
                        core.pool(pool, nc.gpsimd.tensor_copy(xgT.high[:, c, :], xw[:, c, :]))
                        nc.gpsimd.tensor_tensor(xgT.low[:, c, :], xw[:, c, :], xgT.high[:, c, :].bitcast(F32),
                                                ALU.subtract).then_inc(xplaced, 1)

                def scatter(e):
                    pool.wait_ge(yout, 2 * (e + 1))
                    if e:
                        pool.wait_ge(scattered, 16 * e)
                    pool.indirect_dma_start(out=core.x1, out_offset=bass.IndirectOffsetOnAxis(
                        ap=core.moe_idx[:, e:e + 1], axis=0), in_=yo[e % 2][:, :], in_offset=None,
                        compute_op=ALU.add).then_inc(scattered, 16)

                gather(0)
                split_x(0)
                for e in range(E):
                    if e + 1 < E:
                        pool.wait_ge(gathered, 16 * (e + 1))
                        gather(e + 1)
                    if e:
                        scatter(e - 1)
                    if e + 1 < E:
                        split_x(e + 1)
                scatter(E - 1)
                pool.wait_ge(scattered, 16 * E)

            @block.tensor
            def _(pe):
                def turn_x(e):
                    pe.wait_ge(gathered, 16 * (e + 1))
                    for half in range(2):
                        if e:
                            pe.wait_ge(hplaced, FG * (e - 1) + 3 + half)
                        for k in range(4):
                            c = (4 * half + k) * P
                            last = nc.tensor.transpose(bank[4 + half][:, k * P:(k + 1) * P], xg[e % 2][:, c:c + P],
                                                       core.ident[:, :])
                        last.then_inc(xturn, 1)

                def up_group(e, f):
                    n = e * FG + f
                    if n >= 2:
                        pe.wait_ge(hidden, n - 1)
                    for s in range(2):
                        u = e * UNITS + 2 * f + s
                        for k in range(KD):
                            if k % (KD // 2) == 0:
                                pe.wait_ge(low, 2 * u + k // (KD // 2) + 1)
                            last = product(nc, bank[2 * (n % 2) + s][:, :], xgT[:, k, :],
                                           w_view(u, BANK, k, 0, BANK), k == 0, k == KD - 1)
                        last.then_inc(w_used, 1)

                def turn_h(e, f):
                    n = e * FG + f
                    pe.wait_ge(hidden, n + 1)
                    if n >= 2:
                        pe.wait_ge(hplaced, n - 1)
                    pe.wait_ge(xwhole, 2 * (e + 1))
                    for k in range(4):
                        last = nc.tensor.transpose(bank[4 + n % 2][:, k * P:(k + 1) * P], hid[n % 2][:, k * P:(k + 1) * P],
                                                   core.ident[:, :])
                    last.then_inc(hturn, 1)

                def down(e, q):
                    u = e * UNITS + 2 * FG + q
                    if e and q == 0:
                        pe.wait_ge(yout, 2 * e)
                    pe.wait_ge(hplaced, e * FG + q + 1)
                    for kk in range(4):
                        if kk % 2 == 0:
                            pe.wait_ge(low, 2 * u + kk // 2 + 1)
                        k = 4 * q + kk
                        for half in range(2):
                            last = product(nc, bank[6 + half][:, :], hidT[:, k, :],
                                           w_view(u, D, kk, half * BANK, (half + 1) * BANK),
                                           k == 0, k == FF // P - 1)
                    last.then_inc(w_used, 1)

                turn_x(0)
                for e in range(E):
                    pe.wait_ge(xplaced, 2 * (e + 1))
                    for f in range(FG):
                        up_group(e, f)
                        if f:
                            turn_h(e, f - 1)
                    down(e, 0)
                    turn_h(e, FG - 1)
                    down(e, 1)
                    if e + 1 < E:
                        turn_x(e + 1)
                    down(e, 2)
                    down(e, 3)

            def half_piece(u, s):
                c = slice(s * KD * BANK // 2, (s + 1) * KD * BANK // 2)
                return raw[u % RW][:, c], w[u % RP].high[:, c], w[u % RP].low[:, c]

            @block.scalar
            def _(act):
                def split_high(u):
                    if u >= E * UNITS:
                        return
                    act.wait_ge(core.load[u % RW].sem, core.load[u % RW].at(u // RW + 1))
                    if u >= RP:
                        act.wait_ge(w_used, u - RP + 1)
                    for s in range(2):
                        x, hi, _ = half_piece(u, s)
                        nc.scalar.activation(hi, x, ACT.Copy).then_inc(high, 1)

                def modulate(e):
                    if e:
                        act.wait_ge(xplaced, 2 * e)
                    for half in range(2):
                        act.wait_ge(xturn, 2 * e + half + 1)
                        for k in range(4 * half, 4 * half + 4):
                            last = nc.scalar.activation(xw[:, k, :], bank[4 + half][:, (k % 4) * P:(k % 4 + 1) * P],
                                                        ACT.Identity, bias=sh[:, k:k + 1], scale=sc[:, k:k + 1])
                        last.then_inc(xwhole, 1)

                def place_h(n):
                    act.wait_ge(hturn, n + 1)
                    f = n % FG
                    nc.scalar.activation(hidT.high[:, 4 * f:4 * f + 4, :],
                                         bank[4 + n % 2][:, :].rearrange("p (k t) -> p k t", t=P),
                                         ACT.Copy).then_inc(hhigh, 1)

                split_high(0)
                modulate(0)
                split_high(1)
                for e in range(E):
                    for i in range(UNITS):
                        split_high(e * UNITS + i + 2)
                        if i < 2 * FG and i % 2:
                            n = e * FG + i // 2
                            act.wait_ge(w_used, e * UNITS + i + 1)
                            if n >= 2:
                                act.wait_ge(hidden, n - 1)
                            nc.scalar.activation(sa[n % 2][:, :], bank[2 * (n % 2)][:, :], ACT.Silu).then_inc(silu, 1)
                            if i > 1:
                                place_h(n - 1)
                        if i == 2 * FG:
                            place_h(e * FG + FG - 1)
                        if i == 2 * FG + 1 and e + 1 < E:
                            modulate(e + 1)

            @block.vector
            def _(dve):
                def split_low(u):
                    if u >= E * UNITS:
                        return
                    for s in range(2):
                        dve.wait_ge(high, 2 * u + s + 1)
                        x, hi, lo = half_piece(u, s)
                        nc.vector.tensor_tensor(lo, x, hi.bitcast(F32), ALU.subtract).then_inc(low, 1)

                def place_h(n):
                    dve.wait_ge(hhigh, n + 1)
                    f = n % FG
                    nc.vector.tensor_tensor(hidT.low[:, 4 * f:4 * f + 4, :],
                                            bank[4 + n % 2][:, :].rearrange("p (k t) -> p k t", t=P),
                                            hidT.high[:, 4 * f:4 * f + 4, :].bitcast(F32), ALU.subtract).then_inc(hplaced, 1)

                def result(e):
                    dve.wait_ge(w_used, (e + 1) * UNITS)
                    if e >= 2:
                        dve.wait_ge(scattered, 16 * (e - 1))
                    for half in range(2):
                        c = slice(half * BANK, (half + 1) * BANK)
                        nc.vector.scalar_tensor_tensor(yo[e % 2][:, c], bank[6 + half][:, :], core.moe_gate[:, e:e + 1],
                                                       g2[:, c], ALU.mult, ALU.mult).then_inc(yout, 1)

                split_low(0)
                split_low(1)
                dve.wait_ge(gain, 16)
                for e in range(E):
                    for i in range(UNITS):
                        split_low(e * UNITS + i + 2)
                        if i == 0 and e:
                            result(e - 1)
                        if i < 2 * FG and i % 2:
                            n = e * FG + i // 2
                            dve.wait_ge(silu, n + 1)
                            if n >= 2:
                                dve.wait_ge(hturn, n - 1)
                            nc.vector.tensor_tensor(hid[n % 2][:, :], sa[n % 2][:, :], bank[2 * (n % 2) + 1][:, :],
                                                    ALU.mult).then_inc(hidden, 1)
                            if i > 1:
                                place_h(n - 1)
                        if i == 2 * FG:
                            place_h(e * FG + FG - 1)
                result(E - 1)
        for j in range(RW):
            core.load[j].close(len(range(j, E * UNITS, RW)))


def stage_final_norm(core, name="final"):
    nc, io = core.nc, core.io
    RX = 3
    with Stage(core, name) as st:
        x = [st.sb(f"x{i}", [P, D]) for i in range(RX)]
        y = [st.sb(f"y{i}", [P, D]) for i in range(RX)]
        junk, gain = st.sb("junk", [P, D]), st.sb("gain", [P, D])
        ss, rms = st.sb("ss", [P, NT]), st.sb("rms", [P, NT])
        gains, rooted, done = st.sem("gains"), st.sem("rooted"), st.sem("done")
        with st.block() as block:
            @block.sync
            def _(sp):
                sp.dma_start(gain[:, :], io["final_g"].partition_broadcast(P)).then_inc(gains, 16)
                for t in range(NT):
                    if t >= RX:
                        sp.wait_ge(done, t - RX + 1)
                    sp.dma_start(x[t % RX][:, :], core.x1[t * P:(t + 1) * P, :]).then_inc(core.load[t % RX].sem, 16)

            @block.scalar
            def _(act):
                for t in range(NT):
                    act.wait_ge(core.load[t % RX].sem, core.load[t % RX].at(t // RX + 1))
                    core.act(act, nc.scalar.activation(junk[:, :], x[t % RX][:, :], ACT.Square, accum_out=ss[:, t:t + 1]))
                    nc.scalar.activation(rms[:, t:t + 1], ss[:, t:t + 1], ACT.Sqrt, bias=core.eps[:, 0:1],
                                         scale=1.0 / D).then_inc(rooted, 1)

            @block.vector
            def _(dve):
                dve.wait_ge(gains, 16)
                for t in range(NT):
                    dve.wait_ge(rooted, t + 1)
                    core.dve(dve, nc.vector.reciprocal(rms[:, t:t + 1], rms[:, t:t + 1]))
                    if t >= RX:
                        dve.wait_ge(core.store[t % RX].sem, core.store[t % RX].at(t // RX))
                    nc.vector.scalar_tensor_tensor(y[t % RX][:, :], x[t % RX][:, :], rms[:, t:t + 1], gain[:, :],
                                                   ALU.mult, ALU.mult).then_inc(done, 1)

            @block.gpsimd
            def _(pool):
                for t in range(NT):
                    pool.wait_ge(done, t + 1)
                    pool.dma_start(core.x2[t * P:(t + 1) * P, :], y[t % RX][:, :]).then_inc(core.store[t % RX].sem, 16)
                for j in range(RX):
                    pool.wait_ge(core.store[j].sem, core.store[j].at(len(range(j, NT, RX))))
        for j in range(RX):
            core.load[j].close(len(range(j, NT, RX)))
            core.store[j].close(len(range(j, NT, RX)))


def lam_init(l):
    return 0.8 - 0.6 * math.exp(-0.3 * l)


def stage_qk(core, l, tiles_q, q_parts, k_high, k_low, neg_lam, name):
    nc, io = core.nc, core.io
    HM = 2 * HEADS2
    items = [(0, t) for t in tiles_q] + [(1, t) for t in range(NT + NC_)]
    RX = 3
    with Stage(core, name) as st:
        cos, sin = st.sb("cos", [P, NT, QK]), st.sb("sin", [P, NT, QK])
        g = st.sb("g", [P, 2, QK])
        cosg = [st.sb(f"cosg{i}", [P, NT, QK]) for i in range(2)]
        sing = [st.sb(f"sing{i}", [P, NT, QK]) for i in range(2)]
        lv, lp, ls = st.sb("lv", [P, 4, QK]), st.sb("lp", [P, 2, QK]), st.sb("ls", [P, 2])
        x = [st.sb(f"x{i}", [P, HM, QK]) for i in range(RX)]
        sq = [st.sb(f"sq{i}", [P, HM, QK]) for i in range(2)]
        rms = st.sb("rms", [P, len(items), HM])
        y1 = [st.sb(f"ya{i}", [P, HM, QK]) for i in range(2)]
        y2 = [st.sb(f"yb{i}", [P, HM, QK]) for i in range(2)]
        y = [st.sb(f"y{i}", [P, HM, QK]) for i in range(2)]
        stacked = [st.sb(f"stacked{i}", [P, HM, 2, QK], F32R) for i in range(2)]
        low = [st.sb(f"low{i}", [P, HM, QK], F32R) for i in range(2)]
        bank = st.banks(6)
        inputs, squared, summed, rooted, high, split, ready, turned, placed, lsum, lexp = (st.sem(k) for k in (
            "inputs", "squared", "summed", "rooted", "high", "split", "ready", "turned", "placed", "lsum", "lexp"))
        n_q = len(tiles_q)
        with st.block() as block:
            @block.sync
            def _(sp):
                sp.dma_start(cos[:, :, :], io["t_rope_cos"].rearrange("(t p) d -> p t d", p=P)).then_inc(inputs, 16)
                sp.dma_start(sin[:, :, :], io["t_rope_sin"].rearrange("(t p) d -> p t d", p=P)).then_inc(inputs, 16)
                sp.dma_start(g[:, :, :], io["qk_norm_g_2"][l].partition_broadcast(P)).then_inc(inputs, 16)
                sp.dma_start(lv[:, :, :], io["lam_vecs_2"][l].partition_broadcast(P)).then_inc(inputs, 16)
                for i, (which, t) in enumerate(items):
                    if i >= RX:
                        sp.wait_ge(ready, i - RX + 1)
                    sp.dma_start(x[i % RX][:, :, :], core.qk_tok[which, t * P:(t + 1) * P, :].rearrange(
                        "p (h d) -> p h d", d=QK)).then_inc(core.load[i % RX].sem, 16)

            @block.scalar
            def _(act):
                def measure(i):
                    act.wait_ge(core.load[i % RX].sem, core.load[i % RX].at(i // RX + 1))
                    if i >= 2:
                        act.wait_ge(summed, i - 1)
                    nc.scalar.activation(sq[i % 2][:, :, :], x[i % RX][:, :, :], ACT.Square).then_inc(squared, 1)

                def key_high(i):
                    act.wait_ge(ready, i + 1)
                    if i >= 2:
                        act.wait_ge(turned, i - 1)
                    nc.scalar.activation(stacked[i % 2][:, :, :, :],
                                         y[i % 2][:, :, :].unsqueeze(2).to_broadcast([P, HM, 2, QK]), ACT.Copy).then_inc(high, 1)

                def place(i):
                    which, t = items[i]
                    c = slice(t * P, (t + 1) * P)
                    act.wait_ge(turned, i + 1)
                    dst = k_high if which else q_parts
                    out = [dst[:, 0:4, c], dst[:, 4:8, c]] + ([k_low[:, :, c]] if which else [])
                    for j, o in enumerate(out):
                        last = nc.scalar.activation(o, bank[3 * (i % 2) + j][:, :].rearrange("p (h t) -> p h t", t=P), ACT.Copy)
                    last.then_inc(placed, 1)

                act.wait_ge(lsum, 1)
                nc.scalar.activation(ls[:, :], ls[:, :], ACT.Exp).then_inc(lexp, 1)
                measure(0)
                for i in range(len(items) + 2):
                    if i + 1 < len(items):
                        measure(i + 1)
                    if i < len(items):
                        act.wait_ge(summed, i + 1)
                        nc.scalar.activation(rms[:, i, :], rms[:, i, :], ACT.Sqrt, bias=core.eps[:, 0:1],
                                             scale=1.0 / QK).then_inc(rooted, 1)
                    if n_q <= i - 1 < len(items):
                        key_high(i - 1)
                    if i >= 2:
                        place(i - 2)

            @block.gpsimd
            def _(pool):
                for i, (which, t) in enumerate(items):
                    pool.wait_ge(ready, i + 1)
                    if i >= 2:
                        pool.wait_ge(turned, i - 1)
                    if which:
                        pool.wait_ge(high, i - n_q + 1)
                        nc.gpsimd.tensor_tensor(low[i % 2][:, :, :], y[i % 2][:, :, :],
                                                stacked[i % 2][:, :, 0, :].bitcast(F32), ALU.subtract).then_inc(split, 1)
                        continue
                    yy = y[i % 2][:, :, :].rearrange("p (h m) d -> p h m d", m=2)
                    ss_ = stacked[i % 2][:, :, :, :].rearrange("p (h m) s d -> p h m s d", m=2)
                    for m in range(2):
                        core.pool(pool, nc.gpsimd.tensor_copy(ss_[:, :, m, m, :], yy[:, :, m, :]))
                    for m in range(2):
                        last = nc.gpsimd.tensor_tensor(ss_[:, :, m, 1 - m, :], yy[:, :, m, :],
                                                       ss_[:, :, m, m, :].bitcast(F32), ALU.subtract)
                    last.then_inc(split, 1)

            @block.tensor
            def _(pe):
                for i, (which, t) in enumerate(items):
                    pe.wait_ge(split, i + 1)
                    if i >= 2:
                        pe.wait_ge(placed, i - 1)
                    for h in range(HM):
                        src = stacked[i % 2][:, h, :, :].rearrange("p s d -> p (s d)").bitcast(F32)
                        last = nc.tensor.transpose(bank[3 * (i % 2) + h // 4][:, (h % 4) * P:(h % 4 + 1) * P], src,
                                                   core.ident[:, :])
                    for h in range(HEADS2 if which else 0):
                        src = low[i % 2][:, 2 * h:2 * h + 2, :].rearrange("p m d -> p (m d)").bitcast(F32)
                        last = nc.tensor.transpose(bank[3 * (i % 2) + 2][:, h * P:(h + 1) * P], src, core.ident[:, :])
                    last.then_inc(turned, 1)

            @block.vector
            def _(dve):
                step = lambda ins: core.dve(dve, ins)
                dve.wait_ge(inputs, 64)
                lvv = lv[:, :, :].rearrange("p (a b) d -> p a b d", b=2)
                step(nc.vector.tensor_tensor(lp[:, :, :], lvv[:, :, 0, :], lvv[:, :, 1, :], ALU.mult))
                nc.vector.tensor_reduce(ls[:, :], lp[:, :, :], AX, ALU.add).then_inc(lsum, 1)
                dve.wait_ge(lexp, 1)
                step(nc.vector.tensor_tensor(neg_lam[:, :], ls[:, 1:2], ls[:, 0:1], ALU.subtract))
                step(nc.vector.tensor_scalar(neg_lam[:, :], neg_lam[:, :], lam_init(l), None, ALU.subtract))
                for w in range(2):
                    gr = g[:, w, :].rearrange("p (a s c) -> p a s c", a=2, s=2)
                    step(nc.vector.tensor_tensor(cosg[w][:, :, :], cos[:, :, :],
                                                 g[:, w:w + 1, :].to_broadcast([P, NT, QK]), ALU.mult))
                    s_in = sin[:, :, :].rearrange("p t (a s c) -> p t a s c", a=2, s=2)
                    s_out = sing[w][:, :, :].rearrange("p t (a s c) -> p t a s c", a=2, s=2)
                    for a in range(2):
                        for s in range(2):
                            step(nc.vector.tensor_tensor(s_out[:, :, a, s, :], s_in[:, :, a, s, :],
                                                         gr[:, a, 1 - s, :].unsqueeze(1).to_broadcast([P, NT, 16]), ALU.mult))
                for i, (w, t) in enumerate(items):
                    xx = x[i % RX]
                    dve.wait_ge(squared, i + 1)
                    nc.vector.tensor_reduce(rms[:, i, :], sq[i % 2][:, :, :], AX, ALU.add).then_inc(summed, 1)
                    dve.wait_ge(rooted, i + 1)
                    step(nc.vector.reciprocal(rms[:, i, :], rms[:, i, :]))
                    step(nc.vector.tensor_tensor(xx[:, :, :], xx[:, :, :],
                                                 rms[:, i, :].unsqueeze(2).to_broadcast([P, HM, QK]), ALU.mult))
                    if i >= 2:
                        dve.wait_ge(split, i - 1)
                    if t < NT:
                        step(nc.vector.tensor_tensor(y1[i % 2][:, :, :], xx[:, :, :],
                                                     cosg[w][:, t:t + 1, :].to_broadcast([P, HM, QK]), ALU.mult))
                        xs = xx[:, :, :].rearrange("p h (a s c) -> p h a s c", a=2, s=2)
                        ys = y2[i % 2][:, :, :].rearrange("p h (a s c) -> p h a s c", a=2, s=2)
                        sg = sing[w][:, t, :].rearrange("p (a s c) -> p a s c", a=2, s=2)
                        for s in range(2):
                            step(nc.vector.tensor_tensor(ys[:, :, :, s, :], xs[:, :, :, 1 - s, :],
                                                         sg[:, :, s, :].unsqueeze(1).to_broadcast([P, HM, 2, 16]), ALU.mult))
                        nc.vector.tensor_tensor(y[i % 2][:, :, :], y1[i % 2][:, :, :], y2[i % 2][:, :, :],
                                                ALU.add).then_inc(ready, 1)
                    else:
                        nc.vector.tensor_tensor(y[i % 2][:, :, :], xx[:, :, :],
                                                g[:, w:w + 1, :].to_broadcast([P, HM, QK]), ALU.mult).then_inc(ready, 1)

        for j in range(RX):
            core.load[j].close(len(range(j, len(items), RX)))


def stage_attend(core, l, tiles_q, q_parts, k_high, k_low, neg_lam, y_att, name):
    nc, io = core.nc, core.io
    TL = NT + NC_
    SCALE = float(QK) ** -0.5
    items = [(h, t, 0 if t < NT else NT, TL) for h in range(HEADS2) for t in tiles_q]
    N = len(items)
    LAG = 2
    groups = []
    for h in range(HEADS2):
        for t in range(0, len(tiles_q), 4):
            groups.append((h, h * len(tiles_q) + t, min(4, len(tiles_q) - t)))
    group_of = {i: g for g, (_, i0, n) in enumerate(groups) for i in range(i0, i0 + n)}
    last_group = {h: g for g, (h, _, _) in enumerate(groups)}

    def due(i):
        for g, (h, i0, n) in enumerate(groups):
            spread = groups[g + 1][2] if g + 1 < len(groups) else 2
            r = i - (i0 + n + LAG)
            if 0 <= r < spread:
                b = blocks(i0)
                yield g, b * r // spread, b * (r + 1) // spread

    def blocks(i):
        return items[i][3] - items[i][2]

    gof, total = [], 0
    for i in range(N):
        gof.append(total)
        total += -(-blocks(i) // 4)
    gof.append(total)
    steps = N + LAG + 2 + 1
    with Stage(core, name) as st:
        v = [st.sb(f"v{i}", [P, TL, P]) for i in range(2)]
        p = [[st.sb(f"p{m}{i}", [P, TOK]) for m in range(2)] for i in range(LAG + 1)]
        pT = [st.sb(f"pT{i}", [P, TL, BANK]) for i in range(2)]
        mx, nb = st.sb("mx", [P, N, 3]), st.sb("nb", [P, N, 2])
        sums, rinv = st.sb("sums", [P, N, 2]), st.sb("rinv", [P, N, 2])
        scores = st.stack.enter_context(nc.psum_tensor(f"{name}_scores", [P, 5 * BANK], F32))
        bank = st.banks(3)
        shared, scored, bounded, exped, inverted, scaled, mixed, turned, placed, odone, ocopied = (st.sem(k) for k in (
            "shared", "scored", "bounded", "exped", "inverted", "scaled", "mixed", "turned", "placed", "o", "o_copied"))
        FIRST, SHARED, SECOND = [(0, 512), (512, 512)], [(0, 1024, 256), (1, 0, 256)], [(256, 512), (768, 512)]

        with st.block() as block:
            @block.sync
            def _(sp):
                for h in range(HEADS2):
                    if h >= 2:
                        sp.wait_ge(odone, last_group[h - 2] + 1)
                    sp.dma_start(v[h % 2][:, :, :], core.v_tok[:, h * P:(h + 1) * P].rearrange("(t p) c -> p t c", p=P)
                                 ).then_inc(core.load[h % 2].sem, 16)

            @block.tensor
            def _(pe):
                def score(i, m, c, n):
                    h, t, k0, k1 = items[i]
                    if c >= (k1 - k0) * P:
                        return None
                    n = min(n, (k1 - k0) * P - c)
                    hm, tok, key = 2 * h + m, slice(t * P, (t + 1) * P), slice(k0 * P + c, k0 * P + c + n)
                    rows = slice(m * QK, (m + 1) * QK)
                    out = scores[:, m * TOK + c:m * TOK + c + n]
                    nc.tensor.matmul(out, q_parts[:, hm, tok], k_high[:, hm, key], start=True, stop=False)
                    if m and c == 0:
                        pe.wait_ge(shared, i + 1)
                    return nc.tensor.matmul(out, q_parts[rows, hm, tok], k_low[rows, h, key], start=False, stop=True)

                def scores_of(i):
                    if i:
                        pe.wait_ge(exped, 2 * i - 1)
                    for c, n in FIRST:
                        last = score(i, 0, c, n) or last
                    if i:
                        pe.wait_ge(exped, 2 * i)
                    last = score(i, *SHARED[0]) or last
                    last.then_inc(shared, 1)
                    score(i, *SHARED[1]).then_inc(scored, 1)
                    last = None
                    for c, n in SECOND:
                        last = score(i, 1, c, n) or last
                    if last is None:
                        pe.wait_ge(scored, 2 * i + 1)
                        pe.sem_inc(scored, 1)
                    else:
                        last.then_inc(scored, 1)

                def turn(i):
                    pe.wait_ge(mixed, i + 1)
                    for gi in range(gof[i], gof[i + 1]):
                        b0 = 4 * (gi - gof[i])
                        if gi >= 2:
                            pe.wait_ge(placed, gi - 1)
                        for b in range(min(4, blocks(i) - b0)):
                            last = nc.tensor.transpose(bank[gi % 2][:, b * P:(b + 1) * P],
                                                       p[i % (LAG + 1)][0][:, (b0 + b) * P:(b0 + b + 1) * P],
                                                       core.ident[:, :])
                        last.then_inc(turned, 1)

                def values(g, b0, b1):
                    h, i0, n = groups[g]
                    k0 = items[i0][2]
                    if b0 == 0:
                        pe.wait_ge(placed, gof[i0 + n])
                        pe.wait_ge(core.load[h % 2].sem, core.load[h % 2].at(h // 2 + 1))
                        if g:
                            pe.wait_ge(ocopied, g)
                    for b in range(b0, b1):
                        last = nc.tensor.matmul(bank[2][:, 0:n * P], v[h % 2][:, k0 + b, :], pT[g % 2][:, b, 0:n * P],
                                                start=(b == 0), stop=(b == blocks(i0) - 1))
                    if b1 == blocks(i0):
                        last.then_inc(odone, 1)

                for i in range(steps):
                    if i < N:
                        scores_of(i)
                    if LAG <= i < N + LAG:
                        turn(i - LAG)
                    for g, b0, b1 in due(i):
                        values(g, b0, b1)

            @block.scalar
            def _(act):
                def exps(i, m):
                    n = blocks(i) * P
                    act.wait_ge(bounded, 2 * i + (m + 1 if blocks(i) * P > SHARED[1][2] else 2))
                    if i > LAG:
                        act.wait_ge(turned, gof[i - LAG])
                    nc.scalar.activation(p[i % (LAG + 1)][m][:, 0:n], scores[:, m * TOK:m * TOK + n], ACT.Exp,
                                         bias=nb[:, i, m:m + 1], scale=SCALE, accum_out=sums[:, i, m:m + 1]).then_inc(exped, 1)

                def place(i):
                    g = group_of[i]
                    col = (i - groups[g][1]) * P
                    if g >= 2:
                        act.wait_ge(odone, g - 1)
                    for gi in range(gof[i], gof[i + 1]):
                        b0 = 4 * (gi - gof[i])
                        nb_ = min(4, blocks(i) - b0)
                        act.wait_ge(turned, gi + 1)
                        nc.scalar.activation(pT[g % 2][:, b0:b0 + nb_, col:col + P],
                                             bank[gi % 2][:, 0:nb_ * P].rearrange("p (b t) -> p b t", t=P),
                                             ACT.Copy).then_inc(placed, 1)

                for i in range(N + LAG):
                    if i >= LAG:
                        place(i - LAG)
                    if i < N:
                        exps(i, 0)
                        exps(i, 1)

            @block.gpsimd
            def _(pool):
                for i in range(N):
                    n = blocks(i) * P
                    pool.wait_ge(inverted, i + 1)
                    b = p[i % (LAG + 1)][1][:, 0:n]
                    nc.gpsimd.tensor_scalar(b, b, rinv[:, i, 1:2], neg_lam[:, :], ALU.mult, ALU.mult).then_inc(scaled, 1)

            @block.vector
            def _(dve):
                step = lambda ins: core.dve(dve, ins)

                def bound(i):
                    n, part = blocks(i) * P, SHARED[1][2]
                    dve.wait_ge(scored, 2 * i + 1)
                    step(nc.vector.tensor_reduce(mx[:, i, 0:1], scores[:, 0:n], AX, ALU.max))
                    step(nc.vector.tensor_reduce(mx[:, i, 1:2], scores[:, TOK:TOK + part], AX, ALU.max))
                    nc.vector.tensor_scalar(nb[:, i, 0:1], mx[:, i, 0:1], -SCALE, None, ALU.mult).then_inc(bounded, 1)
                    dve.wait_ge(scored, 2 * i + 2)
                    rest = part if n > part else 0
                    step(nc.vector.tensor_reduce(mx[:, i, 2:3], scores[:, TOK + rest:TOK + n], AX, ALU.max))
                    nc.vector.tensor_scalar(nb[:, i, 1:2], mx[:, i, 2:3], mx[:, i, 1:2], -SCALE,
                                            ALU.max, ALU.mult).then_inc(bounded, 1)

                def mix(i):
                    n = blocks(i) * P
                    dve.wait_ge(scaled, i + 1)
                    a, b = p[i % (LAG + 1)]
                    nc.vector.scalar_tensor_tensor(a[:, 0:n], a[:, 0:n], rinv[:, i, 0:1], b[:, 0:n],
                                                   ALU.mult, ALU.add).then_inc(mixed, 1)

                for i in range(steps):
                    for g, _, b1 in due(i - 1):
                        h, i0, n = groups[g]
                        if b1 == blocks(i0):
                            t0 = items[i0][1]
                            dve.wait_ge(odone, g + 1)
                            nc.vector.tensor_copy(y_att[:, h, t0 * P:(t0 + n) * P], bank[2][:, 0:n * P]).then_inc(ocopied, 1)
                    if i < N:
                        bound(i)
                    if i and i <= N:
                        mix(i - 1)
                    if i < N:
                        dve.wait_ge(exped, 2 * i + 2)
                        nc.vector.reciprocal(rinv[:, i, :], sums[:, i, :]).then_inc(inverted, 1)
        for j in range(2):
            core.load[j].close(HEADS2 // 2)


def stage_mix2(core, l, segs, y_att, y_mix, name):
    nc, io = core.nc, core.io
    TL = sum(n for _, n in segs)
    W = TL * P
    PADL, PADR = 16, 8
    with Stage(core, name) as st:
        a = st.sb("a", [P, TL, 256])
        tab = st.sb("tab", [P, NT, SEQ])
        tabc = [st.sb(f"tabc{i}", [P, NC_, CTX]) for i in range(2)]
        F = [[st.sb(f"f{cs}{c}", [P, W]) for c in range(2)] for cs in range(2)]
        dft = [st.sb("dcos", [P, P]), st.sb("dsin", [P, P])]
        wf, wp = st.sb("wf", [P, 2, P]), st.sb("wp", [P, 2, P])
        M = [st.sb("m_cos", [P, 2, P]), st.sb("m_sin", [P, 2, P])]
        gate = [st.sb(f"gate{i}", [P, W]) for i in range(3)]
        u = [st.sb(f"u{j}", [P, PADL + SEQ + PADR]) for j in range(2)]
        s1, s2 = st.sb("s1", [P, PADL + SEQ + PADR]), st.sb("s2", [P, PADL + SEQ + PADR])
        icnt, icntc = st.sb("icnt", [P, 2, SEQ]), st.sb("icntc", [P, 2, CTX])
        pooled = [st.sb(f"pooled{j}", [P, W]) for j in range(2)]
        square = [st.sb(f"square{i}", [P, BANK]) for i in range(2)]
        rms = [st.sb(f"rms{i}", [P, BANK]) for i in range(2)]
        ones = st.sb("ones", [P, P])
        gsub = st.sb("gsub", [P, 1])
        bank = st.banks(8)
        loaded_u = st.dma_sem("loaded_u")
        (small, zeroed, cosines, sines, ctx_tables, mdone, mcopied, fdone, fcopied, pool_done, normed,
         silu, rooted, squared, summed, product, placed) = (st.sem(k) for k in (
             "small", "zeroed", "cosines", "sines", "ctx_tables", "m", "m_copied", "f", "f_copied", "pooled",
             "normed", "silu", "rooted", "squared", "summed", "product", "placed"))
        fjobs = []
        for cs in range(2):
            for c in range(2):
                for t0, nt in segs:
                    for col in range(0, nt * P, BANK):
                        fjobs.append((cs, c, t0, nt, col, min(BANK, nt * P - col)))
        first_sine = len(fjobs) // 2
        cols = [(c, min(BANK, W - c)) for c in range(0, W, BANK)]
        pjobs = [(kind, c, c0, n) for kind in range(2) for c in range(2) for c0, n in cols]
        NPJ = len(pjobs)
        seg_u = [(j, t0, nt) for t0, nt in segs for j in range(2)]
        with st.block() as block:
            @block.sync
            def _(sp):
                sp.wait_ge(zeroed, 5)
                for g in range(4):
                    r = slice((g % 2) * 64, (g % 2) * 64 + 64)
                    sp.dma_start(wf[r, g // 2, r], io["w_fourier_2"][l][g]).then_inc(small, 16)
                    sp.dma_start(wp[r, g // 2, r], io["w_pool_2"][l][g]).then_inc(small, 16)
                sp.dma_start(dft[0][:, :], io["t_dim_cos"]).then_inc(small, 16)
                sp.dma_start(dft[1][:, :], io["t_dim_sin"]).then_inc(small, 16)
                sp.dma_start(a[:, :, :], core.a_tok[0:W, :].rearrange("(t p) c -> p t c", p=P)).then_inc(small, 16)
                sp.dma_start(icnt[:, :, :], io["t_inv_count"].rearrange("p (j t) -> p j t", j=2)).then_inc(small, 16)
                sp.dma_start(icntc[:, :, :], io["t_inv_count_ctx"].rearrange("p (j t) -> p j t", j=2)).then_inc(small, 16)
                sp.dma_start(tab[:, :, :], io["t_tok_cos"].rearrange("(t p) k -> p t k", p=P)).then_inc(cosines, 16)
                for i in range(2):
                    sp.dma_start(tabc[i][:, :, :], io["t_ctx_cos" if i == 0 else "t_ctx_sin"].rearrange(
                        "(t p) k -> p t k", p=P)).then_inc(ctx_tables, 16)
                for k in range(3):
                    sp.dma_start(gate[k][:, :], core.gate_t[k * P:(k + 1) * P, 0:W]).then_inc(core.load[k].sem, 16)
                sp.wait_ge(fdone, first_sine)
                sp.dma_start(tab[:, :, :], io["t_tok_sin"].rearrange("(t p) k -> p t k", p=P)).then_inc(sines, 16)
                for k in range(3, KD):
                    sp.wait_ge(placed, (k - 2) * len(cols) if k - 3 < 4 else NPJ + (k - 3 - 4 + 1))
                    sp.dma_start(gate[k % 3][:, :], core.gate_t[k * P:(k + 1) * P, 0:W]).then_inc(core.load[k % 3].sem, 16)

            @block.gpsimd
            def _(pool):
                for tile in (wf, wp):
                    nc.gpsimd.memset(tile[:, :, :], 0.0).then_inc(zeroed, 1)
                for tile in u:
                    nc.gpsimd.memset(tile[:, :], 0.0).then_inc(zeroed, 1)
                nc.gpsimd.memset(ones[:, :], 1.0).then_inc(zeroed, 1)
                for i, (j, t0, nt) in enumerate(seg_u):
                    if i >= 2:
                        pool.wait_ge(pool_done, i - 1)
                        pool.wait_ge(zeroed, 5)
                        nc.gpsimd.memset(u[j][:, PADL:], 0.0).then_inc(zeroed, 1)
                        pool.wait_ge(zeroed, 5 + i - 1)
                    else:
                        pool.wait_ge(zeroed, 5)
                    pool.dma_start(u[j][:, PADL:PADL + nt * P], core.b_t[j * P:(j + 1) * P, t0 * P:(t0 + nt) * P]
                                   ).then_inc(loaded_u, 16)
                    pool.wait_ge(loaded_u, 16 * (i + 1))

            @block.tensor
            def _(pe):
                pe.wait_ge(small, 16 * 13)
                for cs in range(2):
                    for c in range(2):
                        last = nc.tensor.matmul(bank[0][:, (2 * cs + c) * P:(2 * cs + c + 1) * P], dft[cs][:, :],
                                                wf[:, c, :], start=True, stop=True)
                last.then_inc(mdone, 1)
                pe.wait_ge(cosines, 16)
                pe.wait_ge(ctx_tables, 32)
                for i, (cs, c, t0, nt, col, n) in enumerate(fjobs):
                    if i >= 3:
                        pe.wait_ge(fcopied, i - 2)
                    if i == first_sine:
                        pe.wait_ge(sines, 16)
                    for t in range(nt):
                        rhs = tab[:, t, col:col + n] if t0 == 0 else tabc[cs][:, t, col:col + n]
                        last = nc.tensor.matmul(bank[1 + i % 3][:, 0:n], a[:, t0 + t, c * P:(c + 1) * P], rhs,
                                                start=(t == 0), stop=(t == nt - 1))
                    last.then_inc(fdone, 1)
                pe.wait_ge(fcopied, len(fjobs))
                pe.wait_ge(mcopied, 1)
                pe.wait_ge(pool_done, len(seg_u))
                for i, (kind, c, c0, n) in enumerate(pjobs):
                    if i >= 2:
                        pe.wait_ge(placed, i - 1)
                    if kind == 0:
                        for cs in range(2):
                            last = nc.tensor.matmul(bank[4 + i % 2][:, 0:n], M[cs][:, c, :], F[cs][c][:, c0:c0 + n],
                                                    start=(cs == 0), stop=(cs == 1))
                    else:
                        last = nc.tensor.matmul(bank[4 + i % 2][:, 0:n], wp[:, c, :], pooled[c][:, c0:c0 + n],
                                                start=True, stop=True)
                    last.then_inc(product, 1)
                pe.wait_ge(zeroed, 5)
                for m in range(HEADS2 * len(cols)):
                    n = cols[m % len(cols)][1]
                    pe.wait_ge(squared, m + 1)
                    if m >= 2:
                        pe.wait_ge(rooted, m - 1)
                    nc.tensor.matmul(bank[6 + m % 2][:, 0:n], ones[:, :], square[m % 2][:, 0:n],
                                     start=True, stop=True).then_inc(summed, 1)

            @block.scalar
            def _(act):
                def root(m):
                    n = cols[m % len(cols)][1]
                    act.wait_ge(summed, m + 1)
                    if m >= 2:
                        act.wait_ge(normed, m - 1)
                    nc.scalar.activation(rms[m % 2][:, 0:n], bank[6 + m % 2][:, 0:n], ACT.Sqrt, bias=core.eps[:, 0:1],
                                         scale=1.0 / P).then_inc(rooted, 1)

                act.wait_ge(mdone, 1)
                mm = bank[0][:, :].rearrange("p (s c d) -> p s c d", s=2, c=2)
                core.act(act, nc.scalar.activation(M[0][:, :, :], mm[:, 0, :, :], ACT.Copy))
                nc.scalar.activation(M[1][:, :, :], mm[:, 1, :, :], ACT.Copy, scale=-1.0).then_inc(mcopied, 1)
                for i, (cs, c, t0, nt, col, n) in enumerate(fjobs):
                    act.wait_ge(fdone, i + 1)
                    nc.scalar.activation(F[cs][c][:, t0 * P + col:t0 * P + col + n], bank[1 + i % 3][:, 0:n],
                                         ACT.Copy).then_inc(fcopied, 1)
                for k in range(KD):
                    act.wait_ge(core.load[k % 3].sem, core.load[k % 3].at(k // 3 + 1))
                    nc.scalar.activation(gate[k % 3][:, :], gate[k % 3][:, :], ACT.Silu).then_inc(silu, 1)
                    if k < 4:
                        continue
                    for i, (c0, n) in enumerate(cols):
                        m = (k - 4) * len(cols) + i
                        if m >= 2:
                            act.wait_ge(summed, m - 1)
                        nc.scalar.activation(square[m % 2][:, 0:n], y_att[:, k - 4, c0:c0 + n], ACT.Square).then_inc(squared, 1)
                        if m:
                            root(m - 1)
                root(HEADS2 * len(cols) - 1)

            @block.vector
            def _(dve):
                step = lambda ins: core.dve(dve, ins)
                step(nc.vector.tensor_scalar(gsub[:, :], core.col_b[:, AT_B["subln_g_2"] + l:AT_B["subln_g_2"] + l + 1],
                                             1.0 - lam_init(l), None, ALU.mult))
                dve.wait_ge(small, 16 * 13)
                for i, (j, t0, nt) in enumerate(seg_u):
                    n = nt * P
                    dve.wait_ge(loaded_u, 16 * (i + 1))
                    full = PADL + n + PADR
                    ic = icnt if t0 == 0 else icntc

                    def double(dst, src, w):
                        step(nc.vector.tensor_tensor(dst[:, w:full], src[:, w:full], src[:, 0:full - w], ALU.add))

                    def take(rows, src, ahead):
                        o = pooled[j][rows, t0 * P:t0 * P + n]
                        step(nc.vector.tensor_tensor(o, src[rows, PADL + ahead:PADL + ahead + n], ic[rows, j, 0:n], ALU.mult))
                        return nc.vector.tensor_tensor(o, o, u[j][rows, PADL:PADL + n], ALU.subtract)

                    if i == 0:
                        step(nc.vector.memset(s1[:, 0:PADL], 0.0))
                        step(nc.vector.memset(s2[:, 0:PADL], 0.0))
                    double(s1, u[j], 1)
                    if j == 0:
                        step(take(slice(0, 64), s1, 0))
                        double(s2, s1, 2)
                        take(slice(64, 128), s2, 1).then_inc(pool_done, 1)
                    else:
                        double(s2, s1, 2)
                        double(s1, s2, 4)
                        step(take(slice(0, 64), s1, 3))
                        double(s2, s1, 8)
                        take(slice(64, 128), s2, 7).then_inc(pool_done, 1)
                    dve.wait_ge(pool_done, i + 1)
                for i, (kind, c, c0, n) in enumerate(pjobs):
                    k = 2 * kind + c
                    dve.wait_ge(product, i + 1)
                    dve.wait_ge(silu, k + 1)
                    o, y, g = bank[4 + i % 2][:, 0:n], y_mix[:, k, c0:c0 + n], gate[k % 3][:, c0:c0 + n]
                    if kind == 0:
                        nc.vector.tensor_tensor(y, o, g, ALU.mult).then_inc(placed, 1)
                    else:
                        s = AT_B["pool_scale_2"] + 2 * l + c
                        nc.vector.scalar_tensor_tensor(y, o, core.col_b[:, s:s + 1], g, ALU.mult, ALU.mult
                                                       ).then_inc(placed, 1)
                for h in range(HEADS2):
                    k = 4 + h
                    dve.wait_ge(silu, k + 1)
                    for i, (c0, n) in enumerate(cols):
                        m = h * len(cols) + i
                        dve.wait_ge(rooted, m + 1)
                        rr, y = rms[m % 2][:, 0:n], y_att[:, h, c0:c0 + n]
                        step(nc.vector.reciprocal(rr, rr))
                        step(nc.vector.scalar_tensor_tensor(rr, rr, gsub[:, :], gate[k % 3][:, c0:c0 + n],
                                                            ALU.mult, ALU.mult))
                        nc.vector.tensor_tensor(y, y, rr, ALU.mult).then_inc(normed, 1)
                    dve.wait_ge(normed, (h + 1) * len(cols))
                    dve.sem_inc(placed, 1)
        for j in range(3):
            core.load[j].close(len(range(j, KD, 3)))


def stage_out2(core, l, halves, rows, name):
    nc, io = core.nc, core.io
    n_tiles = len(rows)
    with Stage(core, name) as st:
        w = st.sb("w", [P, KD, D])
        gate = [st.sb(f"gate{v}", [P, D]) for v in range(2)]
        x = [st.sb(f"x{i}", [P, D]) for i in range(3)]
        out = [st.sb(f"out{i}", [P, D]) for i in range(3)]
        bank = st.banks(8)
        weights, product, scaled, added = (st.sem(k) for k in ("weights", "product", "scaled", "added"))
        with st.block() as block:
            @block.sync
            def _(sp):
                sp.dma_start(w[:, :, :], io["w_out_2"][l].rearrange("(k p) n -> p k n", p=P)).then_inc(weights, 16)
                for v in range(2):
                    sp.dma_start(gate[v][:, :], core.mod_rows[1 + l][v, 2 * D:3 * D].partition_broadcast(P)
                                 ).then_inc(weights, 16)
                for t, (src, _, _) in enumerate(rows):
                    if t >= 3:
                        sp.wait_ge(added, 2 * (t - 2))
                    sp.dma_start(x[t % 3][:, :], src).then_inc(core.load[t % 3].sem, 16)

            @block.tensor
            def _(pe):
                pe.wait_ge(weights, 48)
                for n in range(2 * n_tiles):
                    t, half = divmod(n, 2)
                    if n >= 8:
                        pe.wait_ge(scaled, n - 7)
                    for k in range(KD):
                        last = nc.tensor.matmul(bank[n % 8][:, :], halves[k // 4][:, k % 4, t * P:(t + 1) * P],
                                                w[:, k, half * BANK:(half + 1) * BANK], start=(k == 0), stop=(k == KD - 1))
                    last.then_inc(product, 1)

            @block.vector
            def _(dve):
                dve.wait_ge(weights, 48)
                for n in range(2 * n_tiles):
                    t, half = divmod(n, 2)
                    c = slice(half * BANK, (half + 1) * BANK)
                    dve.wait_ge(product, n + 1)
                    dve.wait_ge(core.load[t % 3].sem, core.load[t % 3].at(t // 3 + 1))
                    if t >= 3:
                        dve.wait_ge(core.store[t % 3].sem, core.store[t % 3].at(t // 3))
                    nc.vector.tensor_tensor(out[t % 3][:, c], bank[n % 8][:, :], gate[rows[t][2]][:, c],
                                            ALU.mult).then_inc(scaled, 1)
                    dve.wait_ge(scaled, n + 1)
                    nc.vector.tensor_tensor(out[t % 3][:, c], out[t % 3][:, c], x[t % 3][:, c], ALU.add).then_inc(added, 1)

            @block.gpsimd
            def _(pool):
                for t, (_, dst, _) in enumerate(rows):
                    pool.wait_ge(added, 2 * t + 2)
                    pool.dma_start(dst, out[t % 3][:, :]).then_inc(core.store[t % 3].sem, 16)
                for j in range(3):
                    pool.wait_ge(core.store[j].sem, core.store[j].at(len(range(j, n_tiles, 3))))
        for j in range(3):
            core.load[j].close(len(range(j, n_tiles, 3)))
            core.store[j].close(len(range(j, n_tiles, 3)))


def build_program(nc, io, out, tap=None, upto=99):
    core = Core(nc, io, tap)
    with core.stack:
        core.ident = core.keep("ident", [P, P])
        core.col_a, core.col_b = core.keep("col_a", [P, N_A]), core.keep("col_b", [P, N_B])
        core.col_c = core.keep("col_c", [HFF, 4])
        core.lb = core.keep("lb", [P, 2, 8])
        core.mod1 = core.keep("mod1", [P, 48, 2])
        core.mod2 = [core.keep(f"mod2_{l}", [P, 24, 2]) for l in range(2)]
        core.sc = [core.keep(f"sc{i}", [P, 8]) for i in range(7)]
        core.eps = core.keep("eps", [P, 1])
        core.hy_rms, core.hy_rstd = core.keep("hy_rms", [P, NT]), core.keep("hy_rstd", [P, NT])
        core.moe_idx, core.moe_gate = core.keep("moe_idx", [P, E], U32), core.keep("moe_gate", [P, E])
        core.mod_rows = [core.dram("mod_rows1", [2, 48 * P]), core.dram("mod_rows2", [2, 24 * P]),
                         core.dram("mod_rows3", [2, 24 * P])]
        for name, f in STAGES[:upto]:
            f(core, out)


def run_mods(core, out):
    stage_mods(core)


def run_first_projection(core, out):
    io = core.io
    core.proj_t = core.dram("proj_t", [24 * P, TOK])
    core.vg = core.dram("vg", [TOK, 2 * BANK])
    with Stage(core, "h1") as st:
        hT = Parts(st, "hT", [P, KD, TOK])
        m = core.mod1
        stage_norm(core, "norm1", [(io["x"][0], core.sc[0], m[:, 0:8, 0]), (io["ctx"][0], core.sc[1], m[:, 0:8, 1])], hT)
        groups = []
        for src, dst, ctx in ((0, 0, False), (1, 1, False), (2, 2, False), (3, 3, False), (5, 4, True), (6, 5, True)):
            js = []
            for s in range(4):
                row = (dst * 4 + s) * P
                for t0, n in ((0, 512), (512, 512)) + (((SEQ, CTX),) if ctx else ()):
                    js.append(("ch", s, t0, n, core.proj_t[row:row + P, t0:t0 + n]))
            groups.append((io["w_in"][0][:, src * BANK:(src + 1) * BANK], js))
        for src, dst, tiles in ((4, 0, NT + NC_), (7, 1, NT)):
            groups.append((io["w_in"][0][:, src * BANK:(src + 1) * BANK],
                           [("tok", t, 0, BANK, core.vg[t * P:(t + 1) * P, dst * BANK:(dst + 1) * BANK])
                            for t in range(tiles)]))
        stage_project(core, "proj1", hT, groups)


def run_filter(core, out):
    core.spectra = core.dram("spectra", [2, 2, SEQ, HY])
    stage_filter(core)


def run_hyena(core, out):
    core.mix_t = core.dram("mix_t", [D, SEQ])
    stage_hyena(core)


def run_hgrn(core, out):
    core.hg_o = core.dram("hg_o", [SEQ, HG_HEADS * P])
    stage_hgrn(core)


def run_mix_out(core, out):
    core.x1 = core.dram("x1", [SEQ, D])
    stage_mix_out(core)


def run_router(core, out):
    core.xn2 = core.dram("xn2", [SEQ, D])
    with Stage(core, "h2") as st:
        hT = st.sb("hT", [P, KD, SEQ])
        stage_norm(core, "norm2", [(core.x1, core.sc[2], core.mod1[:, 24:32, 0])], hT, xn_dram=core.xn2)
        stage_router(core, hT)


def run_moe(core, out):
    core.x2 = core.dram("x2", [SEQ, D])
    stage_moe(core)
    stage_final_norm(core)


def run_second(core, out, l):
    io = core.io
    nctx = NC_ if l == 0 else 0
    if l == 0:
        core.x3, core.ctx3 = core.dram("x3", [SEQ, D]), core.dram("ctx3", [CTX, D])
        core.a_tok, core.b_t = core.dram("a_tok", [TOK, 256]), core.dram("b_t", [256, TOK])
        core.qk_tok, core.v_tok = core.dram("qk_tok", [2, TOK, BANK]), core.dram("v_tok", [TOK, BANK])
        core.gate_t = core.dram("gate_t", [D, TOK])
    x, ctx = (core.x2, io["ctx_2"][0]) if l == 0 else (core.x3, core.ctx3)
    m = core.mod2[l]
    name = f"layer{l}"
    with Stage(core, name + "_h") as st:
        hT = Parts(st, "hT", [P, KD, TOK])
        stage_norm(core, name + "_norm", [(x, core.sc[3 + 2 * l], m[:, 0:8, 0]), (ctx, core.sc[4 + 2 * l], m[:, 0:8, 1])], hT)
        w = io["w_in_2"][l]
        groups = []
        tiles = range(NT + nctx)
        spans = [(0, 512), (512, 512)] + ([(SEQ, CTX)] if nctx else [])
        groups.append((w[:, 0:BANK],
                       [("tok", t, 0, 256, core.a_tok[t * P:(t + 1) * P, :]) for t in tiles] +
                       [("ch", 2 + s, t0, n, core.b_t[s * P:(s + 1) * P, t0:t0 + n]) for s in range(2) for t0, n in spans]))
        for i in range(3):
            js = []
            for t in (tiles if i == 0 else range(NT + NC_)):
                dst = core.qk_tok[i] if i < 2 else core.v_tok
                js.append(("tok", t, 0, BANK, dst[t * P:(t + 1) * P, :]))
            groups.append((w[:, (1 + i) * BANK:(2 + i) * BANK], js))
        for i in range(2):
            groups.append((w[:, (4 + i) * BANK:(5 + i) * BANK],
                           [("ch", s, t0, n, core.gate_t[(4 * i + s) * P:(4 * i + s + 1) * P, t0:t0 + n])
                            for s in range(4) for t0, n in spans]))
        stage_project(core, name + "_proj", hT, groups)
    TL = NT + nctx
    with Stage(core, name + "_y") as sy:
        y_att = sy.sb("y_att", [P, 4, TL * P])
        with Stage(core, name + "_qk") as sq:
            q_parts = sq.sb("q_parts", [P, 2 * HEADS2, TL * P], F32R)
            k_high, k_low = sq.sb("k_high", [P, 2 * HEADS2, TOK], F32R), sq.sb("k_low", [P, HEADS2, TOK], F32R)
            neg_lam = sq.sb("neg_lam", [P, 1])
            stage_qk(core, l, list(tiles), q_parts, k_high, k_low, neg_lam, name + "_rope")
            stage_attend(core, l, list(tiles), q_parts, k_high, k_low, neg_lam, y_att, name + "_att")
        y_mix = sy.sb("y_mix", [P, 4, TL * P])
        stage_mix2(core, l, [(0, NT)] + ([(NT, NC_)] if nctx else []), y_att, y_mix, name + "_mix")
        dst = (core.x3, core.ctx3) if l == 0 else (out[0], None)
        rows = [(x[t * P:(t + 1) * P, :], dst[0][t * P:(t + 1) * P, :], 0) for t in range(NT)]
        rows += [(ctx[t * P:(t + 1) * P, :], dst[1][t * P:(t + 1) * P, :], 1) for t in range(nctx)]
        stage_out2(core, l, (y_mix, y_att), rows, name + "_out")


STAGES = [("mods", run_mods), ("proj1", run_first_projection), ("filter", run_filter), ("hyena", run_hyena),
          ("hgrn", run_hgrn), ("mixout", run_mix_out), ("router", run_router), ("moe", run_moe),
          ("layer0", lambda core, out: run_second(core, out, 0)), ("layer1", lambda core, out: run_second(core, out, 1))]


def tables():
    f64 = np.float64
    t = {}
    t["t_ident"] = np.eye(P)
    t["t_iota"] = np.tile(np.arange(SEQ), (P, 1))
    t["t_tokid"] = np.arange(SEQ).reshape(NT, P).T
    f32 = np.float32
    pos = np.linspace(0.0, 1.0, SEQ, dtype=f32)[:, None]
    w = (f32(2.0 * math.pi) * np.arange(SEQ, dtype=f32)[:, None] / f32(SEQ)).astype(f32)
    f = np.linspace(1e-4, 15, 16, dtype=f32)[None, :]
    fw = (f * w).astype(f32).astype(f64)
    t["t_pos"] = np.concatenate([pos, np.cos(fw), -np.sin(fw)], axis=1).T
    evens = np.concatenate([np.arange(0, SEQ, 2), np.arange(1, SEQ, 2)])
    t["t_pos"] = t["t_pos"][:, evens]
    lo, hi = math.log(1e-2) / 1.5, math.log(1e-2) / 0.3
    deltas = np.abs(np.linspace(lo, hi, HY, dtype=f32))
    t["t_window"] = np.exp((-pos * deltas[None, :]).astype(f32).astype(f64)) + 0.05
    t["t_window"] = t["t_window"][evens]
    t["t_window0"] = t["t_window"][0:P].copy()
    t["t_window0"][0] = 0.0
    k = np.concatenate([np.arange(0, SEQ, 2), SEQ - 1 - np.arange(0, SEQ, 2)])
    turn = ((2 * k[None, :SEQ // 2] + 1) * evens[:, None]) % (4 * SEQ)
    t["t_lag_cos"], t["t_lag_sin"] = np.cos(turn * math.pi / (2 * SEQ)), np.sin(turn * math.pi / (2 * SEQ))
    turn = ((2 * k[None, :] + 1) * (2 * np.arange(SEQ // 2)[:, None] + 1)) % (8 * SEQ)
    c, s = np.cos(turn * math.pi / (4 * SEQ)), np.sin(turn * math.pi / (4 * SEQ))
    t["t_fwd_add"], t["t_fwd_sub"] = c + s, c - s
    t["t_inv_add"], t["t_inv_sub"] = (c + s).T, (c - s).T
    key, query = np.arange(P)[:, None], np.arange(P)[None, :]
    masks = []
    for l in range(LEVELS):
        block = P >> l
        masks.append((key // block == query // block) & ((key % block < block // 2) != (query % block < block // 2)))
    masks.append(key == query)
    t["t_pair_masks"] = np.stack(masks, axis=1).reshape(P, 8 * P)
    half = QK // 2
    inv = (f32(10000.0) ** (-np.arange(0, half, 2, dtype=f32) / f32(half))).astype(f32)
    rows, cols = np.arange(SEQ) // GRID, np.arange(SEQ) % GRID
    ar = (rows.astype(f32)[:, None] * inv[None, :]).astype(f32).astype(f64)
    ac = (cols.astype(f32)[:, None] * inv[None, :]).astype(f32).astype(f64)
    t["t_rope_cos"] = np.cos(np.concatenate([ar, ar, ac, ac], axis=1))
    t["t_rope_sin"] = np.concatenate([-np.sin(ar), np.sin(ar), -np.sin(ac), np.sin(ac)], axis=1)
    for n, c_name, s_name, f in ((SEQ, "t_tok_cos", "t_tok_sin", 1.0), (CTX, "t_ctx_cos", "t_ctx_sin", 2.0)):
        turn = np.outer(np.arange(n), np.arange(n)) % n * (2 * math.pi / n)
        t[c_name], t[s_name] = f * np.cos(turn), f * np.sin(turn)
    turn = np.outer(np.arange(64), np.arange(64)) % 64 * (2 * math.pi / 64)
    t["t_dim_cos"] = np.kron(np.eye(2), np.cos(turn)) / 256
    t["t_dim_sin"] = np.kron(np.eye(2), np.sin(turn)) / 256
    for n, name in ((SEQ, "t_inv_count"), (CTX, "t_inv_count_ctx")):
        pos_ = np.arange(n)
        c = np.stack([1.0 / (np.minimum(pos_ + w // 2 - 1, n - 1) - np.maximum(pos_ - w // 2, 0) + 1)
                      for w in (2, 4, 8, 16)])
        t[name] = np.repeat(c, 64, axis=0).reshape(2, P, n).transpose(1, 0, 2).reshape(P, 2 * n)
    out = {k: np.ascontiguousarray(v, dtype=np.float32) for k, v in t.items()}
    return out


def kernel(**inputs):
    import concourse.bacc as bacc
    from concourse.bass_utils import run_bass_kernel_spmd

    nc = bacc.Bacc("TRN2", target_bir_lowering=False, num_devices=1)
    arrays = {k: np.ascontiguousarray(v) for k, v in inputs.items()}
    arrays.update(tables())
    io = {k: nc.dram_tensor("in_" + k, a.shape, mybir.dt.from_np(a.dtype), kind="ExternalInput").ap()
          for k, a in arrays.items()}
    out = nc.dram_tensor("out_x", (1, SEQ, D), F32, kind="ExternalOutput").ap()
    build_program(nc, io, out)
    r = run_bass_kernel_spmd(nc, [{"in_" + k: a for k, a in arrays.items()}], core_ids=[0])
    return r.results[0]["out_x"]
```

```python
import math
from contextlib import ExitStack, contextmanager

import concourse.bass as bass
import numpy as np
from concourse import mybir

F32 = mybir.dt.float32
F32R = mybir.dt.float32r
BF16 = mybir.dt.bfloat16
U32 = mybir.dt.uint32
ALU = mybir.AluOpType
ACT = mybir.ActivationFunctionType
AX = mybir.AxisListType.X

P = 128
D = 1024
KD = D // P
SEQ = 1024
NT = SEQ // P
CTX = 256
NC_ = CTX // P
TOK = SEQ + CTX
BANK = 512
GRID = 64
EPS = 1e-6
HY = 512
HG_HEADS = 4
LEVELS = 7
HFF = 64
POS = 33
E = 16
CAP = 128
FF = 2048
EPS_F = 1e-6
TWO_PI = 2.0 * math.pi
TWO_PI_HI = 6.28125
TWO_PI_LO = TWO_PI - TWO_PI_HI
ROUND = 1.5 * 2.0 ** 23
PI_IN = 3.1415925
HEADS2 = 4
QK = 64


class Chain:

    def __init__(self, sem):
        self.sem, self.n = sem, 0

    def __call__(self, eng, ins):
        self.n += 1
        ins.then_inc(self.sem, 1)
        eng.wait_ge(self.sem, self.n)


class Lane:

    def __init__(self, sem):
        self.sem, self.base = sem, 0

    def at(self, k):
        return self.base + 16 * k

    def close(self, k):
        self.base += 16 * k


class Core:

    def __init__(self, nc, io, tap):
        self.nc, self.io, self.tap = nc, io, tap
        self.stack = ExitStack()
        self.zeroed_sems, self.used_sems, self.retired_sems, self.n_stage_sems = [], [], [], 0
        self.dve = Chain(self.sem("dve_step_done"))
        self.act = Chain(self.sem("act_step_done"))
        self.pool = Chain(self.sem("pool_step_done"))
        self.load = [Lane(self.sem(f"load_done_{i}")) for i in range(12)]
        self.store = [Lane(self.sem(f"store_done_{i}")) for i in range(8)]
        self.hstore = [Lane(self.sem(f"store_done_hw_{i}")) for i in range(6)]

    def sem(self, name):
        return self.stack.enter_context(self.nc.semaphore(name))

    def dram(self, name, shape, dt=F32):
        kind = "ExternalOutput" if self.tap and name in self.tap else "Internal"
        return self.nc.dram_tensor(name, shape, dt, kind=kind).ap()

    def keep(self, name, shape, dt=F32):
        return self.stack.enter_context(self.nc.sbuf_tensor(name, shape, dt))


class Stage:

    def __init__(self, core, name):
        self.core, self.nc, self.name = core, core.nc, name
        self.stack = ExitStack()

    def __enter__(self):
        return self

    def __exit__(self, *a):
        self.stack.close()

    def sb(self, name, shape, dt=F32):
        return self.stack.enter_context(self.nc.sbuf_tensor(f"{self.name}_{name}", shape, dt))

    def banks(self, n, dt=F32):
        return [self.stack.enter_context(self.nc.psum_tensor(f"{self.name}_bank{i}", [P, BANK], dt))
                for i in range(n)]

    def sem(self, name):
        core = self.core
        s = core.zeroed_sems.pop() if core.zeroed_sems else core.sem(f"stage_{core.n_stage_sems}_{self.name}_{name}")
        core.n_stage_sems += 1
        core.used_sems.append(s)
        return s

    def dma_sem(self, name):
        return self.core.sem(f"{self.name}_{name}")

    @contextmanager
    def block(self):
        core = self.core
        mine, core.used_sems = core.used_sems, []
        with self.nc.Block() as block:
            retired, core.retired_sems = core.retired_sems, mine
            if retired:
                @block.sync
                def _(sp):
                    for s in retired:
                        sp.sem_clear(s)
            yield block
        core.zeroed_sems += retired


VEC_A = [("c", 8), ("c_ctx", 8), ("c_2", 8), ("c_ctx_2", 8), ("norm1_g", 8), ("norm2_g", 8),
         ("norm_g_2", 16), ("hy_norm_g", 4), ("hg_norm_g", 1), ("hy_conv_w", 36), ("hy_conv_b", 12)]
VEC_B = [("hg_lb", 16), ("pool_scale_2", 4), ("subln_g_2", 2)]
VEC_C = [("hy_pos_b1", 1), ("hy_freq1", 1), ("hy_pos_b2", 1), ("hy_freq2", 1)]


class Parts:

    def __init__(self, st, name, shape):
        self.high, self.low = st.sb(name + "_high", shape, F32R), st.sb(name + "_low", shape, F32R)

    def __getitem__(self, key):
        return self.high[key], self.low[key]


def product(nc, out, lhs, rhs, start, stop):
    nc.tensor.matmul(out, lhs[0], rhs[0], start=start, stop=False)
    nc.tensor.matmul(out, lhs[0], rhs[1], start=False, stop=False)
    return nc.tensor.matmul(out, lhs[1], rhs[0], start=False, stop=stop)


def offsets(vec):
    at, n = {}, 0
    for name, k in vec:
        at[name] = n
        n += k
    return at, n


AT_A, N_A = offsets(VEC_A)
AT_B, N_B = offsets(VEC_B)


def as_rows(ap, width):
    s = " ".join(f"a{i}" for i in range(len(ap.shape)))
    flat = ap.rearrange(f"{s} -> ({s})")
    return flat.rearrange("(r w) -> r w", w=width)


def stage_mods(core):
    nc, io = core.nc, core.io
    groups = [("ada_w", 0, g) for g in range(12)] + [("w_mod_2", l, g) for l in range(2) for g in range(6)]
    RING, RP, RR = 3, 2, 4
    with Stage(core, "mods") as st:
        rows_a, rows_b = st.sb("rows_a", [N_A, P]), st.sb("rows_b", [N_B, P])
        rows_c = st.sb("rows_c", [4, HFF])
        silu_all, silu = st.sb("silu_all", [P, 32]), Parts(st, "silu", [P, 32])
        raw = [st.sb(f"raw{i}", [P, KD, BANK]) for i in range(RING)]
        w = [Parts(st, f"w{i}", [P, KD, BANK]) for i in range(RP)]
        lbmax, lbd = st.sb("lbmax", [P, 8]), st.sb("lbd", [P, 2, 8])
        lbe, lbs = st.sb("lbe", [P, 2, 8]), st.sb("lbs", [P, 8])
        rows = [st.sb(f"rows{i}", [2, BANK]) for i in range(RR)]
        bias = st.sb("bias", [2, len(groups) * BANK])
        bank = st.banks(6)
        vecs, columns, silu_done, mods_done = (st.sem(x) for x in ("vecs", "columns", "silu", "mods"))
        cols_copied, w_used, bias_added = (st.sem(x) for x in ("cols_copied", "w_used", "bias_added"))
        high, low = st.sem("high"), st.sem("low")
        halves = [slice(0, KD // 2), slice(KD // 2, KD)]
        biases, turned = st.sem("biases"), st.sem("turned")
        n_vec = 0
        loads = []
        for dst, vec, width in ((rows_a, VEC_A, P), (rows_b, VEC_B, P), (rows_c, VEC_C, HFF)):
            r = 0
            for name, k in vec:
                loads.append((dst[r:r + k, :], as_rows(io[name], width)))
                r += k
        with st.block() as block:
            @block.sync
            def _(sp):
                sp.dma_start(core.ident[:, :], io["t_ident"]).then_inc(vecs, 16)
                for dst, src in loads:
                    sp.dma_start(dst, src).then_inc(vecs, 16)
                sp.dma_start(bias[:, 0:6 * D], io["ada_b"][0].partition_broadcast(2)).then_inc(biases, 16)
                for l in range(2):
                    sp.dma_start(bias[:, (6 + 3 * l) * D:(9 + 3 * l) * D],
                                 io["b_mod_2"][l].partition_broadcast(2)).then_inc(biases, 16)
                for i in range(len(groups) + RING + 1):
                    if i < len(groups):
                        name, l, g = groups[i]
                        if i >= RING:
                            sp.wait_ge(low, 2 * (i - RING + 1) + 1)
                        sp.dma_start(raw[i % RING][:, :, :],
                                     io[name][l, :, g * BANK:(g + 1) * BANK].rearrange("(k p) n -> p k n", p=P)
                                     ).then_inc(core.load[i % RING].sem, 16)
                    j = i - RING - 1
                    if j >= 0:
                        sp.wait_ge(bias_added, j + 1)
                        m, c = (0, j) if j < 12 else divmod(j - 6, 6)
                        sp.dma_start(core.mod_rows[m][:, c * BANK:(c + 1) * BANK], rows[j % RR][:, :]
                                     ).then_inc(core.hstore[j % RR].sem, 16)
                for j in range(RR):
                    sp.wait_ge(core.hstore[j].sem, core.hstore[j].at(len(groups) // RR))

            @block.gpsimd
            def _(pool):
                nc.gpsimd.memset(core.eps[:, :], EPS)

            @block.tensor
            def _(pe):
                pe.wait_ge(vecs, 16 * (1 + len(loads)))
                nc.tensor.transpose(bank[0][:, 0:N_A], rows_a[:, :], core.ident[0:N_A, 0:N_A])
                nc.tensor.transpose(bank[0][:, P:P + N_B], rows_b[:, :], core.ident[0:N_B, 0:N_B])
                nc.tensor.transpose(bank[0][0:HFF, 2 * P:2 * P + 4], rows_c[:, :],
                                    core.ident[0:4, 0:4]).then_inc(columns, 1)
                def to_columns(i):
                    pe.wait_ge(bias_added, i + 1)
                    for s in range(4):
                        o = 2 * (4 * i + s)
                        last = nc.tensor.transpose(bank[1][:, o:o + 2], rows[i % RR][:, s * P:(s + 1) * P],
                                                   core.ident[0:2, 0:2])
                    last.then_inc(turned, 1)

                for i, (name, l, g) in enumerate(groups):
                    if i >= 4:
                        pe.wait_ge(bias_added, i - 3)
                    v0 = 0 if name == "ada_w" else 2
                    for k in range(KD):
                        if k % (KD // 2) == 0:
                            pe.wait_ge(low, 1 + 2 * i + k // (KD // 2) + 1)
                        last = product(nc, bank[2 + i % 4][0:2, :], silu[:, v0 * 8 + k:v0 * 8 + k + 9:8],
                                       w[i % RP][:, k, :], k == 0, k == KD - 1)
                    last.then_inc(w_used, 1)
                    if i:
                        to_columns(i - 1)
                to_columns(len(groups) - 1)

            @block.scalar
            def _(act):
                act.wait_ge(cols_copied, 1)
                core.act(act, nc.scalar.activation(silu_all[:, :], core.col_a[:, 0:32], ACT.Silu))
                nc.scalar.activation(silu.high[:, :], silu_all[:, :], ACT.Copy).then_inc(silu_done, 1)
                act.wait_ge(cols_copied, 2)
                nc.scalar.activation(lbe[:, :, :], lbd[:, :, :], ACT.Exp).then_inc(mods_done, 1)
                for i in range(len(groups)):
                    act.wait_ge(core.load[i % RING].sem, core.load[i % RING].at(i // RING + 1))
                    if i >= RP:
                        act.wait_ge(w_used, i - RP + 1)
                    for c in halves:
                        nc.scalar.activation(w[i % RP].high[:, c, :], raw[i % RING][:, c, :], ACT.Copy).then_inc(high, 1)

            @block.vector
            def _(dve):
                step = lambda ins: core.dve(dve, ins)
                dve.wait_ge(columns, 1)
                core.dve(dve, nc.vector.tensor_copy(core.col_b[:, :], bank[0][:, P:P + N_B]))
                core.dve(dve, nc.vector.tensor_copy(core.col_c[:, :], bank[0][0:HFF, 2 * P:2 * P + 4]))
                nc.vector.tensor_copy(core.col_a[:, :], bank[0][:, 0:N_A]).then_inc(cols_copied, 1)
                lb = core.col_b[:, AT_B["hg_lb"]:AT_B["hg_lb"] + 16].rearrange("p (l c) -> p l c", l=2)
                core.dve(dve, nc.vector.tensor_tensor(lbmax[:, :], lb[:, 0, :], lb[:, 1, :], ALU.max))
                nc.vector.tensor_tensor(lbd[:, :, :], lb, lbmax[:, :].unsqueeze(1).to_broadcast([P, 2, 8]),
                                        ALU.subtract).then_inc(cols_copied, 1)
                dve.wait_ge(mods_done, 1)
                core.dve(dve, nc.vector.tensor_tensor(lbs[:, :], lbe[:, 0, :], lbe[:, 1, :], ALU.add))
                core.dve(dve, nc.vector.reciprocal(lbs[:, :], lbs[:, :]))
                core.dve(dve, nc.vector.tensor_tensor(core.lb[:, 0, :], lbe[:, 0, :], lbs[:, :], ALU.mult))
                core.dve(dve, nc.vector.tensor_tensor(core.lb[:, 1, :], lbe[:, 1, :], lbs[:, :], ALU.mult))
                dve.wait_ge(silu_done, 1)
                nc.vector.tensor_tensor(silu.low[:, :], silu_all[:, :], silu.high[:, :].bitcast(F32),
                                        ALU.subtract).then_inc(low, 1)

                def add_bias(i):
                    c = slice(i * BANK, (i + 1) * BANK)
                    dve.wait_ge(w_used, i + 1)
                    if i >= RR:
                        dve.wait_ge(turned, i - RR + 1)
                        dve.wait_ge(core.hstore[i % RR].sem, core.hstore[i % RR].at(i // RR))
                    nc.vector.tensor_tensor(rows[i % RR][:, :], bank[2 + i % 4][0:2, :], bias[:, c], ALU.add
                                            ).then_inc(bias_added, 1)

                dve.wait_ge(biases, 48)
                for i in range(len(groups)):
                    for s, c in enumerate(halves):
                        dve.wait_ge(high, 2 * i + s + 1)
                        nc.vector.tensor_tensor(w[i % RP].low[:, c, :], raw[i % RING][:, c, :],
                                                w[i % RP].high[:, c, :].bitcast(F32), ALU.subtract).then_inc(low, 1)
                    if i:
                        add_bias(i - 1)
                add_bias(len(groups) - 1)
                dve.wait_ge(turned, len(groups))
                for m, o, n in ((core.mod1, 0, 48), (core.mod2[0], 96, 24), (core.mod2[1], 144, 24)):
                    step(nc.vector.tensor_copy(m[:, :, :], bank[1][:, o:o + 2 * n].rearrange("p (c v) -> p c v", v=2)))
                for out, m, c0, v, g in (
                        (core.sc[0], core.mod1, 8, 0, AT_A["norm1_g"]), (core.sc[1], core.mod1, 8, 1, AT_A["norm1_g"]),
                        (core.sc[2], core.mod1, 32, 0, AT_A["norm2_g"]),
                        (core.sc[3], core.mod2[0], 8, 0, AT_A["norm_g_2"]), (core.sc[4], core.mod2[0], 8, 1, AT_A["norm_g_2"]),
                        (core.sc[5], core.mod2[1], 8, 0, AT_A["norm_g_2"] + 8), (core.sc[6], core.mod2[1], 8, 1, AT_A["norm_g_2"] + 8)):
                    core.dve(dve, nc.vector.scalar_tensor_tensor(out[:, :], m[:, c0:c0 + 8, v], 1.0,
                                                                 core.col_a[:, g:g + 8], ALU.add, ALU.mult))
        for i in range(RING):
            core.load[i].close(len(range(i, len(groups), RING)))
        for i in range(RR):
            core.hstore[i].close(len(groups) // RR)


def stage_norm(core, name, segs, hT, xn_dram=None, ahead=()):
    nc = core.nc
    tiles = [(src[t * P:(t + 1) * P, :], sc, sh) for src, sc, sh in segs for t in range(src.shape[0] // P)]
    n = len(tiles)
    RX = 3
    with Stage(core, name) as st:
        x = [st.sb(f"x{i}", [P, D]) for i in range(RX)]
        xn = [st.sb(f"xn{i}", [P, D]) for i in range(RX)]
        junk = st.sb("junk", [P, D])
        ss, rms, rstd = st.sb("ss", [P, n]), st.sb("rms", [P, n]), st.sb("rstd", [P, n])
        parts = isinstance(hT, Parts)
        whole = [[st.sb(f"whole{half}_{i}", [P, 4, P]) for i in range(2)] for half in range(2)] if parts else None
        split = st.sem("split")
        bank = st.banks(4)

        def modulated(i, k):
            if parts:
                return whole[k // 4][i % 2][:, k % 4, :], hT.high[:, k, i * P:(i + 1) * P]
            return (hT[:, k, i * P:(i + 1) * P],)

        rms_done, xn_done, turned, out_a, out_v = (st.sem(k) for k in ("rms", "xn", "turned", "out_a", "out_v"))
        with st.block() as block:
            @block.sync
            def _(sp):
                for i, (src, _, _) in enumerate(tiles):
                    if i >= RX:
                        sp.wait_ge(xn_done, i - RX + 1)
                    sp.dma_start(x[i % RX][:, :], src).then_inc(core.load[i % RX].sem, 16)
                    if i == n - 2:
                        for dst, w_src, lane in ahead:
                            sp.dma_start(dst, w_src).then_inc(core.load[lane].sem, 16)

            @block.gpsimd
            def _(pool):
                if parts:
                    for i in range(n):
                        for half, moved in enumerate((out_a, out_v)):
                            pool.wait_ge(moved, i + 1)
                            src, c = whole[half][i % 2][:, :, :], slice(4 * half, 4 * half + 4)
                            high, low = (y[:, c, i * P:(i + 1) * P] for y in (hT.high, hT.low))
                            nc.gpsimd.tensor_tensor(low, src, high.bitcast(F32), ALU.subtract).then_inc(split, 1)
                if xn_dram is not None:
                    for i in range(n):
                        pool.wait_ge(xn_done, i + 1)
                        pool.dma_start(xn_dram[i * P:(i + 1) * P, :], xn[i % RX][:, :]
                                       ).then_inc(core.store[i % RX].sem, 16)
                    for j in range(RX):
                        pool.wait_ge(core.store[j].sem, core.store[j].at(len(range(j, n, RX))))

            @block.scalar
            def _(act):
                def measure(i):
                    act.wait_ge(core.load[i % RX].sem, core.load[i % RX].at(i // RX + 1))
                    core.act(act, nc.scalar.activation(junk[:, :], x[i % RX][:, :], ACT.Square,
                                                       accum_out=ss[:, i:i + 1]))
                    nc.scalar.activation(rms[:, i:i + 1], ss[:, i:i + 1], ACT.Sqrt, bias=core.eps[:, 0:1],
                                         scale=1.0 / D).then_inc(rms_done, 1)

                measure(0)
                for i, (_, sc, sh) in enumerate(tiles):
                    if i + 1 < n:
                        measure(i + 1)
                    act.wait_ge(turned, 2 * i + 1)
                    if parts and i >= 2:
                        act.wait_ge(split, 2 * (i - 2) + 1)
                    for k in range(4):
                        for to in modulated(i, k):
                            last = nc.scalar.activation(to, bank[2 * (i % 2)][:, k * P:(k + 1) * P], ACT.Identity,
                                                        bias=sh[:, k:k + 1], scale=sc[:, k:k + 1])
                    last.then_inc(out_a, 1)

            @block.vector
            def _(dve):
                def normalise(i):
                    dve.wait_ge(rms_done, i + 1)
                    core.dve(dve, nc.vector.reciprocal(rstd[:, i:i + 1], rms[:, i:i + 1]))
                    if i >= RX:
                        dve.wait_ge(turned, 2 * (i - RX) + 2)
                        if xn_dram is not None:
                            dve.wait_ge(core.store[i % RX].sem, core.store[i % RX].at(i // RX))
                    nc.vector.tensor_scalar(xn[i % RX][:, :], x[i % RX][:, :], rstd[:, i:i + 1], None,
                                            ALU.mult).then_inc(xn_done, 1)

                normalise(0)
                for i, (_, sc, sh) in enumerate(tiles):
                    if i + 1 < n:
                        normalise(i + 1)
                    dve.wait_ge(turned, 2 * i + 2)
                    if parts and i >= 2:
                        dve.wait_ge(split, 2 * (i - 2) + 2)
                    for k in range(4, 8):
                        for to in modulated(i, k):
                            last = nc.vector.tensor_scalar(to, bank[2 * (i % 2) + 1][:, (k - 4) * P:(k - 3) * P],
                                                           sc[:, k:k + 1], sh[:, k:k + 1], ALU.mult, ALU.add)
                    last.then_inc(out_v, 1)

            @block.tensor
            def _(pe):
                for i in range(n):
                    pe.wait_ge(xn_done, i + 1)
                    if i >= 2:
                        pe.wait_ge(out_a, i - 1)
                        pe.wait_ge(out_v, i - 1)
                    for half in range(2):
                        for k in range(4):
                            c = (4 * half + k) * P
                            last = nc.tensor.transpose(bank[2 * (i % 2) + half][:, k * P:(k + 1) * P],
                                                       xn[i % RX][:, c:c + P], core.ident[:, :])
                        last.then_inc(turned, 1)
        for j in range(RX):
            core.load[j].close(len(range(j, n, RX)))
            if xn_dram is not None:
                core.store[j].close(len(range(j, n, RX)))


W_LANE = 8


def project_ahead(raw, groups):
    return [(raw[g][:, :, 0:src.shape[1]], src.rearrange("(k p) n -> p k n", p=P), W_LANE + g)
            for g, (src, _) in enumerate(groups[:len(raw)])]


def stage_project(core, name, hT, raw, groups):
    nc = core.nc
    RW, RP, RS, NB = 2, 2, 8, 8
    SP_ = 4
    KP = KD // SP_
    jobs = [(g, j) for g, (_, js) in enumerate(groups) for j in js]
    first = {}
    for i, (g, _) in enumerate(jobs):
        first.setdefault(g, i)
    with Stage(core, name) as st:
        w = [Parts(st, f"w{i}", [P, KD, BANK]) for i in range(RP)]
        out = [st.sb(f"out{i}", [P, BANK]) for i in range(RS)]
        bank = st.banks(NB)
        done, copied_a, copied_v, high, low = (st.sem(k) for k in ("product", "copied_a", "copied_v", "high", "low"))

        def wait_copied(eng, i):
            eng.wait_ge(copied_v if i % 2 else copied_a, i // 2 + 1)

        with st.block() as block:
            @block.sync
            def _(sp):
                for g, (src, _) in enumerate(groups):
                    if g < RW:
                        continue
                    sp.wait_ge(low, SP_ * (g - RW + 1))
                    sp.dma_start(raw[g % RW][:, :, 0:src.shape[1]], src.rearrange("(k p) n -> p k n", p=P)
                                 ).then_inc(core.load[W_LANE + g % RW].sem, 16)

            @block.tensor
            def _(pe):
                for i, (g, (kind, a, b, n, _)) in enumerate(jobs):
                    if i >= NB:
                        wait_copied(pe, i - NB)
                    for k in range(KD):
                        if first[g] == i and k % KP == 0:
                            pe.wait_ge(low, SP_ * g + k // KP + 1)
                        if kind == "ch":
                            lhs, rhs = w[g % RP][:, k, a * P:(a + 1) * P], hT[:, k, b:b + n]
                        else:
                            lhs, rhs = hT[:, k, a * P:(a + 1) * P], w[g % RP][:, k, b:b + n]
                        last = product(nc, bank[i % NB][:, 0:n], lhs, rhs, k == 0, k == KD - 1)
                    last.then_inc(done, 1)

            def piece(g, p):
                c = slice(p * KP, (p + 1) * KP)
                return raw[g % RW][:, c, :], w[g % RP].high[:, c, :], w[g % RP].low[:, c, :]

            def split_high(eng, g, p):
                if p == 0:
                    eng.wait_ge(core.load[W_LANE + g % RW].sem, core.load[W_LANE + g % RW].at(g // RW + 1))
                    if g >= RP:
                        eng.wait_ge(done, first[g - RP + 1])
                x, hi, _ = piece(g, p)
                nc.scalar.activation(hi, x, ACT.Copy).then_inc(high, 1)

            def split_low(eng, g, p):
                eng.wait_ge(high, SP_ * g + p + 1)
                x, hi, lo = piece(g, p)
                nc.vector.tensor_tensor(lo, x, hi.bitcast(F32), ALU.subtract).then_inc(low, 1)

            def run(eng, fn, odd, sem, split):
                for p in range(SP_):
                    split(eng, 0, p)
                for i, (g, (kind, a, b, n, _)) in enumerate(jobs):
                    if i - first[g] < SP_ and g + 1 < len(groups):
                        split(eng, g + 1, i - first[g])
                    if i % 2 != odd:
                        continue
                    eng.wait_ge(done, i + 1)
                    if i >= RS:
                        eng.wait_ge(core.store[i % RS].sem, core.store[i % RS].at(i // RS))
                    fn(out[i % RS][:, 0:n], bank[i % NB][:, 0:n]).then_inc(sem, 1)

            @block.scalar
            def _(act):
                run(act, lambda o, i: nc.scalar.activation(o, i, ACT.Copy), 0, copied_a, split_high)

            @block.vector
            def _(dve):
                run(dve, nc.vector.tensor_copy, 1, copied_v, split_low)

            @block.gpsimd
            def _(pool):
                for i, (g, (kind, a, b, n, dst)) in enumerate(jobs):
                    wait_copied(pool, i)
                    pool.dma_start(dst, out[i % RS][:, 0:n]).then_inc(core.store[i % RS].sem, 16)
                for j in range(RS):
                    pool.wait_ge(core.store[j].sem, core.store[j].at(len(range(j, len(jobs), RS))))
        for j in range(RW):
            core.load[W_LANE + j].close(len(range(j, len(groups), RW)))
        for j in range(RS):
            core.store[j].close(len(range(j, len(jobs), RS)))


def stage_filter(core, name="filter"):
    nc, io = core.nc, core.io
    NU = 2 * NT
    HF = NT // 2
    RS = 6
    with Stage(core, name) as st:
        z, w1, w2 = st.sb("z", [POS, SEQ]), st.sb("w1", [POS, HFF]), st.sb("w2", [HFF, HFF])
        w3 = st.sb("w3", [HFF, 4 * HY])
        tab = [st.sb("cos", [P, NT, SEQ // 2]), st.sb("sin", [P, NT, SEQ // 2])]
        win, win0 = st.sb("win", [P, NT, HY]), st.sb("win0", [P, HY])
        lin, turns, h = st.sb("lin", [HFF, SEQ]), st.sb("turns", [HFF, SEQ]), st.sb("h", [HFF, SEQ])
        ha, hb = [[st.sb(f"h{c}{i}", [P, HY]) for i in range(2)] for c in "ab"]
        aa, ab = [[st.sb(f"abs{c}{i}", [P, HY]) for i in range(2)] for c in "ab"]
        acc = [st.sb(f"acc{o}", [P, HY]) for o in range(2)]
        eo = [[st.sb(f"{c}{i}", [P, HY]) for i in range(2)] for c in ("even", "odd")]
        fold = [[st.sb(f"sum{o}", [P, NT, HY]), st.sb(f"dif{o}", [P, NT, HY])] for o in range(2)]
        gain = [st.sb(f"gain{o}", [P, HY]) for o in range(2)]
        skip = [st.sb(f"skip{o}", [P, HY]) for o in range(2)]
        ones = st.sb("ones", [P, P])
        out = [st.sb(f"out{i}", [P, HY]) for i in range(RS)]
        bank = st.banks(8)
        small, tables, lay, sines, taps, windowed, absd, folded, normed, gains, spec, scaled, final, ones_set = (
            st.sem(k) for k in ("small", "tables", "layer", "sines", "taps", "windowed", "abs", "folded",
                                "normed", "gains", "spec", "scaled", "final", "ones"))
        summed, windows = st.sem("summed"), st.sem("windows")
        b1, fr1, b2, fr2 = (core.col_c[:, i:i + 1] for i in range(4))
        pairs = [(o, f, s) for o in range(2) for f in range(HF) for s in range(2)]
        with st.block() as block:
            @block.sync
            def _(sp):
                sp.dma_start(z[:, :], io["t_pos"]).then_inc(small, 16)
                sp.dma_start(w1[:, :], io["hy_pos_w1"][0]).then_inc(small, 16)
                sp.dma_start(w2[:, :], io["hy_pos_w2"][0]).then_inc(small, 16)
                sp.dma_start(w3[:, :], io["hy_pos_w3"][0]).then_inc(small, 16)
                for o in range(2):
                    sp.dma_start(skip[o][:, :], io["hy_bias"][0][o].partition_broadcast(P)).then_inc(small, 16)
                sp.dma_start(win[:, :, :], io["t_window"].rearrange("(j p) c -> p j c", p=P)).then_inc(windows, 16)
                sp.dma_start(win0[:, :], io["t_window0"]).then_inc(windows, 16)
                sp.dma_start(tab[0][:, :, :], io["t_lag_cos"].rearrange("(j p) k -> p j k", p=P)).then_inc(tables, 16)
                sp.dma_start(tab[1][:, :, :], io["t_lag_sin"].rearrange("(j p) k -> p j k", p=P)).then_inc(tables, 16)
                for i, (o, f, s) in enumerate(pairs):
                    for m in range(2):
                        n = 2 * i + m
                        sp.wait_ge(final, n + 1)
                        row = (f + m * HF) * P
                        sp.dma_start(core.spectra[o, s, row:row + P, :], out[n % RS][:, :]
                                     ).then_inc(core.hstore[n % RS].sem, 16)
                for j in range(RS):
                    sp.wait_ge(core.hstore[j].sem, core.hstore[j].at(len(range(j, 2 * len(pairs), RS))))

            @block.tensor
            def _(pe):
                pe.wait_ge(small, 16 * 6)
                for layer, (w, x, k) in enumerate(((w1, z, POS), (w2, h, HFF))):
                    if layer:
                        pe.wait_ge(sines, 1)
                    for t in range(2):
                        last = nc.tensor.matmul(bank[6 + t][0:HFF, :], w[0:k, :], x[0:k, t * BANK:(t + 1) * BANK],
                                                start=True, stop=True)
                    last.then_inc(lay, 1)
                pe.wait_ge(sines, 2)
                pe.wait_ge(ones_set, 1)

                for u in range(NU):
                    j, o = divmod(u, 2)
                    if u >= 2:
                        pe.wait_ge(windowed, u - 1)
                    for s in range(2):
                        last = nc.tensor.matmul(bank[2 * (u % 2) + s][:, :], h[:, j * P:(j + 1) * P],
                                                w3[:, (2 * o + s) * HY:(2 * o + s + 1) * HY], start=True, stop=True)
                    last.then_inc(taps, 1)
                pe.wait_ge(summed, NU)
                for o in range(2):
                    nc.tensor.matmul(bank[6 + o][:, :], ones[:, :], acc[o][:, :], start=True, stop=True).then_inc(normed, 1)
                pe.wait_ge(folded, NU)
                pe.wait_ge(windowed, NU)
                pe.wait_ge(tables, 32)
                for i, (o, f, s) in enumerate(pairs):
                    if i >= 3:
                        pe.wait_ge(scaled, 2 * (i - 2))
                    for odd in range(2):
                        for j in range(HF):
                            jj = odd * HF + j
                            last = nc.tensor.matmul(bank[2 * (i % 3) + odd][:, :], tab[s][:, jj, f * P:(f + 1) * P],
                                                    fold[o][s][:, jj, :], start=(j == 0), stop=(j == HF - 1))
                        last.then_inc(spec, 1)

            @block.scalar
            def _(act):
                for layer in range(2):
                    act.wait_ge(gains, layer + 1)
                    nc.scalar.activation(h[:, :], lin[:, :], ACT.Sin).then_inc(sines, 1)

                for u in range(NU):
                    act.wait_ge(windowed, u + 1)
                    if u >= 2:
                        act.wait_ge(summed, u - 1)
                    nc.scalar.activation(aa[u % 2][:, :], ha[u % 2][:, :], ACT.Abs)
                    nc.scalar.activation(ab[u % 2][:, :], hb[u % 2][:, :], ACT.Abs).then_inc(absd, 1)

            @block.gpsimd
            def _(pool):
                nc.gpsimd.memset(ones[:, :], 1.0).then_inc(ones_set, 1)
                for u in range(NU):
                    j, o = divmod(u, 2)
                    pool.wait_ge(windowed, u + 1)
                    nc.gpsimd.tensor_tensor(fold[o][0][:, j, :], ha[u % 2][:, :], hb[u % 2][:, :], ALU.add)
                    nc.gpsimd.tensor_tensor(fold[o][1][:, j, :], ha[u % 2][:, :], hb[u % 2][:, :],
                                            ALU.subtract).then_inc(folded, 1)
                for i, (o, f, s) in enumerate(pairs):
                    pool.wait_ge(scaled, 2 * (i + 1))
                    for m in range(2):
                        n = 2 * i + m
                        if n >= RS:
                            pool.wait_ge(core.hstore[n % RS].sem, core.hstore[n % RS].at(n // RS))
                        a, b = (eo[0], eo[1]) if s == 0 else (eo[1], eo[0])
                        nc.gpsimd.tensor_tensor(out[n % RS][:, :], a[i % 2][:, :], b[i % 2][:, :],
                                                ALU.subtract if m else ALU.add).then_inc(final, 1)

            @block.vector
            def _(dve):
                step = lambda ins: core.dve(dve, ins)
                for layer, (b, fr) in enumerate(((b1, fr1), (b2, fr2))):
                    dve.wait_ge(lay, layer + 1)
                    if layer:
                        dve.wait_ge(sines, 1)
                    for t in range(2):
                        c = slice(t * BANK, (t + 1) * BANK)
                        step(nc.vector.tensor_scalar(lin[:, c], bank[6 + t][0:HFF, :], b, fr, ALU.add, ALU.mult))
                    step(nc.vector.tensor_scalar(turns[:, :], lin[:, :], 1.0 / TWO_PI, ROUND, ALU.mult, ALU.add))
                    step(nc.vector.tensor_scalar(turns[:, :], turns[:, :], ROUND, None, ALU.subtract))
                    step(nc.vector.scalar_tensor_tensor(lin[:, :], turns[:, :], -TWO_PI_HI, lin[:, :], ALU.mult, ALU.add))
                    step(nc.vector.scalar_tensor_tensor(lin[:, :], turns[:, :], -TWO_PI_LO, lin[:, :], ALU.mult, ALU.add))
                    nc.vector.tensor_scalar(lin[:, :], lin[:, :], PI_IN, -PI_IN, ALU.min, ALU.max).then_inc(gains, 1)

                def add_up(u):
                    j, o = divmod(u, 2)
                    dve.wait_ge(absd, u + 1)
                    if j:
                        step(nc.vector.tensor_tensor(acc[o][:, :], acc[o][:, :], aa[u % 2][:, :], ALU.add))
                        ins = nc.vector.tensor_tensor(acc[o][:, :], acc[o][:, :], ab[u % 2][:, :], ALU.add)
                    else:
                        ins = nc.vector.tensor_tensor(acc[o][:, :], aa[u % 2][:, :], ab[u % 2][:, :], ALU.add)
                    ins.then_inc(summed, 1)
                    dve.wait_ge(summed, u + 1)

                dve.wait_ge(windows, 32)
                dve.wait_ge(small, 16 * 6)
                for u in range(NU):
                    j, o = divmod(u, 2)
                    dve.wait_ge(taps, u + 1)
                    if u >= 2:
                        dve.wait_ge(folded, u - 1)
                        dve.wait_ge(absd, u - 1)
                    nc.vector.tensor_tensor(ha[u % 2][:, :], bank[2 * (u % 2)][:, :], win[:, j, :], ALU.mult)
                    nc.vector.tensor_tensor(hb[u % 2][:, :], bank[2 * (u % 2) + 1][:, :],
                                            win0[:, :] if j == 0 else win[:, j, :], ALU.mult).then_inc(windowed, 1)
                    if u:
                        add_up(u - 1)
                add_up(NU - 1)
                dve.wait_ge(normed, 2)
                for o in range(2):
                    step(nc.vector.tensor_scalar(gain[o][:, :], bank[6 + o][:, :], EPS, None, ALU.add))
                    step(nc.vector.reciprocal(gain[o][:, :], gain[o][:, :]))
                    step(nc.vector.tensor_scalar(gain[o][:, :], gain[o][:, :], 0.5 / SEQ, None, ALU.mult))
                    step(nc.vector.tensor_scalar(skip[o][:, :], skip[o][:, :], 0.5 / SEQ, None, ALU.mult))
                for i, (o, f, s) in enumerate(pairs):
                    if i >= 2:
                        dve.wait_ge(final, 2 * (i - 1))
                    for odd in range(2):
                        dve.wait_ge(spec, 2 * i + odd + 1)
                        to = eo[odd][i % 2][:, :]
                        ins = nc.vector.tensor_tensor(to, bank[2 * (i % 3) + odd][:, :], gain[o][:, :], ALU.mult)
                        if s == 0 and odd == 0:
                            step(ins)
                            ins = nc.vector.tensor_tensor(to, to, skip[o][:, :], ALU.add)
                        ins.then_inc(scaled, 1)
        for j in range(RS):
            core.hstore[j].close(len(range(j, 2 * len(pairs), RS)))


def stage_hyena(core, name="hyena"):
    nc, io = core.nc, core.io
    CH, TH = HY // P, SEQ // 2
    RAW, RSP = 2, 4
    with Stage(core, name) as st:
        raw = [st.sb(f"raw{i}", [P, SEQ]) for i in range(RAW)]
        mix = [st.sb(f"mix{i}", [P, SEQ]) for i in range(3 * CH)]
        fwd = [st.sb("fwd_add", [P, 4, SEQ]), st.sb("fwd_sub", [P, 4, SEQ])]
        inv = [st.sb("inv_add", [P, NT, TH]), st.sb("inv_sub", [P, NT, TH])]
        spec = [st.sb(f"spec{i}", [P, 2, HY]) for i in range(RSP)]
        fs = [[st.sb(f"fold{s}{i}", [P, TH]) for s in "ad"] for i in range(2)]
        u = [st.sb("u_add", [P, 4, HY]), st.sb("u_sub", [P, 4, HY])]
        pq = [st.sb("p", [P, NT, HY]), st.sb("q", [P, NT, HY])]
        prod = [st.sb(f"prod{i}", [P, TH]) for i in range(4)]
        bsb, sm, df = st.sb("bsb", [P, TH]), prod[2], prod[3]
        ones = st.sb("ones", [P, 1])
        bank = st.banks(8)
        (table, lohi, folded, turned, u_ready, spectrum, multiplied, filtered, back, b_copied, used, y_done,
         squared, ssq, rooted, ones_set) = (st.sem(k) for k in (
             "table", "lohi", "folded", "turned", "u_ready", "spectrum", "multiplied", "filtered", "back",
             "b_copied", "used", "y_done", "squared", "ssq", "rooted", "ones"))
        w0, b0 = AT_A["hy_conv_w"], AT_A["hy_conv_b"]
        order = [0, 1, 2, 3, 4, 5, 6, 7, 8, 9, 10, 11]

        def half(tile, h):
            return tile[:, 0:TH] if h == 0 else tile[:, SEQ - 1:TH - 1:-1]

        with st.block() as block:
            @block.sync
            def _(sp):
                between = {3: ("t_fwd_add", fwd[0]), 4: ("t_fwd_sub", fwd[1]), 7: ("t_inv_add", inv[0]), 9: ("t_inv_sub", inv[1])}
                for i in order:
                    if i in between:
                        src, dst = between[i]
                        sp.dma_start(dst[:, :, :], io[src].rearrange("(j p) k -> p j k", p=P)).then_inc(table, 16)
                    if i >= RAW:
                        sp.wait_ge(used, i - RAW + 1)
                    sp.dma_start(raw[i % RAW][:, :], core.proj_t[i * P:(i + 1) * P, 0:SEQ]
                                 ).then_inc(core.load[i % RAW].sem, 16)

            @block.gpsimd
            def _(pool):
                nc.gpsimd.memset(ones[:, :], 1.0).then_inc(ones_set, 1)
                for o in range(2):
                    for c in range(CH):
                        n = o * CH + c
                        pool.wait_ge(lohi, n + 1)
                        if n >= 2:
                            pool.wait_ge(turned, 2 * (n - 1))
                        lo, hi = (half(mix[c], 0), half(mix[c], 1)) if o == 0 else (mix[c][:, 0:TH], mix[c][:, TH:SEQ])
                        nc.gpsimd.tensor_tensor(fs[n % 2][0][:, :], lo, hi, ALU.add)
                        nc.gpsimd.tensor_tensor(fs[n % 2][1][:, :], lo, hi, ALU.subtract).then_inc(folded, 1)
                    for f in range(NT):
                        n = o * NT + f
                        pool.wait_ge(multiplied, n + 1)
                        nc.gpsimd.tensor_tensor(pq[0][:, f, :], prod[0][:, :], prod[1][:, :], ALU.add)
                        nc.gpsimd.tensor_tensor(pq[1][:, f, :], prod[2][:, :], prod[3][:, :],
                                                ALU.subtract).then_inc(filtered, 1)

            @block.scalar
            def _(act):
                for o in range(2):
                    for c in range(CH):
                        for s in range(2):
                            n = 2 * (o * CH + c) + s
                            act.wait_ge(turned, n + 1)
                            nc.scalar.activation(u[s][:, :, c * P:(c + 1) * P],
                                                 bank[n % 2][:, :].rearrange("p (j c) -> p j c", c=P),
                                                 ACT.Copy).then_inc(u_ready, 1)
                        if o == 0 and c == 1:
                            for f in range(RSP):
                                act.dma_start(spec[f][:, :, :], core.spectra[0, :, f * P:(f + 1) * P, :].rearrange(
                                    "s p c -> p s c")).then_inc(core.load[4 + f].sem, 16)
                    for f in range(NT):
                        n = o * NT + f + RSP
                        if n < 2 * NT:
                            act.wait_ge(multiplied, n - RSP + 1)
                            act.dma_start(spec[n % RSP][:, :, :],
                                          core.spectra[n // NT, :, (n % NT) * P:(n % NT + 1) * P, :].rearrange("s p c -> p s c")
                                          ).then_inc(core.load[4 + n % RSP].sem, 16)
                    for c in range(CH):
                        n = o * CH + c
                        act.wait_ge(back, n + 1)
                        if n:
                            act.wait_ge(lohi if n <= CH else y_done, CH + n if n <= CH else n - CH)
                        nc.scalar.activation(bsb[:, :], bank[2 + 2 * (n % 3) + 1][:, :], ACT.Copy).then_inc(b_copied, 1)
                        if o:
                            act.wait_ge(y_done, c + 1)
                            core.act(act, nc.scalar.activation(mix[CH + c][:, :], mix[2 * CH + c][:, :], ACT.Square))
                            nc.scalar.activation(mix[c][:, :], mix[2 * CH + c][:, :], ACT.Copy,
                                                 scale=core.col_a[:, AT_A["hy_norm_g"] + c:AT_A["hy_norm_g"] + c + 1]
                                                 ).then_inc(squared, 1)
                            act.wait_ge(squared, c + 1)
                            act.dma_start(core.mix_t[c * P:(c + 1) * P, :], mix[c][:, :]).then_inc(core.hstore[c].sem, 16)
                act.wait_ge(ssq, 1)
                nc.scalar.activation(core.hy_rms[:, :], bank[0][:, 0:NT], ACT.Sqrt, bias=core.eps[:, 0:1],
                                     scale=1.0 / HY).then_inc(rooted, 1)
                for c in range(CH):
                    act.wait_ge(core.hstore[c].sem, core.hstore[c].at(1))

            @block.tensor
            def _(pe):
                for o in range(2):
                    for c in range(CH):
                        n = o * CH + c
                        pe.wait_ge(folded, n + 1)
                        for s in range(2):
                            if 2 * n + s >= 2:
                                pe.wait_ge(u_ready, 2 * n + s - 1)
                            for j in range(4):
                                last = nc.tensor.transpose(bank[s][:, j * P:(j + 1) * P],
                                                           fs[n % 2][s][:, j * P:(j + 1) * P], core.ident[:, :])
                            last.then_inc(turned, 1)
                    pe.wait_ge(u_ready, 2 * CH * (o + 1))
                    pe.wait_ge(table, 32)
                    for f in range(NT):
                        n = o * NT + f
                        if n >= 3:
                            pe.wait_ge(multiplied, n - 2)
                        if f < 3 and o:
                            pe.wait_ge(lohi, 2 * CH)
                        for s in range(2):
                            src = u[s] if f < NT // 2 else u[1 - s]
                            for j in range(4):
                                last = nc.tensor.matmul(bank[2 + 2 * (n % 3) + s][:, :], fwd[s][:, j, f * P:(f + 1) * P],
                                                        src[:, j, :], start=(j == 0), stop=(j == 3))
                        last.then_inc(spectrum, 1)
                    pe.wait_ge(filtered, NT * (o + 1))
                    pe.wait_ge(table, 64)
                    for c in range(CH):
                        n = o * CH + c
                        if c == 0:
                            pe.wait_ge(multiplied, NT * (o + 1))
                        if c == 3:
                            pe.wait_ge(lohi if o == 0 else y_done, CH + 1 if o == 0 else 1)
                        for s in range(2):
                            for i, f in enumerate(list(range(NT))):
                                even = f < NT // 2
                                k = s if even else 1 - s
                                last = nc.tensor.matmul(bank[2 + 2 * (n % 3) + s][:, :],
                                                        pq[k][:, f, c * P:(c + 1) * P], inv[k][:, f, :],
                                                        start=(i == 0), stop=(i == NT - 1))
                        last.then_inc(back, 1)
                pe.wait_ge(squared, CH)
                pe.wait_ge(ones_set, 1)
                for t in range(NT):
                    for c in range(CH):
                        last = nc.tensor.matmul(bank[0][:, t:t + 1], mix[CH + c][:, t * P:(t + 1) * P], ones[:, :],
                                                start=(c == 0), stop=(c == CH - 1))
                last.then_inc(ssq, 1)

            @block.vector
            def _(dve):
                step = lambda ins: core.dve(dve, ins)

                def short_conv(i):
                    dve.wait_ge(core.load[i % RAW].sem, core.load[i % RAW].at(i // RAW + 1))
                    w = [core.col_a[:, w0 + 12 * j + i:w0 + 12 * j + i + 1] for j in range(3)]
                    r = raw[i % RAW][:, :].rearrange("p (r c) -> p r c", c=GRID)
                    m = mix[i][:, :].rearrange("p (r c) -> p r c", c=GRID)
                    step(nc.vector.tensor_scalar(mix[i][:, :], raw[i % RAW][:, :], w[1], core.col_a[:, b0 + i:b0 + i + 1],
                                                 ALU.mult, ALU.add))
                    step(nc.vector.scalar_tensor_tensor(m[:, :, 1:GRID], r[:, :, 0:GRID - 1], w[0], m[:, :, 1:GRID],
                                                        ALU.mult, ALU.add))
                    return nc.vector.scalar_tensor_tensor(m[:, :, 0:GRID - 1], r[:, :, 1:GRID], w[2],
                                                          m[:, :, 0:GRID - 1], ALU.mult, ALU.add)

                for i in range(CH):
                    short_conv(i).then_inc(used, 1)
                    dve.wait_ge(used, i + 1)
                    dve.sem_inc(lohi, 1)
                for o in range(2):
                    for f in range(NT):
                        n = o * NT + f
                        dve.wait_ge(spectrum, n + 1)
                        dve.wait_ge(core.load[4 + n % RSP].sem, core.load[4 + n % RSP].at(n // RSP + 1))
                        if n:
                            dve.wait_ge(filtered, n)
                        p, q = bank[2 + 2 * (n % 3)][:, :], bank[2 + 2 * (n % 3) + 1][:, :]
                        c_, d_ = spec[n % RSP][:, 0, :], spec[n % RSP][:, 1, :]
                        nc.vector.tensor_tensor(prod[0][:, :], p, c_, ALU.mult)
                        nc.vector.tensor_tensor(prod[1][:, :], q, d_, ALU.mult)
                        nc.vector.tensor_tensor(prod[2][:, :], q, c_, ALU.mult)
                        nc.vector.tensor_tensor(prod[3][:, :], p, d_, ALU.mult).then_inc(multiplied, 1)
                        if o == 0:
                            short_conv(CH + f).then_inc(used, 1)
                            dve.wait_ge(used, CH + f + 1)
                    for c in range(CH):
                        n = o * CH + c
                        a = bank[2 + 2 * (n % 3)][:, :]
                        dve.wait_ge(b_copied, n + 1)
                        step(nc.vector.tensor_tensor(sm[:, :], a, bsb[:, :], ALU.add))
                        step(nc.vector.tensor_tensor(df[:, :], a, bsb[:, :], ALU.subtract))
                        x = mix[(o + 1) * CH + c]
                        if o == 0:
                            nc.vector.tensor_tensor(mix[c][:, 0:TH], sm[:, :], half(x, 0), ALU.mult)
                            nc.vector.tensor_tensor(mix[c][:, TH:SEQ], df[:, :], half(x, 1), ALU.mult).then_inc(lohi, 1)
                            dve.wait_ge(lohi, CH + c + 1)
                        else:
                            nc.vector.tensor_tensor(x[:, 0:TH], sm[:, :], half(x, 0), ALU.mult)
                            nc.vector.tensor_tensor(half(x, 1), df[:, :], half(x, 1), ALU.mult).then_inc(y_done, 1)
                            dve.wait_ge(y_done, c + 1)
                dve.wait_ge(rooted, 1)
                step(nc.vector.reciprocal(core.hy_rstd[:, :], core.hy_rms[:, :]))
        for j in range(RAW):
            core.load[j].close(3 * CH // RAW)
        for j in range(RSP):
            core.load[4 + j].close(2 * NT // RSP)
        for j in range(CH):
            core.hstore[j].close(1)


def stage_hgrn(core, name="hgrn"):
    nc, io = core.nc, core.io
    H, TL = HG_HEADS, NT + NC_
    ORDER = [[NT + c for c in range(NC_)] + list(range(NT)), [NT + c for c in reversed(range(NC_))] + list(reversed(range(NT)))]
    STEPS = TL - 1
    SB = 4
    NSB = -(-2 * STEPS // SB)
    WITH_TILE = [range(a, a + 1) if a < 3 else range(3, NSB) for a in range(NT // 2)]
    UT = NT // 2
    NP = 2 * LEVELS
    ON_DVE = range(LEVELS, LEVELS + 4)
    NB = 2
    with Stage(core, name) as st:
        z = [st.sb(f"z{d}", [P, TL * P]) for d in range(2)]
        gates, X = st.sb("gates", [P, TL, P + 1]), [st.sb(f"x{d}", [P, TL, P + 1]) for d in range(2)]
        carry = st.sb("carry", [P, TL, P + 1])
        k_ = [[st.sb(f"k{d}{i}", [P, TL, P]) for d in range(2)] for i in range(2)]
        ksum = [st.sb(f"ksum{i}", [P, NT, P]) for i in range(2)]
        q_ = [st.sb(f"q{i}", [P, NT, P]) for i in range(2)]
        qh = [[st.sb(f"qh{d}{i}", [P, NT, P]) for d in range(2)] for i in range(2)]
        kh = [st.sb(f"kh{d}", [P, TL, P]) for d in range(2)]
        dec = [[st.sb(f"dec{d}{i}", [P, TL]) for d in range(2)] for i in range(2)]
        S = [[st.sb(f"s{d}{i}", [P, NT, P]) for d in range(2)] for i in range(2)]
        s0 = st.sb("s0", [P, P])
        R = [st.sb(f"r{i}", [P, NP, UT, P]) for i in range(2)]
        kt = [st.sb(f"kt{i}", [P, SB, P]) for i in range(2)]
        masked = [st.sb(f"masked{i}", [P, 4, P]) for i in range(4)]
        ob = [st.sb(f"ob{i}", [P, P]) for i in range(4)]
        v = st.sb("v", [P, TL, BANK])
        mask = st.sb("mask", [P, 4 * NB, P])
        bank = st.banks(8)
        (inputs, zeroed, sig, qsilu, qscaled, fdone, gdone, xdone, ddk, ek, khd, turned, kts, ds, sdone, dd, ed,
         rd, prod, maskd, odone, ocopied) = (st.sem(x) for x in (
             "inputs", "zeroed", "sigmoid", "q_silu", "q_scaled", "f", "log_f", "x", "carry_exponent", "carry_exp",
             "carried", "turned", "kt", "ds", "state", "exponent", "exp", "level", "product", "masked", "o", "o_copied"))

        def blocks(ap, l):
            return ap.rearrange("p t (b r) -> p t b r", r=P >> l)

        def piece_of(j, u):
            side, l = divmod(j, LEVELS)
            return blocks(R[u % 2][:, j, :, :], l), P >> l + 1, side, l

        def running(d, l, u):
            t0, shift = (u % 2) * UT, 1 - d
            m = blocks(X[d][:, t0:t0 + UT, 0:P], l)[:, :, :, P >> l + 1:(P >> l + 1) + 1]
            return (blocks(X[d][:, t0:t0 + UT, shift:shift + P], l), m.to_broadcast([P, UT, 1 << l, P >> l + 1]))

        rdv = st.sem("level_dve")

        def batch(k):
            return range(SB * k, min(SB * k + SB, 2 * STEPS))

        with st.block() as block:
            @block.sync
            def _(sp):

                def load(h):
                    for d in range(2):
                        if h:
                            sp.wait_ge(xdone, 2 * (h - 1) + d + 1)
                        row = (16 + 4 * d + h) * P
                        sp.dma_start(z[d][:, :], core.proj_t[row:row + P, :]).then_inc(core.load[d].sem, 16)
                    if h >= 2:
                        sp.wait_ge(prod, NB * NT * (h - 1))
                        sp.wait_ge(khd, 2 * (h - 1))
                    row = (12 + h) * P
                    sp.dma_start(q_[h % 2][:, :, :], core.proj_t[row:row + P, 0:SEQ].rearrange("p (t c) -> p t c", c=P)
                                 ).then_inc(core.load[2 + h % 2].sem, 16)

                load(0)
                sp.dma_start(v[:, :, :], core.vg[:, 0:BANK].rearrange("(t p) c -> p t c", p=P)).then_inc(inputs, 16)
                sp.dma_start(mask[:, :, :], io["t_pair_masks"].rearrange("p (i t) -> p i t", t=P)).then_inc(inputs, 16)
                for h in range(H):
                    if h + 1 < H:
                        load(h + 1)
                    for t in range(NT):
                        n = h * NT + t
                        sp.wait_ge(ocopied, n + 1)
                        sp.dma_start(core.hg_o[t * P:(t + 1) * P, h * P:(h + 1) * P], ob[n % 4][:, :]
                                     ).then_inc(core.hstore[n % 4].sem, 16)
                for j in range(4):
                    sp.wait_ge(core.hstore[j].sem, core.hstore[j].at(H * NT // 4))

            @block.gpsimd
            def _(pool):
                nc.gpsimd.memset(gates[:, :, 0:1], 0.0)
                nc.gpsimd.memset(carry[:, :, :], 1.0).then_inc(zeroed, 1)
                pool.wait_ge(zeroed, 1)
                nc.gpsimd.memset(carry[:, :, 0:1], 0.0).then_inc(zeroed, 1)

                def prep(h):
                    for d in range(2):
                        pool.wait_ge(ek, 2 * h + d + 1)
                        nc.gpsimd.tensor_tensor(kh[d][:, :, :], kh[d][:, :, :], k_[h % 2][d][:, :, :], ALU.mult)
                        nc.gpsimd.tensor_tensor(qh[h % 2][d][:, :, :], qh[h % 2][d][:, :, :], q_[h % 2][:, :, :],
                                                ALU.mult).then_inc(khd, 1)

                def level(u, j):
                    pool.wait_ge(ed, u * NP + j + 1)
                    out, half, side, l = piece_of(j, u)
                    b, t0 = u // 2 % 2, u % 2 * UT
                    if side:
                        r = R[u % 2][:, j, :, :]
                        nc.gpsimd.tensor_tensor(r, r, q_[b][:, t0:t0 + UT, :], ALU.mult).then_inc(rd, 1)
                    else:
                        kf, kb = (blocks(k_[b][d][:, t0:t0 + UT, :], l) for d in range(2))
                        nc.gpsimd.tensor_tensor(out[:, :, :, 0:half], out[:, :, :, 0:half], kf[:, :, :, 0:half], ALU.mult)
                        nc.gpsimd.tensor_tensor(out[:, :, :, half:], out[:, :, :, half:], kb[:, :, :, half:],
                                                ALU.mult).then_inc(rd, 1)

                prep(0)
                for j in range(NP):
                    if j not in ON_DVE:
                        level(0, j)
                for u in range(2 * H):
                    h, second = divmod(u, 2)
                    if second and h + 1 < H:
                        prep(h + 1)
                    for j in range(NP if u + 1 < 2 * H else 0):
                        if j not in ON_DVE:
                            level(u + 1, j)

            @block.scalar
            def _(act):
                def prep(h):
                    for d in range(2):
                        act.wait_ge(core.load[d].sem, core.load[d].at(h + 1))
                        nc.scalar.activation(z[d][:, :], z[d][:, :], ACT.Sigmoid).then_inc(sig, 1)
                    act.wait_ge(core.load[2 + h % 2].sem, core.load[2 + h % 2].at(h // 2 + 1))
                    nc.scalar.activation(q_[h % 2][:, :, :], q_[h % 2][:, :, :], ACT.Silu).then_inc(qsilu, 1)
                    for d in range(2):
                        i = 2 * h + d
                        act.wait_ge(fdone, i + 1)
                        if i:
                            act.wait_ge(xdone, i)
                        else:
                            act.wait_ge(zeroed, 2)
                        nc.scalar.activation(gates[:, :, 1:P + 1], z[d][:, :].rearrange("p (t c) -> p t c", c=P),
                                             ACT.Ln).then_inc(gdone, 1)
                    for d in range(2):
                        i = 2 * h + d
                        act.wait_ge(ddk, i + 1)
                        x = X[d]
                        nc.scalar.activation(dec[h % 2][d][:, :], x[:, :, P], ACT.Exp)
                        if d == 0:
                            nc.scalar.activation(kh[d][:, :, :], kh[d][:, :, :], ACT.Exp)
                            nc.scalar.activation(qh[h % 2][d][:, :, :], x[:, 0:NT, 1:P + 1], ACT.Exp).then_inc(ek, 1)
                        else:
                            nc.scalar.activation(kh[d][:, :, :], x[:, :, 0:P], ACT.Exp)
                            nc.scalar.activation(qh[h % 2][d][:, :, :], qh[h % 2][d][:, :, :], ACT.Exp).then_inc(ek, 1)

                def level(u, j):
                    act.wait_ge(dd, u * NP + j + 1)
                    r = R[u % 2][:, j, :, :]
                    nc.scalar.activation(r, r, ACT.Exp).then_inc(ed, 1)

                def kt_copy(h, k):
                    n = h * NSB + k
                    m = len(batch(k))
                    act.wait_ge(turned, n + 1)
                    if n >= 2:
                        act.wait_ge(ds, n - 1)
                    nc.scalar.activation(kt[n % 2][:, 0:m, :], bank[4 + n % 2][:, 0:m * P].rearrange("p (s k) -> p s k", k=P),
                                         ACT.Copy).then_inc(kts, 1)

                def o_copy(h, t):
                    n = h * NT + t
                    act.wait_ge(odone, n + 1)
                    if n >= 4:
                        act.wait_ge(core.hstore[n % 4].sem, core.hstore[n % 4].at(n // 4))
                    nc.scalar.activation(ob[n % 4][:, :], bank[3][:, 0:P], ACT.Copy).then_inc(ocopied, 1)

                prep(0)
                for k in range(NSB):
                    kt_copy(0, k)
                for j in range(NP):
                    level(0, j)
                for u in range(2 * H):
                    h, second = divmod(u, 2)
                    if second and h + 1 < H:
                        prep(h + 1)
                    for a in range(UT):
                        if second and h + 1 < H:
                            kt_copy(h + 1, WITH_TILE[a][0])
                        if u + 1 < 2 * H:
                            for b in range(4):
                                if 4 * a + b < NP:
                                    level(u + 1, 4 * a + b)
                        if second and h + 1 < H:
                            for k in WITH_TILE[a][1:]:
                                kt_copy(h + 1, k)
                        if a:
                            o_copy(h, second * UT + a - 1)
                    o_copy(h, second * UT + UT - 1)

            @block.tensor
            def _(pe):
                def turn(h, k):
                    n = h * NSB + k
                    pe.wait_ge(khd, 2 * h + batch(k)[-1] // STEPS + 1)
                    if n >= 2:
                        pe.wait_ge(kts, n - 1)
                    for j, s in enumerate(batch(k)):
                        d, i = divmod(s, STEPS)
                        last = nc.tensor.transpose(bank[4 + n % 2][:, j * P:(j + 1) * P], kh[d][:, ORDER[d][i], :],
                                                   core.ident[:, :])
                    last.then_inc(turned, 1)

                def state(h, k):
                    n = h * NSB + k
                    pe.wait_ge(kts, n + 1)
                    if n >= 2:
                        h0, k0 = divmod(n - 2, NSB)
                        pe.wait_ge(sdone, h0 * 2 * STEPS + batch(k0)[-1] + 1)
                    for j, s in enumerate(batch(k)):
                        d, i = divmod(s, STEPS)
                        last = nc.tensor.matmul(bank[6 + n % 2][:, j * P:(j + 1) * P], kt[n % 2][:, j, :],
                                                v[:, ORDER[d][i], h * P:(h + 1) * P], start=True, stop=True)
                    last.then_inc(ds, 1)

                def out(h, t):
                    n = h * NT + t
                    if n:
                        pe.wait_ge(ocopied, n)
                    o = bank[3][:, 0:P]
                    for b in range(NB):
                        m = NB * n + b
                        pe.wait_ge(maskd, m + 1)
                        for i in range(4):
                            nc.tensor.matmul(o, masked[m % 4][:, i, :], v[:, t, h * P:(h + 1) * P],
                                             start=(b + i == 0), stop=False)
                    if t == 0:
                        pe.wait_ge(sdone, 2 * STEPS * (h + 1))
                    for d in range(2):
                        last = nc.tensor.matmul(o, qh[h % 2][d][:, t, :], S[h % 2][d][:, t, :], start=False, stop=(d == 1))
                    last.then_inc(odone, 1)

                pe.wait_ge(inputs, 32)
                turn(0, 0)
                for k in range(NSB):
                    if k + 1 < NSB:
                        turn(0, k + 1)
                    state(0, k)
                for u in range(2 * H):
                    h, second = divmod(u, 2)
                    pe.wait_ge(rd, (NP - len(ON_DVE)) * (u + 1))
                    pe.wait_ge(rdv, len(ON_DVE) * (u + 1))
                    for a in range(UT):
                        t = second * UT + a
                        if second and h + 1 < H:
                            turn(h + 1, WITH_TILE[a][0])
                        for b in range(NB):
                            m = NB * (h * NT + t) + b
                            if m >= 3:
                                pe.wait_ge(maskd, m - 2)
                            for i in range(4):
                                l = 4 * b + i
                                if l < LEVELS:
                                    lhs, rhs = R[u % 2][:, l, a, :], R[u % 2][:, LEVELS + l, a, :]
                                else:
                                    lhs, rhs = ksum[h % 2][:, t, :], q_[h % 2][:, t, :]
                                last = nc.tensor.matmul(bank[m % 3][:, i * P:(i + 1) * P], lhs, rhs, start=True, stop=True)
                            last.then_inc(prod, 1)
                            if b == 0 and a:
                                out(h, t - 1)
                        if second and h + 1 < H:
                            state(h + 1, WITH_TILE[a][0])
                            for k in WITH_TILE[a][1:]:
                                turn(h + 1, k)
                                state(h + 1, k)
                    out(h, second * UT + UT - 1)

            @block.vector
            def _(dve):
                step = lambda ins: core.dve(dve, ins)

                def prep(h):
                    b = h % 2
                    if h >= 2:
                        dve.wait_ge(prod, NB * NT * (h - 1))
                        dve.wait_ge(odone, NT * (h - 1))
                    for d in range(2):
                        dve.wait_ge(sig, 2 * h + d + 1)
                        c = d * 4 + h
                        nc.vector.tensor_scalar(z[d][:, :], z[d][:, :], core.lb[:, 1, c:c + 1], core.lb[:, 0, c:c + 1],
                                                ALU.mult, ALU.add).then_inc(fdone, 1)
                    dve.wait_ge(qsilu, h + 1)
                    nc.vector.tensor_scalar(q_[b][:, :, :], q_[b][:, :, :], float(P) ** -0.5, None,
                                            ALU.mult).then_inc(qscaled, 1)
                    for d in range(2):
                        i = 2 * h + d
                        dve.wait_ge(fdone, i + 1)
                        step(nc.vector.tensor_scalar(k_[b][d][:, :, :], z[d][:, :].rearrange("p (t c) -> p t c", c=P),
                                                     -1.0, 1.0, ALU.mult, ALU.add))
                        if d:
                            step(nc.vector.tensor_tensor(ksum[b][:, :, :], k_[b][0][:, 0:NT, :], k_[b][1][:, 0:NT, :], ALU.add))
                        dve.wait_ge(gdone, i + 1)
                        if i < 1:
                            dve.wait_ge(zeroed, 2)
                        if h:
                            dve.wait_ge(ek, i - 1)
                        nc.vector.tensor_tensor_scan(X[d][:, :, :].rearrange("p t c -> p (t c)"),
                                                     carry[:, :, :].rearrange("p t c -> p (t c)"),
                                                     gates[:, :, :].rearrange("p t c -> p (t c)"),
                                                     0.0, ALU.mult, ALU.add).then_inc(xdone, 1)
                        dve.wait_ge(xdone, i + 1)
                        if h:
                            dve.wait_ge(turned, NSB * (h - 1) + (STEPS - 1) // SB + 1 if d == 0 else NSB * h)
                        last = X[d][:, :, P:P + 1]
                        if d == 0:
                            nc.vector.tensor_tensor(kh[d][:, :, :], last.to_broadcast([P, TL, P]), X[d][:, :, 1:P + 1],
                                                    ALU.subtract).then_inc(ddk, 1)
                        else:
                            nc.vector.tensor_tensor(qh[b][d][:, :, :], last[:, 0:NT, :].to_broadcast([P, NT, P]),
                                                    X[d][:, 0:NT, 0:P], ALU.subtract).then_inc(ddk, 1)

                def level(u, j):
                    if u >= 2 and j == 0:
                        dve.wait_ge(prod, NB * UT * (u - 1))
                    out, half, side, l = piece_of(j, u)
                    (xl, ml), (xr, mr) = running(side, l, u), running(1 - side, l, u)
                    nc.vector.tensor_tensor(out[:, :, :, 0:half], ml, xl[:, :, :, 0:half], ALU.subtract)
                    nc.vector.tensor_tensor(out[:, :, :, half:], xr[:, :, :, half:], mr, ALU.subtract).then_inc(dd, 1)

                    if j - 2 in ON_DVE:
                        dve.wait_ge(ed, u * NP + j - 1)
                        t0 = u % 2 * UT
                        piece = R[u % 2][:, j - 2, :, :]
                        nc.vector.tensor_tensor(piece, piece, q_[u // 2 % 2][:, t0:t0 + UT, :], ALU.mult).then_inc(rdv, 1)

                def carry_state(h, k):
                    n = h * NSB + k
                    dve.wait_ge(ds, n + 1)
                    for j, s in enumerate(batch(k)):
                        d, i = divmod(s, STEPS)
                        new = bank[6 + n % 2][:, j * P:(j + 1) * P]
                        to = s0[:, :] if i == 0 else S[h % 2][d][:, ORDER[d][i + 1], :]
                        if i == 0:
                            ins = nc.vector.tensor_copy(to, new)
                        else:
                            was = s0[:, :] if i == 1 else S[h % 2][d][:, ORDER[d][i], :]
                            t = ORDER[d][i]
                            ins = nc.vector.scalar_tensor_tensor(to, was, dec[h % 2][d][:, t:t + 1], new, ALU.mult, ALU.add)
                        ins.then_inc(sdone, 1)
                        dve.wait_ge(sdone, 2 * STEPS * h + s + 1)

                prep(0)
                for k in range(NSB):
                    carry_state(0, k)
                for j in range(NP):
                    level(0, j)
                dve.wait_ge(inputs, 32)
                for u in range(2 * H):
                    h, second = divmod(u, 2)
                    if second and h + 1 < H:
                        prep(h + 1)
                    for a in range(UT):
                        t = second * UT + a
                        for b in range(NB):
                            n = h * NT + t
                            m = NB * n + b
                            dve.wait_ge(prod, m + 1)
                            if n >= 2:
                                dve.wait_ge(odone, n - 1)
                            nc.vector.tensor_tensor(masked[m % 4][:, :, :], bank[m % 3][:, :].rearrange("p (i t) -> p i t", t=P),
                                                    mask[:, 4 * b:4 * b + 4, :], ALU.mult).then_inc(maskd, 1)
                            for j in range(4 * a + 2 * b, 4 * a + 2 * b + 2):
                                if u + 1 < 2 * H and j < NP:
                                    level(u + 1, j)
                        if second and h + 1 < H:
                            for k in WITH_TILE[a]:
                                carry_state(h + 1, k)
        for j in range(2):
            core.load[j].close(H)
            core.load[2 + j].close(H // 2)
        for j in range(4):
            core.hstore[j].close(H * NT // 4)


def stage_mix_out(core, name="mixout"):
    nc, io = core.nc, core.io
    H = HG_HEADS
    WP = 4
    RY = 3
    with Stage(core, name) as st:
        o = [st.sb(f"o{i}", [P, H, P]) for i in range(2)]
        g = [st.sb(f"g{i}", [P, BANK]) for i in range(2)]
        og = [st.sb(f"og{i}", [P, H, P]) for i in range(2)]
        junk = st.sb("junk", [P, P])
        ss, rms = st.sb("ss", [P, NT, H]), st.sb("rms", [P, NT, H])
        yT = st.sb("yT", [P, KD, SEQ])
        y = [Parts(st, f"y{i}", [P, KD, P]) for i in range(RY)]
        raw = [st.sb(f"raw{i}", [P, KD // WP, D]) for i in range(2)]
        w = Parts(st, "w", [P, KD, D])
        gate = st.sb("gate", [P, D])
        x = [st.sb(f"x{i}", [P, D]) for i in range(3)]
        out = [st.sb(f"out{i}", [P, BANK]) for i in range(4)]
        bank = st.banks(8)
        hyena, gain, rooted, silu, gated, turned, placed, done, added, w_high, w_low, y_high, y_low = (
            st.sem(k) for k in ("hyena", "gain", "rooted", "silu", "gated", "turned", "placed", "product", "added",
                                "w_high", "w_low", "y_high", "y_low"))
        with st.block() as block:
            @block.sync
            def _(sp):
                def tile(t):
                    if t >= 2:
                        sp.wait_ge(gated, t - 1)
                    sp.dma_start(o[t % 2][:, :, :], core.hg_o[t * P:(t + 1) * P, :].rearrange("p (h c) -> p h c", c=P)
                                 ).then_inc(core.load[t % 2].sem, 16)
                    sp.dma_start(g[t % 2][:, :], core.vg[t * P:(t + 1) * P, BANK:2 * BANK]
                                 ).then_inc(core.load[2 + t % 2].sem, 16)

                tile(0)
                tile(1)
                for p in range(WP):
                    if p == 2:
                        sp.dma_start(yT[:, 0:4, :], core.mix_t[0:HY, :].rearrange("(k p) t -> p k t", p=P)).then_inc(hyena, 16)
                    if p >= 2:
                        sp.wait_ge(w_low, p - 1)
                    sp.dma_start(raw[p % 2][:, :, :], io["w_out"][0][p * D // WP:(p + 1) * D // WP, :].rearrange(
                        "(k p) n -> p k n", p=P)).then_inc(core.load[7 + p % 2].sem, 16)
                sp.dma_start(gate[:, :], core.mod_rows[0][0, 2 * D:3 * D].partition_broadcast(P)).then_inc(gain, 16)
                for t in range(NT):
                    if t >= 2:
                        tile(t)
                    if t >= 3:
                        sp.wait_ge(added, 2 * (t - 2))
                    sp.dma_start(x[t % 3][:, :], io["x"][0][t * P:(t + 1) * P, :]).then_inc(core.load[4 + t % 3].sem, 16)

            def w_piece(p):
                c = slice(p * KD // WP, (p + 1) * KD // WP)
                return raw[p % 2][:, :, :], w.high[:, c, :], w.low[:, c, :]

            @block.scalar
            def _(act):
                def head(t):
                    act.wait_ge(core.load[t % 2].sem, core.load[t % 2].at(t // 2 + 1))
                    for h in range(H):
                        core.act(act, nc.scalar.activation(junk[:, :], o[t % 2][:, h, :], ACT.Square,
                                                           accum_out=ss[:, t, h:h + 1]))
                    nc.scalar.activation(rms[:, t, :], ss[:, t, :], ACT.Sqrt, bias=core.eps[:, 0:1],
                                         scale=1.0 / P).then_inc(rooted, 1)
                    act.wait_ge(core.load[2 + t % 2].sem, core.load[2 + t % 2].at(t // 2 + 1))
                    nc.scalar.activation(g[t % 2][:, :], g[t % 2][:, :], ACT.Silu).then_inc(silu, 1)

                def place(t):
                    act.wait_ge(turned, t + 1)
                    nc.scalar.activation(yT[:, 4:8, t * P:(t + 1) * P],
                                         bank[t % 2][:, :].rearrange("p (k t) -> p k t", t=P), ACT.Copy,
                                         scale=core.col_a[:, AT_A["hg_norm_g"]:AT_A["hg_norm_g"] + 1]).then_inc(placed, 1)
                    act.wait_ge(placed, t + 1)
                    act.wait_ge(hyena, 16)
                    if t >= RY:
                        act.wait_ge(done, 2 * (t - RY + 1))
                    nc.scalar.activation(y[t % RY].high[:, :, :], yT[:, :, t * P:(t + 1) * P], ACT.Copy).then_inc(y_high, 1)

                head(0)
                for p in range(WP):
                    act.wait_ge(core.load[7 + p % 2].sem, core.load[7 + p % 2].at(p // 2 + 1))
                    raw_, hi, _ = w_piece(p)
                    nc.scalar.activation(hi, raw_, ACT.Copy).then_inc(w_high, 1)
                    if p == 1:
                        head(1)
                place(0)
                for t in range(1, NT):
                    if t + 1 < NT:
                        head(t + 1)
                    place(t)

            @block.tensor
            def _(pe):
                def turn(t):
                    pe.wait_ge(gated, t + 1)
                    if t >= 2:
                        pe.wait_ge(placed, t - 1)
                    for h in range(H):
                        last = nc.tensor.transpose(bank[t % 2][:, h * P:(h + 1) * P], og[t % 2][:, h, :], core.ident[:, :])
                    last.then_inc(turned, 1)

                turn(0)
                for t in range(NT):
                    if t + 1 < NT:
                        turn(t + 1)
                    pe.wait_ge(y_low, t + 1)
                    for half in range(2):
                        n = 2 * t + half
                        if n >= 3:
                            pe.wait_ge(added, n - 2)
                        for k in range(KD):
                            if n == 0 and k % (KD // WP) == 0:
                                pe.wait_ge(w_low, k // (KD // WP) + 1)
                            part = k // 4
                            last = product(nc, bank[2 + 2 * (n % 3) + part][:, :], y[t % RY][:, k, :],
                                           w[:, k, half * BANK:(half + 1) * BANK], k % 4 == 0, k % 4 == 3)
                        last.then_inc(done, 1)

            @block.vector
            def _(dve):
                step = lambda ins: core.dve(dve, ins)

                def gated_output(t):
                    dve.wait_ge(rooted, t + 1)
                    step(nc.vector.reciprocal(rms[:, t, :], rms[:, t, :]))
                    if t >= 2:
                        dve.wait_ge(turned, t - 1)
                    step(nc.vector.tensor_tensor(og[t % 2][:, :, :], o[t % 2][:, :, :],
                                                 rms[:, t, :].unsqueeze(2).to_broadcast([P, H, P]), ALU.mult))
                    dve.wait_ge(silu, t + 1)
                    nc.vector.tensor_tensor(og[t % 2][:, :, :], og[t % 2][:, :, :],
                                            g[t % 2][:, :].rearrange("p (h c) -> p h c", c=P), ALU.mult).then_inc(gated, 1)

                def results(t):
                    dve.wait_ge(core.load[4 + t % 3].sem, core.load[4 + t % 3].at(t // 3 + 1))
                    for half in range(2):
                        n = 2 * t + half
                        c = slice(half * BANK, (half + 1) * BANK)
                        dve.wait_ge(done, n + 1)
                        if n >= 4:
                            dve.wait_ge(core.store[n % 4].sem, core.store[n % 4].at(n // 4))
                        r = out[n % 4][:, :]
                        a, b = bank[2 + 2 * (n % 3)][:, :], bank[3 + 2 * (n % 3)][:, :]
                        step(nc.vector.tensor_scalar(r, a, core.hy_rstd[:, t:t + 1], None, ALU.mult))
                        step(nc.vector.tensor_tensor(r, r, b, ALU.add))
                        step(nc.vector.tensor_tensor(r, r, gate[:, c], ALU.mult))
                        nc.vector.tensor_tensor(r, r, x[t % 3][:, c], ALU.add).then_inc(added, 1)

                gated_output(0)
                for p in range(WP):
                    dve.wait_ge(w_high, p + 1)
                    raw_, hi, lo = w_piece(p)
                    nc.vector.tensor_tensor(lo, raw_, hi.bitcast(F32), ALU.subtract).then_inc(w_low, 1)
                    if p == 1:
                        gated_output(1)
                dve.wait_ge(gain, 16)
                for t in range(NT):
                    if t + 2 < NT:
                        gated_output(t + 2)
                    results(t)

            @block.gpsimd
            def _(pool):
                def low(t):
                    pool.wait_ge(y_high, t + 1)
                    nc.gpsimd.tensor_tensor(y[t % RY].low[:, :, :], yT[:, :, t * P:(t + 1) * P],
                                            y[t % RY].high[:, :, :].bitcast(F32), ALU.subtract).then_inc(y_low, 1)

                low(0)
                for t in range(NT):
                    if t + 1 < NT:
                        low(t + 1)
                    for half in range(2):
                        n = 2 * t + half
                        pool.wait_ge(added, n + 1)
                        pool.dma_start(core.x1[t * P:(t + 1) * P, half * BANK:(half + 1) * BANK], out[n % 4][:, :]
                                       ).then_inc(core.store[n % 4].sem, 16)
                for j in range(4):
                    pool.wait_ge(core.store[j].sem, core.store[j].at(NT // 2))
        for j in range(2):
            core.load[j].close(NT // 2)
            core.load[2 + j].close(NT // 2)
            core.load[7 + j].close(WP // 2)
        for j in range(3):
            core.load[4 + j].close(len(range(j, NT, 3)))
        for j in range(4):
            core.store[j].close(NT // 2)


FG = FF // BANK
UNITS = 3 * FG


def load_piece(core, sp, raw, n):
    e, i = divmod(n, UNITS)
    if i < 2 * FG:
        w = core.io["exp_w1" if i % 2 == 0 else "exp_w3"][0][e]
        src, cols = w[:, (i // 2) * BANK:(i // 2 + 1) * BANK], BANK
    else:
        q = i - 2 * FG
        src, cols = core.io["exp_w2"][0][e][q * BANK:(q + 1) * BANK, :], D
    sp.dma_start(raw[n % len(raw)][:, :].rearrange("p (k n) -> p k n", n=cols), src.rearrange("(k p) n -> p k n", p=P)
                 ).then_inc(core.load[n % len(raw)].sem, 16)


def stage_router(core, hT, raw, name="router"):
    nc, io = core.nc, core.io
    ROUNDS = CAP // 8
    with Stage(core, name) as st:
        rw = st.sb("rw", [P, KD, E])
        iota, tokid = st.sb("iota", [P, P]), st.sb("tokid", [P, NT, 2])
        aff, mx, sm = st.sb("aff", [P, NT, E]), st.sb("mx", [P, NT]), st.sb("sm", [P, NT])
        tv = st.sb("tv", [P, NT, E, 6], BF16)
        rest = [st.sb(f"rest{i}", [P, NT, E]) for i in range(2)]
        logit_rows = st.sb("logit_rows", [E, SEQ])
        part_sum = st.sb("part_sum", [P, E, 2])
        work, best = st.sb("work", [E, SEQ]), st.sb("best", [E, 8])
        mask, one, rank = st.sb("mask", [E, SEQ]), st.sb("one", [E, SEQ]), st.sb("rank", [E, SEQ])
        slot = st.sb("slot", [P, NT, E])
        hot = [st.sb(f"hot{i}", [P, NT, P], BF16) for i in range(2)]
        bank = st.banks(7)
        split = st.sem("split")
        rows_done, inputs, logits, less, exps, ready, turned, ranked, unturned, onehot, picked, ones_set = (st.sem(k) for k in (
            "rows", "inputs", "logits", "less", "exps", "ready", "turned", "ranked", "unturned", "onehot", "picked", "ones"))
        with st.block() as block:
            @block.sync
            def _(sp):
                with nc.allow_non_contiguous_dma(reason="64-byte rows"):
                    sp.dma_start(rw[:, :, :], io["router_w"][0].rearrange("(k p) e -> p k e", p=P)).then_inc(inputs, 16)
                sp.dma_start(iota[:, :], io["t_iota"][:, 0:P]).then_inc(inputs, 16)
                sp.dma_start(tokid[:, :, :], io["t_tokid"].rearrange("p (t v) -> p t v", v=2)).then_inc(inputs, 16)
                for n in range(len(raw)):
                    load_piece(core, sp, raw, n)

            @block.gpsimd
            def _(pool):
                nc.gpsimd.memset(one[:, :], 1.0).then_inc(ones_set, 1)
                core.pool(pool, nc.gpsimd.memset(tv[:, :, :, :], 0.0))
                pool.wait_ge(inputs, 48)
                for v in range(2):
                    core.pool(pool, nc.gpsimd.tensor_copy(tv[:, :, :, v], tokid[:, :, v:v + 1].to_broadcast([P, NT, E])))
                pool.wait_ge(ready, 1)
                left = aff
                for v in range(3):
                    core.pool(pool, nc.gpsimd.tensor_copy(tv[:, :, :, 2 + v], left[:, :, :]))
                    if v < 2:
                        core.pool(pool, nc.gpsimd.tensor_tensor(rest[v][:, :, :], left[:, :, :], tv[:, :, :, 2 + v], ALU.subtract))
                        left = rest[v]
                pool.sem_inc(split, 1)

            @block.tensor
            def _(pe):
                pe.wait_ge(inputs, 48)
                for c in range(2):
                    for k in range(KD):
                        last = nc.tensor.matmul(bank[5 + c][0:E, :], rw[:, k, :], hT[:, k, c * BANK:(c + 1) * BANK],
                                                start=(k == 0), stop=(k == KD - 1))
                    last.then_inc(logits, 1)
                for t in range(NT):
                    pe.wait_ge(rows_done, t // 4 + 1)
                    last = nc.tensor.transpose(bank[0][:, t * E:(t + 1) * E], logit_rows[:, t * P:(t + 1) * P],
                                               core.ident[0:E, 0:E])
                last.then_inc(logits, 1)
                pe.wait_ge(ready, 1)
                for t in range(NT):
                    last = nc.tensor.transpose(bank[1 + t // 4][0:E, (t % 4) * P:(t % 4 + 1) * P], aff[:, t, :], core.ident[:, :])
                last.then_inc(turned, 1)
                pe.wait_ge(ranked, 1)
                pe.wait_ge(split, 1)
                for t in range(NT):
                    last = nc.tensor.transpose(bank[3][:, t * E:(t + 1) * E], rank[:, t * P:(t + 1) * P], core.ident[0:E, 0:E])
                last.then_inc(unturned, 1)
                for e in range(E):
                    pe.wait_ge(onehot, e + 1)
                    for t in range(NT):
                        last = nc.tensor.matmul(bank[4][:, 6 * e:6 * e + 6], hot[e % 2][:, t, :], tv[:, t, e, :],
                                                start=(t == 0), stop=(t == NT - 1))
                    last.then_inc(picked, 1)

            @block.scalar
            def _(act):
                for c in range(2):
                    act.wait_ge(logits, c + 1)
                    nc.scalar.activation(logit_rows[:, c * BANK:(c + 1) * BANK], bank[5 + c][0:E, :], ACT.Copy).then_inc(rows_done, 1)
                act.wait_ge(less, 1)
                nc.scalar.activation(aff[:, :, :], aff[:, :, :], ACT.Exp).then_inc(exps, 1)

            @block.vector
            def _(dve):
                step = lambda ins: core.dve(dve, ins)
                dve.wait_ge(logits, 3)
                lg = bank[0][:, 0:NT * E].rearrange("p (t e) -> p t e", e=E)
                step(nc.vector.tensor_reduce(mx[:, :], lg, AX, ALU.max))
                nc.vector.tensor_tensor(aff[:, :, :], lg, mx[:, :].unsqueeze(2).to_broadcast([P, NT, E]),
                                        ALU.subtract).then_inc(less, 1)
                dve.wait_ge(exps, 1)
                step(nc.vector.tensor_reduce(sm[:, :], aff[:, :, :], AX, ALU.add))
                step(nc.vector.reciprocal(sm[:, :], sm[:, :]))
                nc.vector.tensor_tensor(aff[:, :, :], aff[:, :, :], sm[:, :].unsqueeze(2).to_broadcast([P, NT, E]),
                                        ALU.mult).then_inc(ready, 1)
                dve.wait_ge(inputs, 48)
                dve.wait_ge(ready, 1)
                dve.wait_ge(turned, 1)
                for h in range(2):
                    step(nc.vector.tensor_copy(work[:, h * BANK:(h + 1) * BANK], bank[1 + h][0:E, :]))
                for _r in range(ROUNDS):
                    step(nc.vector.max(best[:, :], work[:, :]))
                    step(nc.vector.match_replace(work[:, :], best[:, :], work[:, :], -1.0))
                step(nc.vector.tensor_scalar(mask[:, :], work[:, :], 0.0, None, ALU.is_lt))
                dve.wait_ge(ones_set, 1)
                step(nc.vector.tensor_tensor_scan(rank[:, :], one[:, :], mask[:, :], 0.0, ALU.mult, ALU.add))
                step(nc.vector.tensor_tensor(rank[:, :], rank[:, :], mask[:, :], ALU.mult))
                nc.vector.tensor_scalar(rank[:, :], rank[:, :], 1.0, None, ALU.subtract).then_inc(ranked, 1)
                dve.wait_ge(unturned, 1)
                step(nc.vector.tensor_copy(slot[:, :, :], bank[3][:, 0:NT * E].rearrange("p (t e) -> p t e", e=E)))
                for e in range(E):
                    if e >= 2:
                        dve.wait_ge(picked, e - 1)
                    nc.vector.tensor_tensor(hot[e % 2][:, :, :], iota[:, :].unsqueeze(1).to_broadcast([P, NT, P]),
                                            slot[:, :, e:e + 1].to_broadcast([P, NT, P]), ALU.is_equal).then_inc(onehot, 1)
                dve.wait_ge(picked, E)
                sel = bank[4][:, 0:6 * E].rearrange("p (e v) -> p e v", v=6)
                step(nc.vector.tensor_reduce(part_sum[:, :, 0], sel[:, :, 0:2], AX, ALU.add))
                step(nc.vector.tensor_reduce(part_sum[:, :, 1], sel[:, :, 2:5], AX, ALU.add))
                step(nc.vector.tensor_copy(core.moe_idx[:, :], part_sum[:, :, 0]))
                step(nc.vector.tensor_copy(core.moe_gate[:, :], part_sum[:, :, 1]))


def stage_moe(core, raw, name="moe"):
    nc, io = core.nc, core.io
    RW, RP = len(raw), 3
    with Stage(core, name) as st:
        w = [Parts(st, f"w{i}", [P, KD * BANK]) for i in range(RP)]
        xg = [st.sb(f"xg{i}", [P, D]) for i in range(2)]
        xw, xgT = st.sb("xw", [P, KD, P]), Parts(st, "xgT", [P, KD, P])
        sa = [st.sb(f"sa{i}", [P, BANK]) for i in range(2)]
        hid = [st.sb(f"hid{i}", [P, BANK]) for i in range(2)]
        hidT = Parts(st, "hidT", [P, FF // P, P])
        yo = [st.sb(f"yo{i}", [P, D]) for i in range(2)]
        g2 = st.sb("g2", [P, D])
        bank = st.banks(8)
        gathered, scattered = st.dma_sem("gathered"), st.dma_sem("scattered")
        (high, low, xwhole, gain, w_used, xturn, xplaced, silu, hidden, hturn, hhigh, hplaced, yout) = (
            st.sem(k) for k in ("high", "low", "x_whole", "gain", "w_used", "x_turned", "x_placed", "silu", "hidden",
                                "h_turned", "h_high", "h_placed", "y_out"))
        sc, sh = core.sc[2], core.mod1[:, 24:32, 0]

        def w_view(n, cols, k, c0, c1):
            return w[n % RP][:, k * cols + c0:k * cols + c1]

        with st.block() as block:
            @block.sync
            def _(sp):
                sp.dma_start(g2[:, :], core.mod_rows[0][0, 5 * D:6 * D].partition_broadcast(P)).then_inc(gain, 16)
                for n in range(RW, E * UNITS):
                    sp.wait_ge(low, 2 * (n - RW + 1))
                    load_piece(core, sp, raw, n)

            @block.gpsimd
            def _(pool):
                def gather(e):
                    if e >= 2:
                        pool.wait_ge(xturn, 2 * (e - 1))
                    pool.indirect_dma_start(out=xg[e % 2][:, :], out_offset=None, in_=core.xn2,
                                            in_offset=bass.IndirectOffsetOnAxis(ap=core.moe_idx[:, e:e + 1], axis=0)
                                            ).then_inc(gathered, 16)

                def split_x(e):
                    for half in range(2):
                        pool.wait_ge(xwhole, 2 * e + half + 1)
                        c = slice(4 * half, 4 * half + 4)
                        core.pool(pool, nc.gpsimd.tensor_copy(xgT.high[:, c, :], xw[:, c, :]))
                        nc.gpsimd.tensor_tensor(xgT.low[:, c, :], xw[:, c, :], xgT.high[:, c, :].bitcast(F32),
                                                ALU.subtract).then_inc(xplaced, 1)

                def scatter(e):
                    pool.wait_ge(yout, 2 * (e + 1))
                    if e:
                        pool.wait_ge(scattered, 16 * e)
                    pool.indirect_dma_start(out=core.x1, out_offset=bass.IndirectOffsetOnAxis(
                        ap=core.moe_idx[:, e:e + 1], axis=0), in_=yo[e % 2][:, :], in_offset=None,
                        compute_op=ALU.add).then_inc(scattered, 16)

                gather(0)
                split_x(0)
                for e in range(E):
                    if e + 1 < E:
                        pool.wait_ge(gathered, 16 * (e + 1))
                        gather(e + 1)
                    if e:
                        scatter(e - 1)
                    if e + 1 < E:
                        split_x(e + 1)
                scatter(E - 1)
                pool.wait_ge(scattered, 16 * E)

            @block.tensor
            def _(pe):
                def turn_x(e):
                    pe.wait_ge(gathered, 16 * (e + 1))
                    for half in range(2):
                        if e:
                            pe.wait_ge(hplaced, FG * (e - 1) + 3 + half)
                        for k in range(4):
                            c = (4 * half + k) * P
                            last = nc.tensor.transpose(bank[4 + half][:, k * P:(k + 1) * P], xg[e % 2][:, c:c + P],
                                                       core.ident[:, :])
                        last.then_inc(xturn, 1)

                def up_group(e, f):
                    n = e * FG + f
                    if n >= 2:
                        pe.wait_ge(hidden, n - 1)
                    for s in range(2):
                        u = e * UNITS + 2 * f + s
                        for k in range(KD):
                            if k % (KD // 2) == 0:
                                pe.wait_ge(low, 2 * u + k // (KD // 2) + 1)
                            last = product(nc, bank[2 * (n % 2) + s][:, :], xgT[:, k, :],
                                           w_view(u, BANK, k, 0, BANK), k == 0, k == KD - 1)
                        last.then_inc(w_used, 1)

                def turn_h(e, f):
                    n = e * FG + f
                    pe.wait_ge(hidden, n + 1)
                    if n >= 2:
                        pe.wait_ge(hplaced, n - 1)
                    pe.wait_ge(xwhole, 2 * (e + 1))
                    for k in range(4):
                        last = nc.tensor.transpose(bank[4 + n % 2][:, k * P:(k + 1) * P], hid[n % 2][:, k * P:(k + 1) * P],
                                                   core.ident[:, :])
                    last.then_inc(hturn, 1)

                def down(e, q):
                    u = e * UNITS + 2 * FG + q
                    if e and q == 0:
                        pe.wait_ge(yout, 2 * e)
                    pe.wait_ge(hplaced, e * FG + q + 1)
                    for kk in range(4):
                        if kk % 2 == 0:
                            pe.wait_ge(low, 2 * u + kk // 2 + 1)
                        k = 4 * q + kk
                        for half in range(2):
                            last = product(nc, bank[6 + half][:, :], hidT[:, k, :],
                                           w_view(u, D, kk, half * BANK, (half + 1) * BANK),
                                           k == 0, k == FF // P - 1)
                    last.then_inc(w_used, 1)

                turn_x(0)
                for e in range(E):
                    pe.wait_ge(xplaced, 2 * (e + 1))
                    for f in range(FG):
                        up_group(e, f)
                        if f:
                            turn_h(e, f - 1)
                    down(e, 0)
                    turn_h(e, FG - 1)
                    down(e, 1)
                    if e + 1 < E:
                        turn_x(e + 1)
                    down(e, 2)
                    down(e, 3)

            def half_piece(u, s):
                c = slice(s * KD * BANK // 2, (s + 1) * KD * BANK // 2)
                return raw[u % RW][:, c], w[u % RP].high[:, c], w[u % RP].low[:, c]

            @block.scalar
            def _(act):
                def split_high(u):
                    if u >= E * UNITS:
                        return
                    act.wait_ge(core.load[u % RW].sem, core.load[u % RW].at(u // RW + 1))
                    if u >= RP:
                        act.wait_ge(w_used, u - RP + 1)
                    for s in range(2):
                        x, hi, _ = half_piece(u, s)
                        nc.scalar.activation(hi, x, ACT.Copy).then_inc(high, 1)

                def modulate(e):
                    if e:
                        act.wait_ge(xplaced, 2 * e)
                    for half in range(2):
                        act.wait_ge(xturn, 2 * e + half + 1)
                        for k in range(4 * half, 4 * half + 4):
                            last = nc.scalar.activation(xw[:, k, :], bank[4 + half][:, (k % 4) * P:(k % 4 + 1) * P],
                                                        ACT.Identity, bias=sh[:, k:k + 1], scale=sc[:, k:k + 1])
                        last.then_inc(xwhole, 1)

                def place_h(n):
                    act.wait_ge(hturn, n + 1)
                    f = n % FG
                    nc.scalar.activation(hidT.high[:, 4 * f:4 * f + 4, :],
                                         bank[4 + n % 2][:, :].rearrange("p (k t) -> p k t", t=P),
                                         ACT.Copy).then_inc(hhigh, 1)

                split_high(0)
                modulate(0)
                split_high(1)
                for e in range(E):
                    for i in range(UNITS):
                        split_high(e * UNITS + i + 2)
                        if i < 2 * FG and i % 2:
                            n = e * FG + i // 2
                            act.wait_ge(w_used, e * UNITS + i + 1)
                            if n >= 2:
                                act.wait_ge(hidden, n - 1)
                            nc.scalar.activation(sa[n % 2][:, :], bank[2 * (n % 2)][:, :], ACT.Silu).then_inc(silu, 1)
                            if i > 1:
                                place_h(n - 1)
                        if i == 2 * FG:
                            place_h(e * FG + FG - 1)
                        if i == 2 * FG + 1 and e + 1 < E:
                            modulate(e + 1)

            @block.vector
            def _(dve):
                def split_low(u):
                    if u >= E * UNITS:
                        return
                    for s in range(2):
                        dve.wait_ge(high, 2 * u + s + 1)
                        x, hi, lo = half_piece(u, s)
                        nc.vector.tensor_tensor(lo, x, hi.bitcast(F32), ALU.subtract).then_inc(low, 1)

                def place_h(n):
                    dve.wait_ge(hhigh, n + 1)
                    f = n % FG
                    nc.vector.tensor_tensor(hidT.low[:, 4 * f:4 * f + 4, :],
                                            bank[4 + n % 2][:, :].rearrange("p (k t) -> p k t", t=P),
                                            hidT.high[:, 4 * f:4 * f + 4, :].bitcast(F32), ALU.subtract).then_inc(hplaced, 1)

                def result(e):
                    dve.wait_ge(w_used, (e + 1) * UNITS)
                    if e >= 2:
                        dve.wait_ge(scattered, 16 * (e - 1))
                    for half in range(2):
                        c = slice(half * BANK, (half + 1) * BANK)
                        nc.vector.scalar_tensor_tensor(yo[e % 2][:, c], bank[6 + half][:, :], core.moe_gate[:, e:e + 1],
                                                       g2[:, c], ALU.mult, ALU.mult).then_inc(yout, 1)

                split_low(0)
                split_low(1)
                dve.wait_ge(gain, 16)
                for e in range(E):
                    for i in range(UNITS):
                        split_low(e * UNITS + i + 2)
                        if i == 0 and e:
                            result(e - 1)
                        if i < 2 * FG and i % 2:
                            n = e * FG + i // 2
                            dve.wait_ge(silu, n + 1)
                            if n >= 2:
                                dve.wait_ge(hturn, n - 1)
                            nc.vector.tensor_tensor(hid[n % 2][:, :], sa[n % 2][:, :], bank[2 * (n % 2) + 1][:, :],
                                                    ALU.mult).then_inc(hidden, 1)
                            if i > 1:
                                place_h(n - 1)
                        if i == 2 * FG:
                            place_h(e * FG + FG - 1)
                result(E - 1)
        for j in range(RW):
            core.load[j].close(len(range(j, E * UNITS, RW)))


def stage_final_norm(core, name="final"):
    nc, io = core.nc, core.io
    RX = 3
    with Stage(core, name) as st:
        x = [st.sb(f"x{i}", [P, D]) for i in range(RX)]
        y = [st.sb(f"y{i}", [P, D]) for i in range(RX)]
        junk, gain = st.sb("junk", [P, D]), st.sb("gain", [P, D])
        ss, rms = st.sb("ss", [P, NT]), st.sb("rms", [P, NT])
        gains, rooted, done = st.sem("gains"), st.sem("rooted"), st.sem("done")
        with st.block() as block:
            @block.sync
            def _(sp):
                sp.dma_start(gain[:, :], io["final_g"].partition_broadcast(P)).then_inc(gains, 16)
                for t in range(NT):
                    if t >= RX:
                        sp.wait_ge(done, t - RX + 1)
                    sp.dma_start(x[t % RX][:, :], core.x1[t * P:(t + 1) * P, :]).then_inc(core.load[t % RX].sem, 16)

            @block.scalar
            def _(act):
                for t in range(NT):
                    act.wait_ge(core.load[t % RX].sem, core.load[t % RX].at(t // RX + 1))
                    core.act(act, nc.scalar.activation(junk[:, :], x[t % RX][:, :], ACT.Square, accum_out=ss[:, t:t + 1]))
                    nc.scalar.activation(rms[:, t:t + 1], ss[:, t:t + 1], ACT.Sqrt, bias=core.eps[:, 0:1],
                                         scale=1.0 / D).then_inc(rooted, 1)

            @block.vector
            def _(dve):
                dve.wait_ge(gains, 16)
                for t in range(NT):
                    dve.wait_ge(rooted, t + 1)
                    core.dve(dve, nc.vector.reciprocal(rms[:, t:t + 1], rms[:, t:t + 1]))
                    if t >= RX:
                        dve.wait_ge(core.store[t % RX].sem, core.store[t % RX].at(t // RX))
                    nc.vector.scalar_tensor_tensor(y[t % RX][:, :], x[t % RX][:, :], rms[:, t:t + 1], gain[:, :],
                                                   ALU.mult, ALU.mult).then_inc(done, 1)

            @block.gpsimd
            def _(pool):
                for t in range(NT):
                    pool.wait_ge(done, t + 1)
                    pool.dma_start(core.x2[t * P:(t + 1) * P, :], y[t % RX][:, :]).then_inc(core.store[t % RX].sem, 16)
                for j in range(RX):
                    pool.wait_ge(core.store[j].sem, core.store[j].at(len(range(j, NT, RX))))
        for j in range(RX):
            core.load[j].close(len(range(j, NT, RX)))
            core.store[j].close(len(range(j, NT, RX)))


def lam_init(l):
    return 0.8 - 0.6 * math.exp(-0.3 * l)


def stage_qk(core, l, tiles_q, q_parts, k_high, k_low, neg_lam, name):
    nc, io = core.nc, core.io
    HM = 2 * HEADS2
    items = [(0, t) for t in tiles_q] + [(1, t) for t in range(NT + NC_)]
    RX = 4
    with Stage(core, name) as st:
        cos, sin = st.sb("cos", [P, NT, QK]), st.sb("sin", [P, NT, QK])
        g = st.sb("g", [P, 2, QK])
        cosg = [st.sb(f"cosg{i}", [P, NT, QK]) for i in range(2)]
        sing = [st.sb(f"sing{i}", [P, NT, QK]) for i in range(2)]
        lv, lp, ls = st.sb("lv", [P, 4, QK]), st.sb("lp", [P, 2, QK]), st.sb("ls", [P, 2])
        x = [st.sb(f"x{i}", [P, HM, QK]) for i in range(RX)]
        sq = [st.sb(f"sq{i}", [P, HM, QK]) for i in range(2)]
        rms = st.sb("rms", [P, len(items), HM])
        y1 = [st.sb(f"ya{i}", [P, HM, QK]) for i in range(2)]
        y2 = [st.sb(f"yb{i}", [P, HM, QK]) for i in range(2)]
        y = [st.sb(f"y{i}", [P, HM, QK]) for i in range(2)]
        stacked = [st.sb(f"stacked{i}", [P, HM, 2, QK], F32R) for i in range(2)]
        low = [st.sb(f"low{i}", [P, HM, QK], F32R) for i in range(2)]
        bank = st.banks(6)
        inputs, squared, summed, rooted, high, split, ready, turned, placed, lsum, lexp = (st.sem(k) for k in (
            "inputs", "squared", "summed", "rooted", "high", "split", "ready", "turned", "placed", "lsum", "lexp"))
        n_q = len(tiles_q)
        with st.block() as block:
            @block.sync
            def _(sp):
                sp.dma_start(cos[:, :, :], io["t_rope_cos"].rearrange("(t p) d -> p t d", p=P)).then_inc(inputs, 16)
                sp.dma_start(sin[:, :, :], io["t_rope_sin"].rearrange("(t p) d -> p t d", p=P)).then_inc(inputs, 16)
                sp.dma_start(g[:, :, :], io["qk_norm_g_2"][l].partition_broadcast(P)).then_inc(inputs, 16)
                sp.dma_start(lv[:, :, :], io["lam_vecs_2"][l].partition_broadcast(P)).then_inc(inputs, 16)
                for i, (which, t) in enumerate(items):
                    if i >= RX:
                        sp.wait_ge(ready, i - RX + 1)
                    sp.dma_start(x[i % RX][:, :, :], core.qk_tok[which, t * P:(t + 1) * P, :].rearrange(
                        "p (h d) -> p h d", d=QK)).then_inc(core.load[i % RX].sem, 16)

            @block.scalar
            def _(act):
                def measure(i):
                    act.wait_ge(core.load[i % RX].sem, core.load[i % RX].at(i // RX + 1))
                    if i >= 2:
                        act.wait_ge(summed, i - 1)
                    nc.scalar.activation(sq[i % 2][:, :, :], x[i % RX][:, :, :], ACT.Square).then_inc(squared, 1)

                def root(i):
                    act.wait_ge(summed, i + 1)
                    nc.scalar.activation(rms[:, i, :], rms[:, i, :], ACT.Sqrt, bias=core.eps[:, 0:1],
                                         scale=1.0 / QK).then_inc(rooted, 1)

                def key_high(i):
                    act.wait_ge(ready, i + 1)
                    if i >= 2:
                        act.wait_ge(turned, i - 1)
                    nc.scalar.activation(stacked[i % 2][:, :, :, :],
                                         y[i % 2][:, :, :].unsqueeze(2).to_broadcast([P, HM, 2, QK]), ACT.Copy).then_inc(high, 1)

                def place(i):
                    which, t = items[i]
                    c = slice(t * P, (t + 1) * P)
                    act.wait_ge(turned, i + 1)
                    dst = k_high if which else q_parts
                    out = [dst[:, 0:4, c], dst[:, 4:8, c]] + ([k_low[:, :, c]] if which else [])
                    for j, o in enumerate(out):
                        last = nc.scalar.activation(o, bank[3 * (i % 2) + j][:, :].rearrange("p (h t) -> p h t", t=P), ACT.Copy)
                    last.then_inc(placed, 1)

                act.wait_ge(lsum, 1)
                nc.scalar.activation(ls[:, :], ls[:, :], ACT.Exp).then_inc(lexp, 1)
                measure(0)
                measure(1)
                root(0)
                for i in range(len(items) + 2):
                    if i + 2 < len(items):
                        measure(i + 2)
                    if i + 1 < len(items):
                        root(i + 1)
                    if n_q <= i - 1 < len(items):
                        key_high(i - 1)
                    if i >= 2:
                        place(i - 2)

            @block.gpsimd
            def _(pool):
                for i, (which, t) in enumerate(items):
                    pool.wait_ge(ready, i + 1)
                    if i >= 2:
                        pool.wait_ge(turned, i - 1)
                    if which:
                        pool.wait_ge(high, i - n_q + 1)
                        nc.gpsimd.tensor_tensor(low[i % 2][:, :, :], y[i % 2][:, :, :],
                                                stacked[i % 2][:, :, 0, :].bitcast(F32), ALU.subtract).then_inc(split, 1)
                        continue
                    yy = y[i % 2][:, :, :].rearrange("p (h m) d -> p h m d", m=2)
                    ss_ = stacked[i % 2][:, :, :, :].rearrange("p (h m) s d -> p h m s d", m=2)
                    for m in range(2):
                        core.pool(pool, nc.gpsimd.tensor_copy(ss_[:, :, m, m, :], yy[:, :, m, :]))
                    for m in range(2):
                        last = nc.gpsimd.tensor_tensor(ss_[:, :, m, 1 - m, :], yy[:, :, m, :],
                                                       ss_[:, :, m, m, :].bitcast(F32), ALU.subtract)
                    last.then_inc(split, 1)

            @block.tensor
            def _(pe):
                for i, (which, t) in enumerate(items):
                    pe.wait_ge(split, i + 1)
                    if i >= 2:
                        pe.wait_ge(placed, i - 1)
                    for h in range(HM):
                        src = stacked[i % 2][:, h, :, :].rearrange("p s d -> p (s d)").bitcast(F32)
                        last = nc.tensor.transpose(bank[3 * (i % 2) + h // 4][:, (h % 4) * P:(h % 4 + 1) * P], src,
                                                   core.ident[:, :])
                    for h in range(HEADS2 if which else 0):
                        src = low[i % 2][:, 2 * h:2 * h + 2, :].rearrange("p m d -> p (m d)").bitcast(F32)
                        last = nc.tensor.transpose(bank[3 * (i % 2) + 2][:, h * P:(h + 1) * P], src, core.ident[:, :])
                    last.then_inc(turned, 1)

            @block.vector
            def _(dve):
                step = lambda ins: core.dve(dve, ins)
                dve.wait_ge(inputs, 64)
                lvv = lv[:, :, :].rearrange("p (a b) d -> p a b d", b=2)
                step(nc.vector.tensor_tensor(lp[:, :, :], lvv[:, :, 0, :], lvv[:, :, 1, :], ALU.mult))
                nc.vector.tensor_reduce(ls[:, :], lp[:, :, :], AX, ALU.add).then_inc(lsum, 1)
                dve.wait_ge(lexp, 1)
                step(nc.vector.tensor_tensor(neg_lam[:, :], ls[:, 1:2], ls[:, 0:1], ALU.subtract))
                step(nc.vector.tensor_scalar(neg_lam[:, :], neg_lam[:, :], lam_init(l), None, ALU.subtract))
                for w in range(2):
                    gr = g[:, w, :].rearrange("p (a s c) -> p a s c", a=2, s=2)
                    step(nc.vector.tensor_tensor(cosg[w][:, :, :], cos[:, :, :],
                                                 g[:, w:w + 1, :].to_broadcast([P, NT, QK]), ALU.mult))
                    s_in = sin[:, :, :].rearrange("p t (a s c) -> p t a s c", a=2, s=2)
                    s_out = sing[w][:, :, :].rearrange("p t (a s c) -> p t a s c", a=2, s=2)
                    for a in range(2):
                        for s in range(2):
                            step(nc.vector.tensor_tensor(s_out[:, :, a, s, :], s_in[:, :, a, s, :],
                                                         gr[:, a, 1 - s, :].unsqueeze(1).to_broadcast([P, NT, 16]), ALU.mult))
                def total(i):
                    dve.wait_ge(squared, i + 1)
                    nc.vector.tensor_reduce(rms[:, i, :], sq[i % 2][:, :, :], AX, ALU.add).then_inc(summed, 1)

                total(0)
                for i, (w, t) in enumerate(items):
                    xx = x[i % RX]
                    if i + 1 < len(items):
                        total(i + 1)
                    dve.wait_ge(rooted, i + 1)
                    step(nc.vector.reciprocal(rms[:, i, :], rms[:, i, :]))
                    step(nc.vector.tensor_tensor(xx[:, :, :], xx[:, :, :],
                                                 rms[:, i, :].unsqueeze(2).to_broadcast([P, HM, QK]), ALU.mult))
                    if i >= 2:
                        dve.wait_ge(split, i - 1)
                    if t < NT:
                        step(nc.vector.tensor_tensor(y1[i % 2][:, :, :], xx[:, :, :],
                                                     cosg[w][:, t:t + 1, :].to_broadcast([P, HM, QK]), ALU.mult))
                        xs = xx[:, :, :].rearrange("p h (a s c) -> p h a s c", a=2, s=2)
                        ys = y2[i % 2][:, :, :].rearrange("p h (a s c) -> p h a s c", a=2, s=2)
                        sg = sing[w][:, t, :].rearrange("p (a s c) -> p a s c", a=2, s=2)
                        for s in range(2):
                            step(nc.vector.tensor_tensor(ys[:, :, :, s, :], xs[:, :, :, 1 - s, :],
                                                         sg[:, :, s, :].unsqueeze(1).to_broadcast([P, HM, 2, 16]), ALU.mult))
                        nc.vector.tensor_tensor(y[i % 2][:, :, :], y1[i % 2][:, :, :], y2[i % 2][:, :, :],
                                                ALU.add).then_inc(ready, 1)
                    else:
                        nc.vector.tensor_tensor(y[i % 2][:, :, :], xx[:, :, :],
                                                g[:, w:w + 1, :].to_broadcast([P, HM, QK]), ALU.mult).then_inc(ready, 1)

        for j in range(RX):
            core.load[j].close(len(range(j, len(items), RX)))


def stage_attend(core, l, tiles_q, q_parts, k_high, k_low, neg_lam, y_att, name):
    nc, io = core.nc, core.io
    TL = NT + NC_
    SCALE = float(QK) ** -0.5
    items = [(h, t, 0 if t < NT else NT, TL) for h in range(HEADS2) for t in tiles_q]
    N = len(items)
    LAG = 2
    groups = []
    for h in range(HEADS2):
        for t in range(0, len(tiles_q), 4):
            groups.append((h, h * len(tiles_q) + t, min(4, len(tiles_q) - t)))
    group_of = {i: g for g, (_, i0, n) in enumerate(groups) for i in range(i0, i0 + n)}
    last_group = {h: g for g, (h, _, _) in enumerate(groups)}

    def due(i):
        for g, (h, i0, n) in enumerate(groups):
            spread = groups[g + 1][2] if g + 1 < len(groups) else 2
            r = i - (i0 + n + LAG)
            if 0 <= r < spread:
                b = blocks(i0)
                yield g, b * r // spread, b * (r + 1) // spread

    def blocks(i):
        return items[i][3] - items[i][2]

    gof, total = [], 0
    for i in range(N):
        gof.append(total)
        total += -(-blocks(i) // 4)
    gof.append(total)
    steps = N + LAG + 2 + 1
    with Stage(core, name) as st:
        v = [st.sb(f"v{i}", [P, TL, P]) for i in range(2)]
        p = [[st.sb(f"p{m}{i}", [P, TOK]) for m in range(2)] for i in range(LAG + 1)]
        pT = [st.sb(f"pT{i}", [P, TL, BANK]) for i in range(2)]
        mx, nb = st.sb("mx", [P, N, 3]), st.sb("nb", [P, N, 2])
        sums, rinv = st.sb("sums", [P, N, 2]), st.sb("rinv", [P, N, 2])
        scores = st.stack.enter_context(nc.psum_tensor(f"{name}_scores", [P, 5 * BANK], F32))
        bank = st.banks(3)
        shared, scored, bounded, exped, inverted, scaled, mixed, turned, placed, odone, ocopied = (st.sem(k) for k in (
            "shared", "scored", "bounded", "exped", "inverted", "scaled", "mixed", "turned", "placed", "o", "o_copied"))
        FIRST, SHARED, SECOND = [(0, 512), (512, 512)], [(0, 1024, 256), (1, 0, 256)], [(256, 512), (768, 512)]

        with st.block() as block:
            @block.sync
            def _(sp):
                for h in range(HEADS2):
                    if h >= 2:
                        sp.wait_ge(odone, last_group[h - 2] + 1)
                    sp.dma_start(v[h % 2][:, :, :], core.v_tok[:, h * P:(h + 1) * P].rearrange("(t p) c -> p t c", p=P)
                                 ).then_inc(core.load[h % 2].sem, 16)

            @block.tensor
            def _(pe):
                def score(i, m, c, n):
                    h, t, k0, k1 = items[i]
                    if c >= (k1 - k0) * P:
                        return None
                    n = min(n, (k1 - k0) * P - c)
                    hm, tok, key = 2 * h + m, slice(t * P, (t + 1) * P), slice(k0 * P + c, k0 * P + c + n)
                    rows = slice(m * QK, (m + 1) * QK)
                    out = scores[:, m * TOK + c:m * TOK + c + n]
                    nc.tensor.matmul(out, q_parts[:, hm, tok], k_high[:, hm, key], start=True, stop=False)
                    if m and c == 0:
                        pe.wait_ge(shared, i + 1)
                    return nc.tensor.matmul(out, q_parts[rows, hm, tok], k_low[rows, h, key], start=False, stop=True)

                def scores_of(i):
                    if i:
                        pe.wait_ge(exped, 2 * i - 1)
                    for c, n in FIRST:
                        last = score(i, 0, c, n) or last
                    if i:
                        pe.wait_ge(exped, 2 * i)
                    last = score(i, *SHARED[0]) or last
                    last.then_inc(shared, 1)
                    score(i, *SHARED[1]).then_inc(scored, 1)
                    last = None
                    for c, n in SECOND:
                        last = score(i, 1, c, n) or last
                    if last is None:
                        pe.wait_ge(scored, 2 * i + 1)
                        pe.sem_inc(scored, 1)
                    else:
                        last.then_inc(scored, 1)

                def turn(i):
                    pe.wait_ge(mixed, i + 1)
                    for gi in range(gof[i], gof[i + 1]):
                        b0 = 4 * (gi - gof[i])
                        if gi >= 2:
                            pe.wait_ge(placed, gi - 1)
                        for b in range(min(4, blocks(i) - b0)):
                            last = nc.tensor.transpose(bank[gi % 2][:, b * P:(b + 1) * P],
                                                       p[i % (LAG + 1)][0][:, (b0 + b) * P:(b0 + b + 1) * P],
                                                       core.ident[:, :])
                        last.then_inc(turned, 1)

                def values(g, b0, b1):
                    h, i0, n = groups[g]
                    k0 = items[i0][2]
                    if b0 == 0:
                        pe.wait_ge(placed, gof[i0 + n])
                        pe.wait_ge(core.load[h % 2].sem, core.load[h % 2].at(h // 2 + 1))
                        if g:
                            pe.wait_ge(ocopied, g)
                    for b in range(b0, b1):
                        last = nc.tensor.matmul(bank[2][:, 0:n * P], v[h % 2][:, k0 + b, :], pT[g % 2][:, b, 0:n * P],
                                                start=(b == 0), stop=(b == blocks(i0) - 1))
                    if b1 == blocks(i0):
                        last.then_inc(odone, 1)

                for i in range(steps):
                    if i < N:
                        scores_of(i)
                    if LAG <= i < N + LAG:
                        turn(i - LAG)
                    for g, b0, b1 in due(i):
                        values(g, b0, b1)

            @block.scalar
            def _(act):
                def exps(i, m):
                    n = blocks(i) * P
                    act.wait_ge(bounded, 2 * i + (m + 1 if blocks(i) * P > SHARED[1][2] else 2))
                    if i > LAG:
                        act.wait_ge(turned, gof[i - LAG])
                    nc.scalar.activation(p[i % (LAG + 1)][m][:, 0:n], scores[:, m * TOK:m * TOK + n], ACT.Exp,
                                         bias=nb[:, i, m:m + 1], scale=SCALE, accum_out=sums[:, i, m:m + 1]).then_inc(exped, 1)

                def place(i):
                    g = group_of[i]
                    col = (i - groups[g][1]) * P
                    if g >= 2:
                        act.wait_ge(odone, g - 1)
                    for gi in range(gof[i], gof[i + 1]):
                        b0 = 4 * (gi - gof[i])
                        nb_ = min(4, blocks(i) - b0)
                        act.wait_ge(turned, gi + 1)
                        nc.scalar.activation(pT[g % 2][:, b0:b0 + nb_, col:col + P],
                                             bank[gi % 2][:, 0:nb_ * P].rearrange("p (b t) -> p b t", t=P),
                                             ACT.Copy).then_inc(placed, 1)

                for i in range(N + LAG):
                    if i >= LAG:
                        place(i - LAG)
                    if i < N:
                        exps(i, 0)
                        exps(i, 1)

            @block.gpsimd
            def _(pool):
                for i in range(N):
                    n = blocks(i) * P
                    pool.wait_ge(inverted, i + 1)
                    b = p[i % (LAG + 1)][1][:, 0:n]
                    nc.gpsimd.tensor_scalar(b, b, rinv[:, i, 1:2], neg_lam[:, :], ALU.mult, ALU.mult).then_inc(scaled, 1)

            @block.vector
            def _(dve):
                step = lambda ins: core.dve(dve, ins)

                def bound(i):
                    n, part = blocks(i) * P, SHARED[1][2]
                    dve.wait_ge(scored, 2 * i + 1)
                    step(nc.vector.tensor_reduce(mx[:, i, 0:1], scores[:, 0:n], AX, ALU.max))
                    step(nc.vector.tensor_reduce(mx[:, i, 1:2], scores[:, TOK:TOK + part], AX, ALU.max))
                    nc.vector.tensor_scalar(nb[:, i, 0:1], mx[:, i, 0:1], -SCALE, None, ALU.mult).then_inc(bounded, 1)
                    dve.wait_ge(scored, 2 * i + 2)
                    rest = part if n > part else 0
                    step(nc.vector.tensor_reduce(mx[:, i, 2:3], scores[:, TOK + rest:TOK + n], AX, ALU.max))
                    nc.vector.tensor_scalar(nb[:, i, 1:2], mx[:, i, 2:3], mx[:, i, 1:2], -SCALE,
                                            ALU.max, ALU.mult).then_inc(bounded, 1)

                def mix(i):
                    n = blocks(i) * P
                    dve.wait_ge(scaled, i + 1)
                    a, b = p[i % (LAG + 1)]
                    nc.vector.scalar_tensor_tensor(a[:, 0:n], a[:, 0:n], rinv[:, i, 0:1], b[:, 0:n],
                                                   ALU.mult, ALU.add).then_inc(mixed, 1)

                for i in range(steps):
                    for g, _, b1 in due(i - 1):
                        h, i0, n = groups[g]
                        if b1 == blocks(i0):
                            t0 = items[i0][1]
                            dve.wait_ge(odone, g + 1)
                            nc.vector.tensor_copy(y_att[:, h, t0 * P:(t0 + n) * P], bank[2][:, 0:n * P]).then_inc(ocopied, 1)
                    if i < N:
                        bound(i)
                    if i and i <= N:
                        mix(i - 1)
                    if i < N:
                        dve.wait_ge(exped, 2 * i + 2)
                        nc.vector.reciprocal(rinv[:, i, :], sums[:, i, :]).then_inc(inverted, 1)
        for j in range(2):
            core.load[j].close(HEADS2 // 2)


def load_out_weights(core, sp, l, raw, p):
    rows = raw[0].shape[1] * P
    sp.dma_start(raw[p % 2][:, :, :], core.io["w_out_2"][l][p * rows:(p + 1) * rows, :].rearrange(
        "(k p) n -> p k n", p=P)).then_inc(core.load[3 + p % 2].sem, 16)


def stage_mix2(core, l, segs, y_att, y_mix, raw, name):
    nc, io = core.nc, core.io
    TL = sum(n for _, n in segs)
    W = TL * P
    PADL, PADR = 16, 8
    RM = 3
    with Stage(core, name) as st:
        a = st.sb("a", [P, TL, 256])
        tab = [st.sb("tcos", [P, NT, BANK]), st.sb("tsin", [P, NT, BANK])]
        eo = [st.sb(f"eo{i}", [P, 2, BANK]) for i in range(2)]
        tabc = [st.sb(f"tabc{i}", [P, NC_, CTX]) for i in range(2)]
        F = [[st.sb(f"f{cs}{c}", [P, W]) for c in range(2)] for cs in range(2)]
        dft = [st.sb("dcos", [P, P]), st.sb("dsin", [P, P])]
        wf, wp = st.sb("wf", [P, 2, P]), st.sb("wp", [P, 2, P])
        M = [st.sb("m_cos", [P, 2, P]), st.sb("m_sin", [P, 2, P])]
        gate = [st.sb(f"gate{i}", [P, W]) for i in range(3)]
        u = [st.sb(f"u{j}", [P, PADL + SEQ + PADR]) for j in range(2)]
        s1, s2 = st.sb("s1", [P, PADL + SEQ + PADR]), st.sb("s2", [P, PADL + SEQ + PADR])
        icnt, icntc = st.sb("icnt", [P, 2, SEQ]), st.sb("icntc", [P, 2, CTX])
        pooled = [st.sb(f"pooled{j}", [P, W]) for j in range(2)]
        square = [st.sb(f"square{i}", [P, BANK]) for i in range(2)]
        rms = [st.sb(f"rms{i}", [P, BANK]) for i in range(RM)]
        ones = st.sb("ones", [P, P])
        gsub = st.sb("gsub", [P, 1])
        bank = st.banks(8)
        loaded_u = st.dma_sem("loaded_u")
        counts, combined = st.sem("counts"), st.sem("combined")
        (small, zeroed, cosines, sines, ctx_tables, mdone, mcopied, fdone, fcopied, pool_done, normed,
         silu, rooted, squared, summed, product_done, placed) = (st.sem(k) for k in (
             "small", "zeroed", "cosines", "sines", "ctx_tables", "m", "m_copied", "f", "f_copied", "pooled",
             "normed", "silu", "rooted", "squared", "summed", "product", "placed"))
        fjobs = [(cs, c, t0, n) for cs in range(2) for c in range(2)
                 for t0, n in [(0, NT // 2), (NT // 2, NT // 2)] + [x for x in segs if x[0]]]
        first_sine = len(fjobs) // 2
        cols = [(c, min(BANK, W - c)) for c in range(0, W, BANK)]
        pjobs = [(kind, c, c0, n) for kind in range(2) for c in range(2) for c0, n in cols]
        NM = HEADS2 * len(cols)
        assert NM == len(fjobs)
        gates = [4, 5, 6, 7, 0, 1, 2, 3]
        SMALL = 16 * (8 + 2 + 2 + (TL > NT))
        seg_u = [(j, t0, nt) for t0, nt in segs for j in range(2)]
        with st.block() as block:
            @block.sync
            def _(sp):
                sp.wait_ge(zeroed, 5)
                for g in range(4):
                    r = slice((g % 2) * 64, (g % 2) * 64 + 64)
                    sp.dma_start(wf[r, g // 2, r], io["w_fourier_2"][l][g]).then_inc(small, 16)
                    sp.dma_start(wp[r, g // 2, r], io["w_pool_2"][l][g]).then_inc(small, 16)
                sp.dma_start(dft[0][:, :], io["t_dim_cos"]).then_inc(small, 16)
                sp.dma_start(dft[1][:, :], io["t_dim_sin"]).then_inc(small, 16)
                for v in range(2):
                    sp.dma_start(a[:, v * NT // 2:(v + 1) * NT // 2, :], core.a_tok[0:SEQ, :].rearrange(
                        "(t p v) c -> v p t c", p=P, v=2)[v]).then_inc(small, 16)
                if TL > NT:
                    sp.dma_start(a[:, NT:, :], core.a_tok[SEQ:W, :].rearrange("(t p) c -> p t c", p=P)).then_inc(small, 16)
                sp.dma_start(tab[0][:, :, :], io["t_tok_cos"].rearrange("(t p) k -> p t k", p=P)).then_inc(cosines, 16)
                for pos in range(2):
                    k = gates[pos]
                    sp.dma_start(gate[pos][:, :], core.gate_t[k * P:(k + 1) * P, 0:W]).then_inc(core.load[pos].sem, 16)
                sp.dma_start(icnt[:, :, :], io["t_inv_count"].rearrange("p (j t) -> p j t", j=2)).then_inc(counts, 16)
                sp.dma_start(icntc[:, :, :], io["t_inv_count_ctx"].rearrange("p (j t) -> p j t", j=2)).then_inc(counts, 16)
                for i in range(2):
                    sp.dma_start(tabc[i][:, :, :], io["t_ctx_cos" if i == 0 else "t_ctx_sin"].rearrange(
                        "(t p) k -> p t k", p=P)).then_inc(ctx_tables, 16)
                sp.dma_start(tab[1][:, :, :], io["t_tok_sin"].rearrange("(t p) k -> p t k", p=P)).then_inc(sines, 16)
                for pos in range(2, KD):
                    k = gates[pos]
                    if pos >= 3:
                        was = pos - 3
                        sp.wait_ge(normed if was < 4 else placed, (was % 4 + 1) * len(cols))
                    sp.dma_start(gate[pos % 3][:, :], core.gate_t[k * P:(k + 1) * P, 0:W]
                                 ).then_inc(core.load[pos % 3].sem, 16)
                for p in range(len(raw)):
                    load_out_weights(core, sp, l, raw, p)

            @block.gpsimd
            def _(pool):
                for tile in (wf, wp):
                    nc.gpsimd.memset(tile[:, :, :], 0.0).then_inc(zeroed, 1)
                for tile in u:
                    nc.gpsimd.memset(tile[:, :], 0.0).then_inc(zeroed, 1)
                nc.gpsimd.memset(ones[:, :], 1.0).then_inc(zeroed, 1)
                for i, (j, t0, nt) in enumerate(seg_u):
                    if i >= 2:
                        pool.wait_ge(pool_done, i - 1)
                        pool.wait_ge(zeroed, 5)
                        nc.gpsimd.memset(u[j][:, PADL:], 0.0).then_inc(zeroed, 1)
                        pool.wait_ge(zeroed, 5 + i - 1)
                    else:
                        pool.wait_ge(zeroed, 5)
                    pool.dma_start(u[j][:, PADL:PADL + nt * P], core.b_t[j * P:(j + 1) * P, t0 * P:(t0 + nt) * P]
                                   ).then_inc(loaded_u, 16)
                    pool.wait_ge(loaded_u, 16 * (i + 1))
                for i, (cs, c) in enumerate((cs, c) for cs in range(2) for c in range(2)):
                    pool.wait_ge(fcopied, i // 2 * first_sine + (i % 2) * (first_sine // 2) + 2)
                    e, o = eo[i % 2][:, 0, :], eo[i % 2][:, 1, :]
                    nc.gpsimd.tensor_tensor(F[cs][c][:, 0:BANK], e, o, ALU.add)
                    nc.gpsimd.tensor_tensor(F[cs][c][:, BANK:SEQ], e, o, ALU.subtract).then_inc(combined, 1)

            @block.tensor
            def _(pe):
                pe.wait_ge(small, SMALL)
                for cs in range(2):
                    for c in range(2):
                        last = nc.tensor.matmul(bank[0][:, (2 * cs + c) * P:(2 * cs + c + 1) * P], dft[cs][:, :],
                                                wf[:, c, :], start=True, stop=True)
                last.then_inc(mdone, 1)
                pe.wait_ge(zeroed, 5)
                pe.wait_ge(cosines, 16)
                for i, (cs, c, t0, nt) in enumerate(fjobs):
                    if i >= 3:
                        pe.wait_ge(fcopied, i - 2)
                    if i == first_sine:
                        pe.wait_ge(sines, 16)
                    if t0 >= NT:
                        pe.wait_ge(ctx_tables, 32)
                    n = BANK if t0 < NT else CTX
                    for t in range(nt):
                        rhs = tab[cs][:, t0 + t, :] if t0 < NT else tabc[cs][:, t, :]
                        last = nc.tensor.matmul(bank[1 + i % 3][:, 0:n], a[:, t0 + t, c * P:(c + 1) * P], rhs,
                                                start=(t == 0), stop=(t == nt - 1))
                    last.then_inc(fdone, 1)
                    n = cols[i % len(cols)][1]
                    pe.wait_ge(squared, i + 1)
                    if i >= 2:
                        pe.wait_ge(rooted, i - 1)
                    nc.tensor.matmul(bank[6 + i % 2][:, 0:n], ones[:, :], square[i % 2][:, 0:n],
                                     start=True, stop=True).then_inc(summed, 1)
                pe.wait_ge(fcopied, len(fjobs))
                pe.wait_ge(combined, 4)
                pe.wait_ge(mcopied, 1)
                pe.wait_ge(pool_done, len(seg_u))
                for i, (kind, c, c0, n) in enumerate(pjobs):
                    if i >= 2:
                        pe.wait_ge(placed, i - 1)
                    if kind == 0:
                        for cs in range(2):
                            last = nc.tensor.matmul(bank[4 + i % 2][:, 0:n], M[cs][:, c, :], F[cs][c][:, c0:c0 + n],
                                                    start=(cs == 0), stop=(cs == 1))
                    else:
                        last = nc.tensor.matmul(bank[4 + i % 2][:, 0:n], wp[:, c, :], pooled[c][:, c0:c0 + n],
                                                start=True, stop=True)
                    last.then_inc(product_done, 1)

            @block.scalar
            def _(act):
                def root(m):
                    n = cols[m % len(cols)][1]
                    act.wait_ge(summed, m + 1)
                    if m >= RM:
                        act.wait_ge(normed, m - RM + 1)
                    nc.scalar.activation(rms[m % RM][:, 0:n], bank[6 + m % 2][:, 0:n], ACT.Sqrt, bias=core.eps[:, 0:1],
                                         scale=1.0 / P).then_inc(rooted, 1)

                act.wait_ge(mdone, 1)
                mm = bank[0][:, :].rearrange("p (s c d) -> p s c d", s=2, c=2)
                core.act(act, nc.scalar.activation(M[0][:, :, :], mm[:, 0, :, :], ACT.Copy))
                nc.scalar.activation(M[1][:, :, :], mm[:, 1, :, :], ACT.Copy, scale=-1.0).then_inc(mcopied, 1)

                def open_gate(pos):
                    g = gate[pos % 3][:, :]
                    act.wait_ge(core.load[pos % 3].sem, core.load[pos % 3].at(pos // 3 + 1))
                    nc.scalar.activation(g, g, ACT.Silu).then_inc(silu, 1)

                def squares(m):
                    h, (c0, n) = m // len(cols), cols[m % len(cols)]
                    if m >= 2:
                        act.wait_ge(summed, m - 1)
                    nc.scalar.activation(square[m % 2][:, 0:n], y_att[:, h, c0:c0 + n], ACT.Square).then_inc(squared, 1)

                squares(0)
                for i, (cs, c, t0, nt) in enumerate(fjobs):
                    act.wait_ge(fdone, i + 1)
                    u_ = 2 * cs + c
                    if t0 < NT:
                        if u_ >= 2:
                            act.wait_ge(combined, u_ - 1)
                        to, n = eo[u_ % 2][:, 0 if t0 == 0 else 1, :], BANK
                    else:
                        to, n = F[cs][c][:, SEQ:W], CTX
                    nc.scalar.activation(to, bank[1 + i % 3][:, 0:n], ACT.Copy).then_inc(fcopied, 1)
                    if i + 1 < NM:
                        squares(i + 1)
                    root(i)
                    if i % len(cols) == 0:
                        open_gate(i // len(cols))
                for pos in range(4, KD):
                    open_gate(pos)

            @block.vector
            def _(dve):
                step = lambda ins: core.dve(dve, ins)
                step(nc.vector.tensor_scalar(gsub[:, :], core.col_b[:, AT_B["subln_g_2"] + l:AT_B["subln_g_2"] + l + 1],
                                             1.0 - lam_init(l), None, ALU.mult))

                def norm(m):
                    h, (c0, n) = m // len(cols), cols[m % len(cols)]
                    dve.wait_ge(rooted, m + 1)
                    dve.wait_ge(silu, h + 1)
                    rr, y = rms[m % RM][:, 0:n], y_att[:, h, c0:c0 + n]
                    step(nc.vector.reciprocal(rr, rr))
                    step(nc.vector.scalar_tensor_tensor(rr, rr, gsub[:, :], gate[h % 3][:, c0:c0 + n], ALU.mult, ALU.mult))
                    nc.vector.tensor_tensor(y, y, rr, ALU.mult).then_inc(normed, 1)

                dve.wait_ge(counts, 32)
                for i, (j, t0, nt) in enumerate(seg_u):
                    n = nt * P
                    dve.wait_ge(loaded_u, 16 * (i + 1))
                    full = PADL + n + PADR
                    ic = icnt if t0 == 0 else icntc

                    def double(dst, src, w):
                        step(nc.vector.tensor_tensor(dst[:, w:full], src[:, w:full], src[:, 0:full - w], ALU.add))

                    def take(rows, src, ahead):
                        o = pooled[j][rows, t0 * P:t0 * P + n]
                        step(nc.vector.tensor_tensor(o, src[rows, PADL + ahead:PADL + ahead + n], ic[rows, j, 0:n], ALU.mult))
                        return nc.vector.tensor_tensor(o, o, u[j][rows, PADL:PADL + n], ALU.subtract)

                    if i == 0:
                        step(nc.vector.memset(s1[:, 0:PADL], 0.0))
                        step(nc.vector.memset(s2[:, 0:PADL], 0.0))
                    double(s1, u[j], 1)
                    if j == 0:
                        step(take(slice(0, 64), s1, 0))
                        double(s2, s1, 2)
                        take(slice(64, 128), s2, 1).then_inc(pool_done, 1)
                    else:
                        double(s2, s1, 2)
                        double(s1, s2, 4)
                        step(take(slice(0, 64), s1, 3))
                        double(s2, s1, 8)
                        take(slice(64, 128), s2, 7).then_inc(pool_done, 1)
                    dve.wait_ge(pool_done, i + 1)
                    for m in range(NM * i // len(seg_u), NM * (i + 1) // len(seg_u)):
                        norm(m)
                for i, (kind, c, c0, n) in enumerate(pjobs):
                    k = 2 * kind + c
                    dve.wait_ge(product_done, i + 1)
                    dve.wait_ge(silu, 4 + k + 1)
                    o, y, g = bank[4 + i % 2][:, 0:n], y_mix[:, k, c0:c0 + n], gate[(4 + k) % 3][:, c0:c0 + n]
                    if kind == 0:
                        nc.vector.tensor_tensor(y, o, g, ALU.mult).then_inc(placed, 1)
                    else:
                        s = AT_B["pool_scale_2"] + 2 * l + c
                        nc.vector.scalar_tensor_tensor(y, o, core.col_b[:, s:s + 1], g, ALU.mult, ALU.mult
                                                       ).then_inc(placed, 1)
        for j in range(3):
            core.load[j].close(len(range(j, KD, 3)))


def stage_out2(core, l, halves, raw, rows, name):
    nc, io = core.nc, core.io
    n_tiles = len(rows)
    WP = 4
    RY = 3
    with Stage(core, name) as st:
        w = Parts(st, "w", [P, KD, D])
        y = [Parts(st, f"y{i}", [P, KD, P]) for i in range(RY)]
        gate = [st.sb(f"gate{v}", [P, D]) for v in range(2)]
        x = [st.sb(f"x{i}", [P, D]) for i in range(3)]
        out = [st.sb(f"out{i}", [P, D]) for i in range(3)]
        bank = st.banks(8)
        gates, done, scaled, added, w_high, w_low, y_high, y_low = (st.sem(k) for k in (
            "gates", "product", "scaled", "added", "w_high", "w_low", "y_high", "y_low"))
        with st.block() as block:
            @block.sync
            def _(sp):
                for p in range(2, WP):
                    sp.wait_ge(w_low, p - 1)
                    load_out_weights(core, sp, l, raw, p)
                for v in range(2):
                    sp.dma_start(gate[v][:, :], core.mod_rows[1 + l][v, 2 * D:3 * D].partition_broadcast(P)
                                 ).then_inc(gates, 16)
                for t, (src, _, _) in enumerate(rows):
                    if t >= 3:
                        sp.wait_ge(added, 2 * (t - 2))
                    sp.dma_start(x[t % 3][:, :], src).then_inc(core.load[t % 3].sem, 16)

            def w_piece(p):
                c = slice(p * KD // WP, (p + 1) * KD // WP)
                return raw[p % 2][:, :, :], w.high[:, c, :], w.low[:, c, :]

            @block.scalar
            def _(act):
                def high(t):
                    if t >= RY:
                        act.wait_ge(done, 2 * (t - RY + 1))
                    for j in range(2):
                        nc.scalar.activation(y[t % RY].high[:, 4 * j:4 * j + 4, :], halves[j][:, :, t * P:(t + 1) * P],
                                             ACT.Copy).then_inc(y_high, 1)

                high(0)
                for p in range(WP):
                    act.wait_ge(core.load[3 + p % 2].sem, core.load[3 + p % 2].at(p // 2 + 1))
                    raw_, hi, _ = w_piece(p)
                    nc.scalar.activation(hi, raw_, ACT.Copy).then_inc(w_high, 1)
                for t in range(1, n_tiles):
                    high(t)

            @block.tensor
            def _(pe):
                for n in range(2 * n_tiles):
                    t, half = divmod(n, 2)
                    pe.wait_ge(y_low, 2 * t + 2)
                    if n >= 8:
                        pe.wait_ge(scaled, n - 7)
                    for k in range(KD):
                        if n == 0 and k % (KD // WP) == 0:
                            pe.wait_ge(w_low, k // (KD // WP) + 1)
                        last = product(nc, bank[n % 8][:, :], y[t % RY][:, k, :], w[:, k, half * BANK:(half + 1) * BANK],
                                       k == 0, k == KD - 1)
                    last.then_inc(done, 1)

            @block.vector
            def _(dve):
                for p in range(WP):
                    dve.wait_ge(w_high, p + 1)
                    raw_, hi, lo = w_piece(p)
                    nc.vector.tensor_tensor(lo, raw_, hi.bitcast(F32), ALU.subtract).then_inc(w_low, 1)
                dve.wait_ge(gates, 32)
                for n in range(2 * n_tiles):
                    t, half = divmod(n, 2)
                    c = slice(half * BANK, (half + 1) * BANK)
                    dve.wait_ge(done, n + 1)
                    dve.wait_ge(core.load[t % 3].sem, core.load[t % 3].at(t // 3 + 1))
                    if t >= 3:
                        dve.wait_ge(core.store[t % 3].sem, core.store[t % 3].at(t // 3))
                    nc.vector.tensor_tensor(out[t % 3][:, c], bank[n % 8][:, :], gate[rows[t][2]][:, c],
                                            ALU.mult).then_inc(scaled, 1)
                    dve.wait_ge(scaled, n + 1)
                    nc.vector.tensor_tensor(out[t % 3][:, c], out[t % 3][:, c], x[t % 3][:, c], ALU.add).then_inc(added, 1)

            @block.gpsimd
            def _(pool):
                def low(t):
                    for j in range(2):
                        pool.wait_ge(y_high, 2 * t + j + 1)
                        c = slice(4 * j, 4 * j + 4)
                        nc.gpsimd.tensor_tensor(y[t % RY].low[:, c, :], halves[j][:, :, t * P:(t + 1) * P],
                                                y[t % RY].high[:, c, :].bitcast(F32), ALU.subtract).then_inc(y_low, 1)

                low(0)
                for t, (_, dst, _) in enumerate(rows):
                    if t + 1 < n_tiles:
                        low(t + 1)
                    pool.wait_ge(added, 2 * t + 2)
                    pool.dma_start(dst, out[t % 3][:, :]).then_inc(core.store[t % 3].sem, 16)
                for j in range(3):
                    pool.wait_ge(core.store[j].sem, core.store[j].at(len(range(j, n_tiles, 3))))
        for j in range(2):
            core.load[3 + j].close(WP // 2)
        for j in range(3):
            core.load[j].close(len(range(j, n_tiles, 3)))
            core.store[j].close(len(range(j, n_tiles, 3)))




def build_program(nc, io, out, tap=None, upto=99):
    core = Core(nc, io, tap)
    with core.stack:
        core.ident = core.keep("ident", [P, P])
        core.col_a, core.col_b = core.keep("col_a", [P, N_A]), core.keep("col_b", [P, N_B])
        core.col_c = core.keep("col_c", [HFF, 4])
        core.lb = core.keep("lb", [P, 2, 8])
        core.mod1 = core.keep("mod1", [P, 48, 2])
        core.mod2 = [core.keep(f"mod2_{l}", [P, 24, 2]) for l in range(2)]
        core.sc = [core.keep(f"sc{i}", [P, 8]) for i in range(7)]
        core.eps = core.keep("eps", [P, 1])
        core.hy_rms, core.hy_rstd = core.keep("hy_rms", [P, NT]), core.keep("hy_rstd", [P, NT])
        core.moe_idx, core.moe_gate = core.keep("moe_idx", [P, E], U32), core.keep("moe_gate", [P, E])
        core.mod_rows = [core.dram("mod_rows1", [2, 48 * P]), core.dram("mod_rows2", [2, 24 * P]),
                         core.dram("mod_rows3", [2, 24 * P])]
        for name, f in STAGES[:upto]:
            f(core, out)


def run_mods(core, out):
    stage_mods(core)


def run_first_projection(core, out):
    io = core.io
    core.proj_t = core.dram("proj_t", [24 * P, TOK])
    core.vg = core.dram("vg", [TOK, 2 * BANK])
    with Stage(core, "h1") as st:
        hT = Parts(st, "hT", [P, KD, TOK])
        raw = [st.sb(f"raw{i}", [P, KD, BANK]) for i in range(2)]
        m = core.mod1
        groups = []
        for src, dst, ctx in ((0, 0, False), (1, 1, False), (2, 2, False), (3, 3, False), (5, 4, True), (6, 5, True)):
            js = []
            for s in range(4):
                row = (dst * 4 + s) * P
                for t0, n in ((0, 512), (512, 512)) + (((SEQ, CTX),) if ctx else ()):
                    js.append(("ch", s, t0, n, core.proj_t[row:row + P, t0:t0 + n]))
            groups.append((io["w_in"][0][:, src * BANK:(src + 1) * BANK], js))
        for src, dst, tiles in ((4, 0, NT + NC_), (7, 1, NT)):
            groups.append((io["w_in"][0][:, src * BANK:(src + 1) * BANK],
                           [("tok", t, 0, BANK, core.vg[t * P:(t + 1) * P, dst * BANK:(dst + 1) * BANK])
                            for t in range(tiles)]))
        stage_norm(core, "norm1", [(io["x"][0], core.sc[0], m[:, 0:8, 0]), (io["ctx"][0], core.sc[1], m[:, 0:8, 1])], hT,
                   ahead=project_ahead(raw, groups))
        stage_project(core, "proj1", hT, raw, groups)


def run_filter(core, out):
    core.spectra = core.dram("spectra", [2, 2, SEQ, HY])
    stage_filter(core)


def run_hyena(core, out):
    core.mix_t = core.dram("mix_t", [D, SEQ])
    stage_hyena(core)


def run_hgrn(core, out):
    core.hg_o = core.dram("hg_o", [SEQ, HG_HEADS * P])
    stage_hgrn(core)


def run_mix_out(core, out):
    core.x1 = core.dram("x1", [SEQ, D])
    stage_mix_out(core)


def run_moe(core, out):
    core.xn2 = core.dram("xn2", [SEQ, D])
    core.x2 = core.dram("x2", [SEQ, D])
    with Stage(core, "moe_w") as sw:
        raw = [sw.sb(f"raw{i}", [P, KD * BANK]) for i in range(3)]
        with Stage(core, "h2") as st:
            hT = st.sb("hT", [P, KD, SEQ])
            stage_norm(core, "norm2", [(core.x1, core.sc[2], core.mod1[:, 24:32, 0])], hT, xn_dram=core.xn2)
            stage_router(core, hT, raw)
        stage_moe(core, raw)
    stage_final_norm(core)


def run_second(core, out, l):
    io = core.io
    nctx = NC_ if l == 0 else 0
    if l == 0:
        core.x3, core.ctx3 = core.dram("x3", [SEQ, D]), core.dram("ctx3", [CTX, D])
        core.a_tok, core.b_t = core.dram("a_tok", [TOK, 256]), core.dram("b_t", [256, TOK])
        core.qk_tok, core.v_tok = core.dram("qk_tok", [2, TOK, BANK]), core.dram("v_tok", [TOK, BANK])
        core.gate_t = core.dram("gate_t", [D, TOK])
    x, ctx = (core.x2, io["ctx_2"][0]) if l == 0 else (core.x3, core.ctx3)
    m = core.mod2[l]
    name = f"layer{l}"
    with Stage(core, name + "_h") as st:
        hT = Parts(st, "hT", [P, KD, TOK])
        raw = [st.sb(f"raw{i}", [P, KD, BANK]) for i in range(2)]
        w = io["w_in_2"][l]
        groups = []
        tiles = range(NT + nctx)
        spans = [(0, 512), (512, 512)] + ([(SEQ, CTX)] if nctx else [])
        groups.append((w[:, 0:BANK],
                       [("tok", t, 0, 256, core.a_tok[t * P:(t + 1) * P, :]) for t in tiles] +
                       [("ch", 2 + s, t0, n, core.b_t[s * P:(s + 1) * P, t0:t0 + n]) for s in range(2) for t0, n in spans]))
        for i in range(3):
            js = []
            for t in (tiles if i == 0 else range(NT + NC_)):
                dst = core.qk_tok[i] if i < 2 else core.v_tok
                js.append(("tok", t, 0, BANK, dst[t * P:(t + 1) * P, :]))
            groups.append((w[:, (1 + i) * BANK:(2 + i) * BANK], js))
        for i in range(2):
            groups.append((w[:, (4 + i) * BANK:(5 + i) * BANK],
                           [("ch", s, t0, n, core.gate_t[(4 * i + s) * P:(4 * i + s + 1) * P, t0:t0 + n])
                            for s in range(4) for t0, n in spans]))
        stage_norm(core, name + "_norm", [(x, core.sc[3 + 2 * l], m[:, 0:8, 0]), (ctx, core.sc[4 + 2 * l], m[:, 0:8, 1])], hT,
                   ahead=project_ahead(raw, groups))
        stage_project(core, name + "_proj", hT, raw, groups)
    TL = NT + nctx
    with Stage(core, name + "_y") as sy:
        y_att = sy.sb("y_att", [P, 4, TL * P])
        with Stage(core, name + "_qk") as sq:
            q_parts = sq.sb("q_parts", [P, 2 * HEADS2, TL * P], F32R)
            k_high, k_low = sq.sb("k_high", [P, 2 * HEADS2, TOK], F32R), sq.sb("k_low", [P, HEADS2, TOK], F32R)
            neg_lam = sq.sb("neg_lam", [P, 1])
            stage_qk(core, l, list(tiles), q_parts, k_high, k_low, neg_lam, name + "_rope")
            stage_attend(core, l, list(tiles), q_parts, k_high, k_low, neg_lam, y_att, name + "_att")
        y_mix = sy.sb("y_mix", [P, 4, TL * P])
        raw = [sy.sb(f"raw{i}", [P, 2, D]) for i in range(2)]
        stage_mix2(core, l, [(0, NT)] + ([(NT, NC_)] if nctx else []), y_att, y_mix, raw, name + "_mix")
        dst = (core.x3, core.ctx3) if l == 0 else (out[0], None)
        rows = [(x[t * P:(t + 1) * P, :], dst[0][t * P:(t + 1) * P, :], 0) for t in range(NT)]
        rows += [(ctx[t * P:(t + 1) * P, :], dst[1][t * P:(t + 1) * P, :], 1) for t in range(nctx)]
        stage_out2(core, l, (y_mix, y_att), raw, rows, name + "_out")


STAGES = [("mods", run_mods), ("proj1", run_first_projection), ("filter", run_filter), ("hyena", run_hyena),
          ("hgrn", run_hgrn), ("mixout", run_mix_out), ("moe", run_moe),
          ("layer0", lambda core, out: run_second(core, out, 0)), ("layer1", lambda core, out: run_second(core, out, 1))]


def tables():
    f64 = np.float64
    t = {}
    t["t_ident"] = np.eye(P)
    t["t_iota"] = np.tile(np.arange(SEQ), (P, 1))
    tok = np.arange(SEQ).reshape(NT, P).T
    t["t_tokid"] = np.stack([tok // P * P, tok % P], axis=2).reshape(P, 2 * NT)
    f32 = np.float32
    pos = np.linspace(0.0, 1.0, SEQ, dtype=f32)[:, None]
    w = (f32(2.0 * math.pi) * np.arange(SEQ, dtype=f32)[:, None] / f32(SEQ)).astype(f32)
    f = np.linspace(1e-4, 15, 16, dtype=f32)[None, :]
    fw = (f * w).astype(f32).astype(f64)
    t["t_pos"] = np.concatenate([pos, np.cos(fw), -np.sin(fw)], axis=1).T
    evens = np.concatenate([np.arange(0, SEQ, 2), np.arange(1, SEQ, 2)])
    t["t_pos"] = t["t_pos"][:, evens]
    lo, hi = math.log(1e-2) / 1.5, math.log(1e-2) / 0.3
    deltas = np.abs(np.linspace(lo, hi, HY, dtype=f32))
    t["t_window"] = np.exp((-pos * deltas[None, :]).astype(f32).astype(f64)) + 0.05
    t["t_window"] = t["t_window"][evens]
    t["t_window0"] = t["t_window"][0:P].copy()
    t["t_window0"][0] = 0.0
    k = np.concatenate([np.arange(0, SEQ, 2), SEQ - 1 - np.arange(0, SEQ, 2)])
    turn = ((2 * k[None, :SEQ // 2] + 1) * evens[:, None]) % (4 * SEQ)
    t["t_lag_cos"], t["t_lag_sin"] = np.cos(turn * math.pi / (2 * SEQ)), np.sin(turn * math.pi / (2 * SEQ))
    turn = ((2 * k[None, :] + 1) * (2 * np.arange(SEQ // 2)[:, None] + 1)) % (8 * SEQ)
    c, s = np.cos(turn * math.pi / (4 * SEQ)), np.sin(turn * math.pi / (4 * SEQ))
    t["t_fwd_add"], t["t_fwd_sub"] = c + s, c - s
    t["t_inv_add"], t["t_inv_sub"] = (c + s).T, (c - s).T
    key, query = np.arange(P)[:, None], np.arange(P)[None, :]
    masks = []
    for l in range(LEVELS):
        block = P >> l
        masks.append((key // block == query // block) & ((key % block < block // 2) != (query % block < block // 2)))
    masks.append(key == query)
    t["t_pair_masks"] = np.stack(masks, axis=1).reshape(P, 8 * P)
    half = QK // 2
    inv = (f32(10000.0) ** (-np.arange(0, half, 2, dtype=f32) / f32(half))).astype(f32)
    rows, cols = np.arange(SEQ) // GRID, np.arange(SEQ) % GRID
    ar = (rows.astype(f32)[:, None] * inv[None, :]).astype(f32).astype(f64)
    ac = (cols.astype(f32)[:, None] * inv[None, :]).astype(f32).astype(f64)
    t["t_rope_cos"] = np.cos(np.concatenate([ar, ar, ac, ac], axis=1))
    t["t_rope_sin"] = np.concatenate([-np.sin(ar), np.sin(ar), -np.sin(ac), np.sin(ac)], axis=1)
    for n, c_name, s_name, f in ((SEQ, "t_tok_cos", "t_tok_sin", 1.0), (CTX, "t_ctx_cos", "t_ctx_sin", 2.0)):
        turn = np.outer(np.arange(n), np.arange(n)) % n * (2 * math.pi / n)
        t[c_name], t[s_name] = f * np.cos(turn), f * np.sin(turn)
    for name in ("t_tok_cos", "t_tok_sin"):
        t[name] = t[name][evens, :BANK]
    turn = np.outer(np.arange(64), np.arange(64)) % 64 * (2 * math.pi / 64)
    t["t_dim_cos"] = np.kron(np.eye(2), np.cos(turn)) / 256
    t["t_dim_sin"] = np.kron(np.eye(2), np.sin(turn)) / 256
    for n, name in ((SEQ, "t_inv_count"), (CTX, "t_inv_count_ctx")):
        pos_ = np.arange(n)
        c = np.stack([1.0 / (np.minimum(pos_ + w // 2 - 1, n - 1) - np.maximum(pos_ - w // 2, 0) + 1)
                      for w in (2, 4, 8, 16)])
        t[name] = np.repeat(c, 64, axis=0).reshape(2, P, n).transpose(1, 0, 2).reshape(P, 2 * n)
    out = {k: np.ascontiguousarray(v, dtype=np.float32) for k, v in t.items()}
    return out


def kernel(**inputs):
    import concourse.bacc as bacc
    from concourse.bass_utils import run_bass_kernel_spmd

    nc = bacc.Bacc("TRN2", target_bir_lowering=False, num_devices=1)
    arrays = {k: np.ascontiguousarray(v) for k, v in inputs.items()}
    arrays.update(tables())
    io = {k: nc.dram_tensor("in_" + k, a.shape, mybir.dt.from_np(a.dtype), kind="ExternalInput").ap()
          for k, a in arrays.items()}
    out = nc.dram_tensor("out_x", (1, SEQ, D), F32, kind="ExternalOutput").ap()
    build_program(nc, io, out)
    r = run_bass_kernel_spmd(nc, [{"in_" + k: a for k, a in arrays.items()}], core_ids=[0])
    return r.results[0]["out_x"]
```
